# Optimizing a Trainium2 kernel written in Bass

```python
import math
import jax, jax.numpy as jnp
from jax import lax
import numpy as np

D_MODEL = 1024
BATCH = 1
SEQ = 256
DEPTH = 2

N_A_LAYERS = DEPTH // 2
N_B_LAYERS = DEPTH - N_A_LAYERS
RET_HEADS = 4
RET_QK_DIM = D_MODEL // RET_HEADS
RET_V_DIM = 2 * RET_QK_DIM
RET_CHUNK = 128
RET_ROT_BASE = 10000.0
ATT_HEADS = 8
ATT_HEAD_DIM = D_MODEL // ATT_HEADS
ROPE_DIM = ATT_HEAD_DIM // 4
ROPE_THETA = 500000.0
MOBA_BLOCK = 256
MOBA_TOPK = 3
MOBA_Q_CHUNK = 32
N_GROUPS = 4
EXPERTS_PER_GROUP = 4
D_EXPERT = D_MODEL // 2
EXPERT_TOPK = 2
NORM_EPS = 1e-6


def rms_norm(x, g):
    x32 = x.astype(jnp.float32)
    y = x32 * lax.rsqrt(jnp.mean(x32 * x32, axis=-1, keepdims=True) + NORM_EPS)
    return (y * g.astype(jnp.float32)).astype(x.dtype)

def rotary(x, pos, rot_dim, theta):
    half = rot_dim // 2
    inv = 1.0 / (theta ** (jnp.arange(half, dtype=jnp.float32) / half))
    ang = pos.astype(jnp.float32)[:, None] * inv[None, :]
    cos = jnp.cos(ang)[:, None, :]
    sin = jnp.sin(ang)[:, None, :]
    xr = x[..., :rot_dim].astype(jnp.float32)
    x1, x2 = xr[..., :half], xr[..., half:]
    rot = jnp.concatenate([x1 * cos - x2 * sin, x2 * cos + x1 * sin], axis=-1).astype(x.dtype)
    return jnp.concatenate([rot, x[..., rot_dim:]], axis=-1)

def retention(x, w_in, w_out):
    B, S, _ = x.shape
    H, dk, dv, C = RET_HEADS, RET_QK_DIM, RET_V_DIM, RET_CHUNK
    f32 = jnp.float32
    proj = x @ w_in
    q, k, v, g = jnp.split(proj, [H * dk, 2 * H * dk, 2 * H * dk + H * dv], axis=-1)
    pos = jnp.arange(S)
    q = rotary(q.reshape(B, S, H, dk), pos, dk, RET_ROT_BASE)
    k = rotary(k.reshape(B, S, H, dk), pos, dk, RET_ROT_BASE) * (dk ** -0.5)
    v = v.reshape(B, S, H, dv)
    n_c = S // C
    qc = q.astype(f32).reshape(B, n_c, C, H, dk).transpose(1, 0, 3, 2, 4)
    kc = k.astype(f32).reshape(B, n_c, C, H, dk).transpose(1, 0, 3, 2, 4)
    vc = v.astype(f32).reshape(B, n_c, C, H, dv).transpose(1, 0, 3, 2, 4)
    log_gamma = jnp.log1p(-jnp.power(2.0, -5.0 - jnp.arange(H, dtype=f32)))
    idx = jnp.arange(C, dtype=f32)
    diff = idx[:, None] - idx[None, :]
    decay_mask = jnp.where(diff >= 0, jnp.exp(log_gamma[:, None, None] * jnp.maximum(diff, 0.0)), 0.0)
    q_decay = jnp.exp(log_gamma[:, None] * (idx + 1.0))
    k_decay = jnp.exp(log_gamma[:, None] * (C - 1.0 - idx))
    chunk_decay = jnp.exp(log_gamma * C)
    scores = jnp.einsum('nbhcd,nbhmd->nbhcm', qc, kc) * decay_mask[None, None]
    o_intra = jnp.einsum('nbhcm,nbhme->nbhce', scores, vc)

    def step(state, inp):
        qi, ki, vi = inp
        o = jnp.einsum('bhcd,bhde->bhce', qi * q_decay[None, :, :, None], state)
        state = state * chunk_decay[None, :, None, None] + jnp.einsum(
            'bhcd,bhce->bhde', ki * k_decay[None, :, :, None], vi)
        return state, o

    state0 = jnp.zeros((B, H, dk, dv), f32)
    _, o_cross = lax.scan(step, state0, (qc, kc, vc))
    o = (o_intra + o_cross).transpose(1, 0, 3, 2, 4).reshape(B, S, H, dv)
    o = o * lax.rsqrt(jnp.mean(o * o, axis=-1, keepdims=True) + NORM_EPS)
    y = jax.nn.silu(g.astype(f32)) * o.reshape(B, S, H * dv)
    return y.astype(x.dtype) @ w_out

def shared_kv(h, kv_norm, w_kv):
    B, S, _ = h.shape
    H, dh, BLK = ATT_HEADS, ATT_HEAD_DIM, MOBA_BLOCK
    hn = rms_norm(h, kv_norm)
    k, v = jnp.split(hn @ w_kv, 2, axis=-1)
    k = rotary(k.reshape(B, S, H, dh), jnp.arange(S), ROPE_DIM, ROPE_THETA)
    v = v.reshape(B, S, H, dh)
    n_blk = -(-S // BLK)
    pad = n_blk * BLK - S
    k = jnp.pad(k, ((0, 0), (0, pad), (0, 0), (0, 0))).transpose(0, 2, 1, 3).reshape(B, H, n_blk, BLK, dh)
    v = jnp.pad(v, ((0, 0), (0, pad), (0, 0), (0, 0))).transpose(0, 2, 1, 3).reshape(B, H, n_blk, BLK, dh)
    k_mean = jnp.mean(k.astype(jnp.float32), axis=3).astype(k.dtype)
    return k, v, k_mean

def moba_attention(x, w_q, w_o, kb, vb, k_mean):
    B, S, _ = x.shape
    H, dh, BLK, QC = ATT_HEADS, ATT_HEAD_DIM, MOBA_BLOCK, MOBA_Q_CHUNK
    n_blk = kb.shape[2]
    s_pad = n_blk * BLK
    topk = min(MOBA_TOPK, n_blk)
    q = (x @ w_q).reshape(B, S, H, dh)
    q = rotary(q, jnp.arange(S), ROPE_DIM, ROPE_THETA) * (dh ** -0.5)
    q = jnp.pad(q, ((0, 0), (0, s_pad - S), (0, 0), (0, 0))).transpose(0, 2, 1, 3)
    n_qc = s_pad // QC
    qs = q.reshape(B, H, n_qc, QC, dh).transpose(2, 0, 1, 3, 4)
    b_idx = jnp.arange(B)[:, None, None, None]
    h_idx = jnp.arange(H)[None, :, None, None]
    blk_ids = jnp.arange(n_blk)
    neg_inf = -jnp.inf

    def attend(args):
        qi, ci = args
        q0 = ci * QC
        blk = q0 // BLK
        gate = jnp.einsum('bhqd,bhnd->bhqn', qi, k_mean).astype(jnp.float32)
        gate = jnp.where(blk_ids < blk, gate, neg_inf)
        _, sel = lax.top_k(gate, topk)
        slot_ok = jnp.arange(topk) < blk
        ks = kb[b_idx, h_idx, sel]
        vs = vb[b_idx, h_idx, sel]
        s_sel = jnp.einsum('bhqd,bhqnkd->bhqnk', qi, ks).astype(jnp.float32)
        s_sel = jnp.where(slot_ok[:, None], s_sel, neg_inf).reshape(B, H, QC, topk * BLK)
        k_own = lax.dynamic_index_in_dim(kb, blk, axis=2, keepdims=False)
        v_own = lax.dynamic_index_in_dim(vb, blk, axis=2, keepdims=False)
        s_own = jnp.einsum('bhqd,bhkd->bhqk', qi, k_own).astype(jnp.float32)
        q_pos = q0 + jnp.arange(QC)
        k_pos = blk * BLK + jnp.arange(BLK)
        s_own = jnp.where(k_pos[None, :] <= q_pos[:, None], s_own, neg_inf)
        p = jax.nn.softmax(jnp.concatenate([s_sel, s_own], axis=-1), axis=-1).astype(vb.dtype)
        p_sel = p[..., :topk * BLK].reshape(B, H, QC, topk, BLK)
        p_own = p[..., topk * BLK:]
        return (jnp.einsum('bhqnk,bhqnkd->bhqd', p_sel, vs)
                + jnp.einsum('bhqk,bhkd->bhqd', p_own, v_own))

    o = lax.map(attend, (qs, jnp.arange(n_qc)))
    o = o.transpose(1, 0, 3, 2, 4).reshape(B, s_pad, H * dh)[:, :S]
    return o @ w_o

def hier_moe(x, w_rg, b_rg, w_re, b_re, w_gate, w_up, w_down):
    B, S, D = x.shape
    G, E = N_GROUPS, EXPERTS_PER_GROUP
    t = x.reshape(-1, D)
    g_prob = jax.nn.softmax((t @ w_rg).astype(jnp.float32) + b_rg, axis=-1)
    g_val, g_idx = lax.top_k(g_prob, 1)
    e_logits_all = jnp.einsum('td,gde->tge', t, w_re).astype(jnp.float32) + b_re
    e_logits = jnp.take_along_axis(e_logits_all, g_idx[:, :, None], axis=1)[:, 0]
    e_val, e_idx = lax.top_k(e_logits, EXPERT_TOPK)
    e_w = jax.nn.softmax(e_val, axis=-1)
    within = jnp.sum(jax.nn.one_hot(e_idx, E) * e_w[..., None], axis=1)
    group_w = jax.nn.one_hot(g_idx[:, 0], G) * g_val
    combine = (group_w[:, :, None] * within[:, None, :]).astype(x.dtype)
    y = jnp.zeros_like(t)
    for g in range(G):
        hg = jax.nn.silu(jnp.einsum('td,edf->tef', t, w_gate[g])) * jnp.einsum('td,edf->tef', t, w_up[g])
        y = y + jnp.einsum('tef,efd->td', hg * combine[:, g, :, None], w_down[g])
    return y.reshape(B, S, D)

def first_inputs(seed: int = 0) -> dict:
    key = jax.random.key(seed)
    ks = jax.random.split(key, 18)
    f32 = jnp.float32

    def normal(k, shape, scale):
        return jax.random.normal(k, shape, f32) * scale

    def gain(k, shape):
        return 1.0 + 0.05 * jax.random.normal(k, shape, f32)

    out_scale = (2.0 * DEPTH) ** -0.5
    ret_in_cols = 2 * RET_HEADS * RET_QK_DIM + 2 * RET_HEADS * RET_V_DIM
    att_w = ATT_HEADS * ATT_HEAD_DIM
    return {
        'x': normal(ks[0], (BATCH, SEQ, D_MODEL), 1.0),
        'ret_norm': gain(ks[1], (N_A_LAYERS, D_MODEL)),
        'ret_w_in': normal(ks[2], (N_A_LAYERS, D_MODEL, ret_in_cols), D_MODEL ** -0.5),
        'ret_w_out': normal(ks[3], (N_A_LAYERS, RET_HEADS * RET_V_DIM, D_MODEL), (RET_HEADS * RET_V_DIM) ** -0.5 * out_scale),
        'kv_norm': gain(ks[4], (D_MODEL,)),
        'w_kv': normal(ks[5], (D_MODEL, 2 * att_w), D_MODEL ** -0.5),
        'attn_norm': gain(ks[6], (N_B_LAYERS, D_MODEL)),
        'w_q': normal(ks[7], (N_B_LAYERS, D_MODEL, att_w), D_MODEL ** -0.5),
        'w_o': normal(ks[8], (N_B_LAYERS, att_w, D_MODEL), att_w ** -0.5 * out_scale),
        'ffn_norm': gain(ks[9], (DEPTH, D_MODEL)),
        'router_group_w': normal(ks[10], (DEPTH, D_MODEL, N_GROUPS), D_MODEL ** -0.5),
        'router_group_b': normal(ks[11], (DEPTH, N_GROUPS), 0.01),
        'router_expert_w': normal(ks[12], (DEPTH, N_GROUPS, D_MODEL, EXPERTS_PER_GROUP), D_MODEL ** -0.5),
        'router_expert_b': normal(ks[13], (DEPTH, N_GROUPS, EXPERTS_PER_GROUP), 0.01),
        'expert_w_gate': normal(ks[14], (DEPTH, N_GROUPS, EXPERTS_PER_GROUP, D_MODEL, D_EXPERT), D_MODEL ** -0.5),
        'expert_w_up': normal(ks[15], (DEPTH, N_GROUPS, EXPERTS_PER_GROUP, D_MODEL, D_EXPERT), D_MODEL ** -0.5),
        'expert_w_down': normal(ks[16], (DEPTH, N_GROUPS, EXPERTS_PER_GROUP, D_EXPERT, D_MODEL), D_EXPERT ** -0.5 * out_scale),
        'final_norm': gain(ks[17], (D_MODEL,)),
    }

def first_block(x, ret_norm, ret_w_in, ret_w_out, kv_norm, w_kv, attn_norm, w_q, w_o,
              ffn_norm, router_group_w, router_group_b, router_expert_w, router_expert_b,
              expert_w_gate, expert_w_up, expert_w_down, final_norm):
    h = x
    kb = vb = k_mean = None
    for layer in range(DEPTH):
        if layer < N_A_LAYERS:
            h = h + retention(rms_norm(h, ret_norm[layer]), ret_w_in[layer], ret_w_out[layer])
        else:
            if layer == N_A_LAYERS:
                kb, vb, k_mean = shared_kv(h, kv_norm, w_kv)
            j = layer - N_A_LAYERS
            h = h + moba_attention(rms_norm(h, attn_norm[j]), w_q[j], w_o[j], kb, vb, k_mean)
        h = h + hier_moe(rms_norm(h, ffn_norm[layer]), router_group_w[layer], router_group_b[layer],
                         router_expert_w[layer], router_expert_b[layer], expert_w_gate[layer],
                         expert_w_up[layer], expert_w_down[layer])
    return rms_norm(h, final_norm)


DEPTH_2 = 4

N_MIXERS = 3
MEM_LEN = 256
EPS = 1e-6
DA_HEADS = 8
DA_QK_DIM = 64
DA_V_DIM = 2 * DA_QK_DIM
Q_BLOCK = 128
REL_BUCKETS = 32
REL_MAX_DIST = 128
HG_EXPAND = 128
HG_HEADS = D_MODEL // HG_EXPAND
HG_V_DIM = D_MODEL // HG_HEADS
HG_CHUNK = 64
SG_CHUNK = 128
SG_GROUPS = 8
SG_WIDTH = D_MODEL
SG_GROUP_DIM = SG_WIDTH // SG_GROUPS
CA_HEADS = 4
CA_HEAD_DIM = D_MODEL // CA_HEADS
D_FF = int(math.ceil(8 * D_MODEL / 3 / 256)) * 256
N_A = (DEPTH_2 + 2) // 3
N_B = (DEPTH_2 + 1) // 3
N_C = DEPTH_2 // 3


def rmsnorm(x, g):
    xf = x.astype(jnp.float32)
    y = xf * lax.rsqrt(jnp.mean(xf * xf, axis=-1, keepdims=True) + EPS)
    return (y * g.astype(jnp.float32)).astype(x.dtype)

def rel_bucket(dist):
    n = jnp.maximum(dist, 0)
    exact = REL_BUCKETS // 2
    nf = jnp.maximum(n, exact).astype(jnp.float32)
    large = exact + (jnp.log(nf / exact) / math.log(REL_MAX_DIST / exact)
                     * (REL_BUCKETS - exact)).astype(jnp.int32)
    large = jnp.minimum(large, REL_BUCKETS - 1)
    return jnp.where(n < exact, n, large)

def diff_attention(h, w_in, w_out, lq1, lk1, lq2, lk2, subln_g, rel_bias, layer_idx):
    B, S, _ = h.shape
    q, k, v = jnp.split(h @ w_in, 3, axis=-1)
    q = q.reshape(B, S, DA_HEADS, 2, DA_QK_DIM)
    k = k.reshape(B, S, DA_HEADS, 2, DA_QK_DIM)
    v = v.reshape(B, S, DA_HEADS, DA_V_DIM)
    lam_init = 0.8 - 0.6 * math.exp(-0.3 * layer_idx)
    lam = (jnp.exp(jnp.sum(lq1.astype(jnp.float32) * lk1.astype(jnp.float32)))
           - jnp.exp(jnp.sum(lq2.astype(jnp.float32) * lk2.astype(jnp.float32))) + lam_init)
    n_blk = S // Q_BLOCK
    qb = q.reshape(B, n_blk, Q_BLOCK, DA_HEADS, 2, DA_QK_DIM).transpose(1, 0, 2, 3, 4, 5)
    starts = jnp.arange(n_blk, dtype=jnp.int32) * Q_BLOCK
    k_pos = jnp.arange(S, dtype=jnp.int32)
    scale = DA_QK_DIM ** -0.5

    def block(args):
        q_blk, start = args
        dist = (start + jnp.arange(Q_BLOCK, dtype=jnp.int32))[:, None] - k_pos[None, :]
        bias = rel_bias.astype(jnp.float32)[:, rel_bucket(dist)]
        logits = jnp.einsum('bqhcd,bkhcd->bhcqk', q_blk, k).astype(jnp.float32) * scale
        logits = logits + bias[None, :, None]
        logits = jnp.where(dist >= 0, logits, -jnp.inf)
        p = jax.nn.softmax(logits, axis=-1)
        attn = p[:, :, 0] - lam * p[:, :, 1]
        return jnp.einsum('bhqk,bkhd->bqhd', attn.astype(v.dtype), v)

    o = lax.map(block, (qb, starts))
    o = o.transpose(1, 0, 2, 3, 4).reshape(B, S, DA_HEADS, DA_V_DIM)
    o = rmsnorm(o, subln_g) * (1.0 - lam_init)
    return o.reshape(B, S, D_MODEL).astype(h.dtype) @ w_out

def hgrn2(h, w_in, w_out, lower_bound, onorm_g):
    B, S, _ = h.shape
    q, f, i, g = jnp.split(h @ w_in, 4, axis=-1)
    lb = lower_bound.astype(jnp.float32)
    ff = f.astype(jnp.float32)
    log_f = jnp.logaddexp(jnp.log(lb), jnp.log1p(-lb) + jax.nn.log_sigmoid(ff))
    key = 1.0 - jnp.exp(log_f)
    qf = jax.nn.silu(q.astype(jnp.float32))
    vf = i.astype(jnp.float32)
    n_ch = S // HG_CHUNK

    def to_chunks(t, d):
        return t.reshape(B, n_ch, HG_CHUNK, HG_HEADS, d).transpose(1, 0, 3, 2, 4)

    qc, kc, gc = (to_chunks(t, HG_EXPAND) for t in (qf, key, log_f))
    vc = to_chunks(vf, HG_V_DIM)
    causal = jnp.tril(jnp.ones((HG_CHUNK, HG_CHUNK), dtype=bool))

    def step(state, xs):
        qt, kt, vt, gt = xs
        G = jnp.cumsum(gt, axis=2)
        o_inter = jnp.einsum('bhtk,bhkv->bhtv', qt * jnp.exp(G), state)
        diff = G[:, :, :, None, :] - G[:, :, None, :, :]
        decay = jnp.exp(jnp.where(causal[:, :, None], diff, -jnp.inf))
        A = jnp.einsum('bhtk,bhsk,bhtsk->bhts', qt, kt, decay)
        o_intra = jnp.einsum('bhts,bhsv->bhtv', A, vt)
        G_last = G[:, :, -1]
        k_dec = kt * jnp.exp(G_last[:, :, None] - G)
        new_state = jnp.exp(G_last)[..., None] * state + jnp.einsum('bhsk,bhsv->bhkv', k_dec, vt)
        return new_state, o_inter + o_intra

    s0 = jnp.zeros((B, HG_HEADS, HG_EXPAND, HG_V_DIM), jnp.float32)
    _, o = lax.scan(step, s0, (qc, kc, vc, gc))
    o = o.transpose(1, 0, 3, 2, 4).reshape(B, S, HG_HEADS, HG_V_DIM).astype(h.dtype)
    o = rmsnorm(o, onorm_g).reshape(B, S, D_MODEL) * jax.nn.silu(g)
    return o @ w_out

def chunked_sgu(h, w_in, w_out, vnorm_g, w_s, b_s):
    B, S, _ = h.shape
    u, v = jnp.split(jax.nn.gelu(h @ w_in, approximate=False), 2, axis=-1)
    v = rmsnorm(v, vnorm_g)
    n = S // SG_CHUNK
    v = v.reshape(B, n, SG_CHUNK, SG_GROUPS, SG_GROUP_DIM)
    w = w_s * jnp.tril(jnp.ones((SG_CHUNK, SG_CHUNK), w_s.dtype))
    mixed = jnp.einsum('gts,bnsgc->bntgc', w, v) + b_s.T[None, None, :, :, None]
    return (u * mixed.reshape(B, S, SG_WIDTH)) @ w_out

def mem_cross_attention(h, mem_n, w_q, w_kv, w_o):
    B, S, _ = h.shape
    q = (h @ w_q).reshape(B, S, CA_HEADS, CA_HEAD_DIM)
    k, v = jnp.split(mem_n @ w_kv, 2, axis=-1)
    k = k.reshape(B, -1, CA_HEADS, CA_HEAD_DIM)
    v = v.reshape(B, -1, CA_HEADS, CA_HEAD_DIM)
    logits = jnp.einsum('bshd,bmhd->bhsm', q, k).astype(jnp.float32) * (CA_HEAD_DIM ** -0.5)
    p = jax.nn.softmax(logits, axis=-1)
    o = jnp.einsum('bhsm,bmhd->bshd', p.astype(v.dtype), v).reshape(B, S, D_MODEL)
    return o @ w_o

def swiglu(h, w_gu, w_down):
    gate, up = jnp.split(h @ w_gu, 2, axis=-1)
    return (jax.nn.silu(gate) * up) @ w_down

def second_inputs(seed: int = 0) -> dict:
    key = jax.random.key(seed)
    k = jax.random.split(key, 32)
    f32 = jnp.float32

    def nrm(kk, shape, scale):
        return jax.random.normal(kk, shape, f32) * scale

    def gain(kk, shape):
        return 1.0 + nrm(kk, shape, 0.02)

    D = D_MODEL
    return {
        "x": nrm(k[0], (BATCH, SEQ, D), 1.0),
        "mem": nrm(k[1], (BATCH, MEM_LEN, D), 1.0),
        "rel_bias": nrm(k[2], (DA_HEADS, REL_BUCKETS), 0.5),
        "norm_mix": gain(k[3], (DEPTH_2, D)),
        "norm_cross": gain(k[4], (DEPTH_2, D)),
        "norm_ffn": gain(k[5], (DEPTH_2, D)),
        "norm_mem": gain(k[6], (D,)),
        "norm_final": gain(k[7], (D,)),
        "da_w_in": nrm(k[8], (N_A, D, 3 * D), D ** -0.5),
        "da_w_out": nrm(k[9], (N_A, D, D), D ** -0.5),
        "da_lq1": nrm(k[10], (N_A, DA_QK_DIM), 0.1),
        "da_lk1": nrm(k[11], (N_A, DA_QK_DIM), 0.1),
        "da_lq2": nrm(k[12], (N_A, DA_QK_DIM), 0.1),
        "da_lk2": nrm(k[13], (N_A, DA_QK_DIM), 0.1),
        "da_subln": gain(k[14], (N_A, DA_V_DIM)),
        "hg_w_in": nrm(k[15], (N_B, D, 4 * D), D ** -0.5),
        "hg_w_out": nrm(k[16], (N_B, D, D), D ** -0.5),
        "hg_lower_bounds": nrm(k[17], (DEPTH_2, HG_HEADS * HG_EXPAND), 0.5),
        "hg_onorm": gain(k[18], (N_B, HG_V_DIM)),
        "sg_w_in": nrm(k[19], (N_C, D, 2 * SG_WIDTH), D ** -0.5),
        "sg_w_out": nrm(k[20], (N_C, SG_WIDTH, D), SG_WIDTH ** -0.5),
        "sg_vnorm": gain(k[21], (N_C, SG_WIDTH)),
        "sg_w_s": nrm(k[22], (N_C, SG_GROUPS, SG_CHUNK, SG_CHUNK), SG_CHUNK ** -0.5),
        "sg_b_s": 1.0 + nrm(k[23], (N_C, SG_GROUPS, SG_CHUNK), 0.1),
        "ca_w_q": nrm(k[24], (DEPTH_2, D, D), D ** -0.5),
        "ca_w_kv": nrm(k[25], (DEPTH_2, D, 2 * D), D ** -0.5),
        "ca_w_o": nrm(k[26], (DEPTH_2, D, D), D ** -0.5),
        "ffn_w_gu": nrm(k[27], (DEPTH_2, D, 2 * D_FF), D ** -0.5),
        "ffn_w_down": nrm(k[28], (DEPTH_2, D_FF, D), D_FF ** -0.5),
    }

def second_block(x, mem, rel_bias, norm_mix, norm_cross, norm_ffn, norm_mem, norm_final,
              da_w_in, da_w_out, da_lq1, da_lk1, da_lq2, da_lk2, da_subln,
              hg_w_in, hg_w_out, hg_lower_bounds, hg_onorm,
              sg_w_in, sg_w_out, sg_vnorm, sg_w_s, sg_b_s,
              ca_w_q, ca_w_kv, ca_w_o, ffn_w_gu, ffn_w_down):
    mem_n = rmsnorm(mem, norm_mem)
    lb = jax.nn.softmax(hg_lower_bounds.astype(jnp.float32), axis=0)
    lb = jnp.cumsum(lb, axis=0) - lb[0]
    for i in range(DEPTH_2):
        kind = i % N_MIXERS
        j = i // N_MIXERS
        hn = rmsnorm(x, norm_mix[i])
        if kind == 0:
            mix = diff_attention(hn, da_w_in[j], da_w_out[j], da_lq1[j], da_lk1[j],
                                 da_lq2[j], da_lk2[j], da_subln[j], rel_bias, i)
        elif kind == 1:
            mix = hgrn2(hn, hg_w_in[j], hg_w_out[j], lb[i], hg_onorm[j])
        else:
            mix = chunked_sgu(hn, sg_w_in[j], sg_w_out[j], sg_vnorm[j], sg_w_s[j], sg_b_s[j])
        x = x + mix
        x = x + mem_cross_attention(rmsnorm(x, norm_cross[i]), mem_n, ca_w_q[i], ca_w_kv[i], ca_w_o[i])
        x = x + swiglu(rmsnorm(x, norm_ffn[i]), ffn_w_gu[i], ffn_w_down[i])
    return rmsnorm(x, norm_final)


def setup_inputs(seed=0):
    out = dict(first_inputs(seed))
    for name, value in second_inputs(seed + 1).items():
        if name != "x":
            out[name + "_2"] = value
    return out


def reference(
    x, ret_norm, ret_w_in, ret_w_out, kv_norm, w_kv, attn_norm, w_q, w_o, ffn_norm,
    router_group_w, router_group_b, router_expert_w, router_expert_b, expert_w_gate,
    expert_w_up, expert_w_down, final_norm, mem_2, rel_bias_2, norm_mix_2, norm_cross_2,
    norm_ffn_2, norm_mem_2, norm_final_2, da_w_in_2, da_w_out_2, da_lq1_2, da_lk1_2, da_lq2_2,
    da_lk2_2, da_subln_2, hg_w_in_2, hg_w_out_2, hg_lower_bounds_2, hg_onorm_2, sg_w_in_2,
    sg_w_out_2, sg_vnorm_2, sg_w_s_2, sg_b_s_2, ca_w_q_2, ca_w_kv_2, ca_w_o_2, ffn_w_gu_2,
    ffn_w_down_2,
):
    x = first_block(
        x, ret_norm, ret_w_in, ret_w_out, kv_norm, w_kv, attn_norm, w_q, w_o, ffn_norm,
        router_group_w, router_group_b, router_expert_w, router_expert_b, expert_w_gate,
        expert_w_up, expert_w_down, final_norm,
    )
    return second_block(
        x, mem_2, rel_bias_2, norm_mix_2, norm_cross_2, norm_ffn_2, norm_mem_2, norm_final_2,
        da_w_in_2, da_w_out_2, da_lq1_2, da_lk1_2, da_lq2_2, da_lk2_2, da_subln_2, hg_w_in_2,
        hg_w_out_2, hg_lower_bounds_2, hg_onorm_2, sg_w_in_2, sg_w_out_2, sg_vnorm_2, sg_w_s_2,
        sg_b_s_2, ca_w_q_2, ca_w_kv_2, ca_w_o_2, ffn_w_gu_2, ffn_w_down_2,
    )


_drawn_inputs = setup_inputs


def setup_inputs(seed=0):
    import zlib

    import numpy as np

    out = dict(_drawn_inputs(seed))
    spreads = {}
    factors = {'attn_norm': 3.715,
     'router_expert_b': 7.304,
     'norm_cross_2': 8.0,
     'norm_mem_2': 8.0,
     'norm_final_2': 2.796,
     'da_lk1_2': 3.289,
     'da_lk2_2': 5.79,
     'da_subln_2': 3.051,
     'hg_lower_bounds_2': 4.706,
     'hg_onorm_2': 5.927,
     'sg_vnorm_2': 8.0}
    for name, (base, spread) in spreads.items():
        noise = np.random.default_rng([zlib.crc32(name.encode()), seed]).standard_normal(out[name].shape)
        drawn = base * np.exp(spread * noise) if base else spread * noise
        out[name] = __import__('jax').numpy.asarray(drawn.astype(out[name].dtype))
    for name, factor in factors.items():
        out[name] = (out[name] * factor).astype(out[name].dtype)
    return out
```

```python
from contextlib import ExitStack
import math

import concourse.bass as bass
import numpy as np
from concourse import mybir

F32 = mybir.dt.float32
F32R = mybir.dt.float32r
U32 = mybir.dt.uint32
ALU = mybir.AluOpType
ACT = mybir.ActivationFunctionType
AX = mybir.AxisListType

P = 128
S = 256
T = S // P
D = 1024
KC = D // P
EPS = 1e-6
WIDE = 512
PIECE = 1024
WP = KC * WIDE // PIECE
KP = KC // WP
FU = 256
DP = FU // P
D_FF = int(math.ceil(8 * D / 3 / 256)) * 256
FFN_UNITS = D_FF // FU
GROUPS, EXPERTS, D_EXPERT = 4, 4, D // 2
MOE_UNITS = GROUPS * EXPERTS * D_EXPERT // FU
PER_EXPERT = D_EXPERT // FU
ROUTER = GROUPS + GROUPS * EXPERTS
RET_HEADS, RET_QK, RET_V = 4, 256, 512
HG_LEVELS = 7
NEG = -1e30

SOFT0 = 6144
BIAS0 = 8192
CUM0 = 10240
MASK0 = CUM0 + (HG_LEVELS + 2) * P
ROUTER0, CAUSAL0, ROPE0, IOTA0, ONE0 = 0, 320, 576, 640, 768
SLOT0, PICK0, GATED0 = 0, 1024, 2048
WI0 = 56
Z0 = 4096
GROUP_UNITS = MOE_UNITS // GROUPS


COUNTED = ("wide", "out", "down", "turn", "norm", "h", "soft", "heads", "mixed")


class Stage:

    def __init__(self, kind, count, chunk=0, src="h", blocks=0, width=0, col=0, halves=1, units=0, moe=None,
                 last=False, n_heads=0, comps=1, chunks=1, dv=0, causal=False, scale=1.0, which="", layer=0):
        self.kind = kind
        self.wide, self.out, self.down, self.turn, self.norm, self.h, self.soft, self.heads, self.mixed = (
            count[k] for k in COUNTED)
        self.chunk, self.src, self.blocks, self.width, self.col = chunk, src, blocks, width, col
        self.halves, self.units, self.moe, self.last = halves, units, moe, last
        self.n_heads, self.comps, self.chunks, self.dv = n_heads, comps, chunks, dv
        self.causal, self.scale, self.which, self.layer = causal, scale, which, layer


def plan():
    c = dict.fromkeys(COUNTED, 0)
    stages = []

    def add(kind, turns="", what=(), **counted):
        stages.append(Stage(kind, c, **dict(what)))
        for k, v in counted.items():
            c[k] += v
        for m in turns:
            c["turn"] += 1
            TURNS.append(m)

    def norm(chunk=0, src="h"):
        add("norm", "s", dict(chunk=chunk, src=src), norm=1)

    def linear(blocks, width, col=0, chunk=0):
        add("linear", what=dict(blocks=blocks, width=width, col=col, chunk=chunk), wide=blocks, out=blocks)

    def residual(halves=1):
        add("residual", what=dict(halves=halves), wide=2 * halves, out=2, h=1)

    def gated(units, moe, last=False):
        add("gated", what=dict(units=units, moe=moe, last=last), wide=units, out=units, down=units, h=1)

    def softmax(heads, comps, chunks, dv, causal, scale, width, which, layer):
        add("attention", "pps", dict(n_heads=heads, comps=comps, chunks=chunks, dv=dv, causal=causal,
                                     scale=scale, width=width, which=which, layer=layer),
            soft=heads * comps, heads=heads, mixed=2)

    add("setup")
    norm()
    linear(12, 6144)
    add("retention", "ppss", mixed=2)
    residual(2)
    norm()
    gated(MOE_UNITS, 0)
    norm()
    linear(4, 3072, col=1024)
    norm(chunk=8)
    linear(2, 3072, chunk=8)
    softmax(8, 1, 1, 128, True, 128.0 ** -0.5, 3072, "moba", 0)
    residual()
    norm()
    gated(MOE_UNITS, 1)
    add("between", norm=1, h=1)
    norm(chunk=8, src="mem")
    for layer in range(4):
        norm()
        if layer % 3 == 0:
            linear(6, 3072)
            softmax(8, 2, 1, 128, True, 64.0 ** -0.5, 3072, "diff", layer // 3)
        elif layer == 1:
            linear(8, 4096)
            add("hgrn", "pps", mixed=2)
        else:
            linear(4, 2048)
            add("sgu", "s", mixed=1)
        residual()
        norm()
        linear(2, 3072)
        linear(4, 3072, col=1024, chunk=8)
        softmax(4, 1, 2, 256, False, 256.0 ** -0.5, 3072, "cross", layer)
        residual()
        norm()
        gated(FFN_UNITS, None, last=layer == 3)
    add("finish", norm=1)
    return stages, c


TURNS = []
PLAN, TOTAL = plan()


def kept(m):
    n = sum(4 if k == "s" else 2 for k in TURNS[:m])
    return n


def lam_init(layer):
    return 0.8 - 0.6 * math.exp(-0.3 * 3 * layer)


def build(nc, dram, out):
    ctx = ExitStack()
    with ctx:
        def sb(name, words, dt=F32):
            return ctx.enter_context(nc.sbuf_tensor(name, [P, words], dt))

        def sem(name):
            return ctx.enter_context(nc.semaphore(name))

        stage_w = sb("stage_w", WP * PIECE)
        stage_d = sb("stage_d", DP * PIECE)
        high_w, low_w = sb("high_w", WP * PIECE, F32R), sb("low_w", WP * PIECE, F32R)
        high_d, low_d = sb("high_d", DP * PIECE, F32R), sb("low_d", DP * PIECE, F32R)
        xh = sb("xh", 2 * KC * S, F32R)
        xl = sb("xl", 2 * KC * S, F32R)
        h = sb("h", T * D)
        proj = sb("proj", T * 6144)
        qk = sb("qk", 2 * KC * S)
        y = sb("y", T * D)
        tmp = sb("tmp", T * D)
        table = sb("table", 1536)
        gain = sb("gain", D)
        hidden_h, hidden_l = sb("hidden_h", T * FU, F32R), sb("hidden_l", T * FU, F32R)
        ident = sb("ident", P)
        stat = sb("stat", 192)
        comb = sb("comb", T * MOE_UNITS)
        lam = sb("lam", 4)
        largest = sb("largest", 1, mybir.dt.int32)
        minus_half = sb("minus_half", 1)
        xhv = xh[:, :].rearrange("p (k s) -> p k s", k=2 * KC)
        xlv = xl[:, :].rearrange("p (k s) -> p k s", k=2 * KC)
        qkv = qk[:, :].rearrange("p (k s) -> p k s", k=2 * KC)
        hv = h[:, :].rearrange("p (t d) -> p t d", t=T)
        yv = y[:, :].rearrange("p (t d) -> p t d", t=T)
        tv = tmp[:, :].rearrange("p (t d) -> p t d", t=T)

        def pv(width):
            return proj[:, 0:T * width].rearrange("p (t n) -> p t n", t=T)

        bank = [ctx.enter_context(nc.psum_tensor(f"bank{b}", [P, 512], F32)) for b in range(8)]
        skew = nc.dram_tensor("skew", (8 * P * 385,), F32).ap()

        def at_of(b):
            at = (b // 2) * 4096 + (b % 2) * 512
            return proj[:, at:at + 512].rearrange("p (n m) -> p n m", n=4)

        landed_w = [sem(f"landed_w{p}") for p in range(WP)]
        landed_d = [sem(f"landed_d{p}") for p in range(DP)]
        split_hw, split_lw = sem("split_hw"), sem("split_lw")
        split_hd, split_ld = sem("split_hd"), sem("split_ld")
        used_w, used_d = sem("used_w"), sem("used_d")
        rows0_done = sem("rows0_done")
        taken = [sem("taken0"), sem("taken1")]
        turned, kept_h, kept_l = sem("turned"), sem("kept_h"), sem("kept_l")
        x_in, gain_in, mem_in, table_in = sem("x_in"), sem("gain_in"), sem("mem_in"), sem("table_in")
        ident_in, lam_in, late_in = sem("ident_in"), sem("lam_in"), sem("late_in")
        mean_ready, rooted = sem("mean_ready"), sem("rooted")
        h_ready, squares, normed = sem("h_ready"), sem("squares"), sem("normed")
        mixed = sem("mixed")
        silu_done, hidden_turned, hidden_high, hidden_low = (
            sem("silu_done"), sem("hidden_turned"), sem("hidden_high"), sem("hidden_low"))
        logits_done = sem("logits_done")
        v_step, s_step, g_step = sem("v_step"), sem("s_step"), sem("g_step")
        scored, maxed, exped, combined = sem("scored"), sem("maxed"), sem("exped"), sem("combined")
        probs_turned, probs_kept = sem("probs_turned"), sem("probs_kept")
        head_done, head_taken = sem("head_done"), sem("head_taken")
        rotated, used_router = sem("rotated"), sem("used_router")
        ret_scored, ret_masked, ret_done, ret_taken = (
            sem("ret_scored"), sem("ret_masked"), sem("ret_done"), sem("ret_taken"))
        bias_rows, bias_copied, skewed, unskewed = (
            sem("bias_rows"), sem("bias_copied"), sem("skewed"), sem("unskewed"))
        lam_exp, lb_in, lb_exp, lb_ready, lb_spread = (
            sem("lam_exp"), sem("lb_in"), sem("lb_exp"), sem("lb_ready"), sem("lb_spread"))
        hg_sig, hg_f, hg_log, hg_sums, hg_decay, hg_x, hg_prod, hg_kept, hg_out = (
            sem("hg_sig"), sem("hg_f"), sem("hg_log"), sem("hg_sums"), sem("hg_decay"), sem("hg_x"),
            sem("hg_prod"), sem("hg_kept"), sem("hg_out"))
        gelus, sg_w_in, sg_w_ready, sg_mixed = (
            sem("gelus"), sem("sg_w_in"), sem("sg_w_ready"), sem("sg_mixed"))
        stored, out_stored = sem("stored"), sem("out_stored")
        table_free = sem("table_free")

        grouped, ranked, counted = sem("grouped"), sem("ranked"), sem("counted")

        class Way:
            def __init__(self, n):
                self.gathered, self.gathered_h, self.gathered_l = (
                    sem(f"gathered{n}"), sem(f"gathered_h{n}"), sem(f"gathered_l{n}"))
                self.slots_kept, self.z_left, self.z_right = (
                    sem(f"slots_kept{n}"), sem(f"z_left{n}"), sem(f"z_right{n}"))
                self.scattered, self.added, self.v_step = sem(f"scattered{n}"), sem(f"added{n}"), sem(f"way_v{n}")

        ways = [Way(n) for n in range(2)]
        block = ctx.enter_context(nc.Block())

        @block.sync
        def _(sp):
            def load_wide(n, first=False):
                for p in range(WP):
                    if not first:
                        sp.wait_ge(split_lw, 4 * (n - 1) + p + 1)
                    src = dram["wide"][bass.ds(n, 1), p, :, :].rearrange("a p n -> p (a n)")
                    sp.dma_start(stage_w[:, p * PIECE:(p + 1) * PIECE], src).then_inc(landed_w[p], 16)

            def load_down(n, first=False):
                for p in range(DP):
                    if not first:
                        sp.wait_ge(split_ld, DP * (n - 1) + p + 1)
                    src = dram["down"][bass.ds(n, 1), p, :, :].rearrange("a p n -> p (a n)")
                    sp.dma_start(stage_d[:, p * PIECE:(p + 1) * PIECE], src).then_inc(landed_d[p], 16)

            load_wide(0, first=True)
            for s in PLAN:
                if s.kind in ("linear", "residual"):
                    blocks = s.blocks if s.kind == "linear" else 2 * s.halves
                    with sp.Fori(1, blocks + 1) as i:
                        load_wide(s.wide + i)
                elif s.kind == "gated":
                    load_wide(s.wide + 1)
                    load_down(s.down, first=s.down == 0)
                    with sp.Fori(1, s.units - 1) as i:
                        load_wide(s.wide + 1 + i)
                        load_down(s.down + i)
                    if not s.last:
                        load_wide(s.wide + s.units)
                    load_down(s.down + s.units - 1)

        @block.gpsimd
        def _(pool):
            step, roots = [0], [0]

            def link(ins):
                step[0] += 1
                ins.then_inc(g_step, 1)
                pool.wait_ge(g_step, step[0])

            def root(at, n):
                roots[0] += 1
                pool.wait_ge(mean_ready, roots[0])
                nc.gpsimd.tensor_tensor(stat[:, at:at + n], stat[:, at:at + n],
                                        minus_half[:, :].broadcast_to([P, n]), ALU.pow).then_inc(rooted, 1)

            def load_gain(n):
                if n:
                    pool.wait_ge(normed, 2 * n)
                pool.dma_start(gain[:, :], dram["gains"][n:n + 1, :].broadcast_to([P, D])).then_inc(gain_in, 16)

            def setup():
                link(nc.gpsimd.memset(minus_half[:, :], -0.5))
                pool.dma_start(ident[:, :], dram["ident"]).then_inc(ident_in, 16)
                load_gain(0)
                pool.dma_start(qk[:, 0:512], dram["lambdas"].broadcast_to([P, 512])).then_inc(lam_in, 16)
                pool.dma_start(table[:, :], dram["ret_table"]).then_inc(table_in, 16)

            def rotate(col):
                x = pv(6144)[:, :, col:col + 1024].rearrange("p t (h a c) -> p t h a c", h=RET_HEADS, a=2)
                x1, x2 = x[:, :, :, 0, :], x[:, :, :, 1, :]
                cos, sin = (table[:, o:o + S].rearrange("p (t h c) -> p t h c", t=T, h=1)
                            .broadcast_to([P, T, RET_HEADS, P]) for o in (1024, 1280))
                a, b = (tmp[:, o:o + 1024].rearrange("p (t h c) -> p t h c", t=T, h=RET_HEADS)
                        for o in (0, 1024))
                eng = nc.gpsimd
                link(eng.tensor_tensor(a, x1, sin, ALU.mult))
                link(eng.tensor_tensor(b, x2, sin, ALU.mult))
                link(eng.tensor_tensor(x1, x1, cos, ALU.mult))
                link(eng.tensor_tensor(x2, x2, cos, ALU.mult))
                link(eng.tensor_tensor(x1, x1, b, ALU.subtract))
                return eng.tensor_tensor(x2, x2, a, ALU.add)

            def retention():
                pool.wait_ge(table_in, 16)
                for n in range(2):
                    for t in range(T):
                        pool.wait_ge(taken[t], 2 * (n + 1))
                    rotate(n * 1024).then_inc(rotated, 1)
                    pool.wait_ge(rotated, n + 1)

            def after_retention(s):
                pool.wait_ge(table_free, 1)
                pool.wait_ge(turned, 4 * (s.turn + 4))
                for dst, src in ((table[:, 0:ONE0 + 1], dram["small_table"]),
                                 (table[:, 1024:1408], dram["head_gains"].broadcast_to([P, 3 * P])),
                                 (proj[0:33, 0:384], dram["buckets"]),
                                 (proj[0:33, 384:392], dram["rel_bias"]),
                                 (proj[:, CUM0:MASK0 + HG_LEVELS * P], dram["hg_consts"]),
                                 (stat[:, 128:168], dram["router_bias"].broadcast_to([P, 2 * ROUTER]))):
                    pool.dma_start(dst, src).then_inc(late_in, 16)

            def skew_bias():
                pool.wait_ge(bias_copied, 8)
                rows = proj[:, 512:512 + 8 * 384].rearrange("p (h j) -> p h j", h=8)
                pool.dma_start(skew.rearrange("(h p j) -> p h j", h=8, j=385)[:, :, 0:384], rows).then_inc(skewed, 16)
                pool.wait_ge(skewed, 16)
                back = bass.AP(skew.tensor, 127, [[384, P], [P * 385, 8], [1, S]])
                pool.dma_start(proj[:, BIAS0:BIAS0 + 8 * S].rearrange("p (h k) -> p h k", h=8), back)\
                    .then_inc(unskewed, 16)

            for s in PLAN:
                if s.kind in ("norm", "between", "finish", "sgu"):
                    root(0, T)
                elif s.kind == "hgrn" or s.kind == "attention" and s.which == "diff":
                    root(16, 16)
                if s.kind == "setup":
                    setup()
                elif s.kind == "retention":
                    load_gain(1)
                    retention()
                    root(16, T * RET_HEADS)
                    after_retention(s)
                elif s.kind in ("norm", "between") and s.norm >= 1:
                    load_gain(s.norm + 1)
                    if s.norm == 1:
                        skew_bias()
                if s.kind == "between":
                    pool.dma_start(tv, dram["mem"].rearrange("(t p) d -> p t d", p=P)).then_inc(mem_in, 16)
                    pool.dma_start(stat[:, 128:160], dram["lower_bounds"]).then_inc(lb_in, 16)
                if s.kind == "linear" and s.width == 2048:
                    pool.dma_start(proj[:, 4096:5120], dram["sg_w"]).then_inc(sg_w_in, 16)
                    pool.dma_start(proj[:, 5120:6144], dram["sg_gain"].broadcast_to([P, D])).then_inc(sg_w_in, 16)
                    pool.dma_start(stat[:, 128:136], dram["sg_bias"]).then_inc(sg_w_in, 16)

        @block.scalar
        def _(act):
            step = [0]

            def link(ins):
                step[0] += 1
                ins.then_inc(s_step, 1)
                act.wait_ge(s_step, step[0])

            def high_wide(n, p, first=False):
                act.wait_ge(landed_w[p], 16 * (n + 1))
                if not first:
                    act.wait_ge(used_w, WP * (n - 1) + p + 1)
                w = slice(p * PIECE, (p + 1) * PIECE)
                act.activation(high_w[:, w], stage_w[:, w], ACT.Copy).then_inc(split_hw, 1)

            def high_down(n, p, first=False):
                act.wait_ge(landed_d[p], 16 * (n + 1))
                if not first:
                    act.wait_ge(used_d, DP * (n - 1) + p + 1)
                w = slice(p * PIECE, (p + 1) * PIECE)
                act.activation(high_d[:, w], stage_d[:, w], ACT.Copy).then_inc(split_hd, 1)

            def keep_split(m, chunk):
                for b in range(4):
                    act.wait_ge(turned, 4 * m + b + 1)
                    act.activation(xh[:, (chunk + 2 * b) * S:(chunk + 2 * b + 2) * S], bank[b][:, :],
                                   ACT.Copy).then_inc(kept_h, 1)

            def keep_plain(m, chunk):
                for b in range(2):
                    act.wait_ge(turned, 4 * m + b + 1)
                    act.activation(qk[:, (chunk + 2 * b) * S:(chunk + 2 * b + 2) * S], bank[b][:, :],
                                   ACT.Copy).then_inc(kept_h, 1)

            def squares_of(s):
                if s.kind == "norm" and s.src == "mem":
                    act.wait_ge(mem_in, 16)
                elif s.h == 0:
                    act.wait_ge(x_in, 16)
                else:
                    act.wait_ge(h_ready, s.h)
                src = tv if s.kind == "norm" and s.src == "mem" else hv
                act.activation(yv[:, 0, :], src[:, 0, :], ACT.Square, accum_out=stat[:, 0:1]).then_inc(squares, 1)

            def linear(s):
                out_v = pv(s.width)
                if s.norm == 3:
                    act.wait_ge(skewed, 16)
                with act.Fori(0, s.blocks) as i:
                    act.wait_ge(rows0_done, s.wide + i + 1)
                    act.activation(out_v[:, 0, bass.ds(s.col + i * WIDE, WIDE)], bank[4][:, :], ACT.Copy)\
                       .then_inc(taken[0], 1)
                    for p in range(WP):
                        high_wide(s.wide + 1 + i, p)

            def residual(s):
                with act.Fori(0, 2 * s.halves) as i:
                    for p in range(WP):
                        high_wide(s.wide + 1 + i, p)

            def sparse(s):
                way = ways[s.moe]

                def keep_gathered(g):
                    act.wait_ge(way.gathered, 3 * g + 1)
                    act.activation(qk[:, SLOT0 + g * S:SLOT0 + (g + 1) * S], bank[6][:, S:2 * S], ACT.Copy)\
                        .then_inc(way.slots_kept, 1)
                    for i in range(2):
                        act.wait_ge(way.gathered, 3 * g + i + 2)
                        c = KC * (g % 2) + 4 * i
                        act.activation(xhv[:, c:c + 4, 0:P], bank[5 + 2 * i][:, :].rearrange("p (k m) -> p k m", k=4),
                                       ACT.Copy).then_inc(way.gathered_h, 1)

                def keep_z(g):
                    act.wait_ge(used_d, DP * (s.down + GROUP_UNITS * (g + 1)))
                    if g >= 2:
                        act.wait_ge(way.scattered, 4 * (g - 1))
                    z = Z0 + (g % 2) * D
                    act.activation(proj[:, z:z + WIDE], bank[2 * (g % 2)][:, :], ACT.Copy).then_inc(way.z_left, 1)

                def unit(u, prefetch=True):
                    if prefetch:
                        for p in range(WP - 1):
                            high_wide(s.wide + u + 1, p)
                    act.wait_ge(used_w, WP * (s.wide + u + 1))
                    act.activation(qk[:, GATED0:GATED0 + FU], bank[4][:, 0:FU], ACT.Silu).then_inc(silu_done, 2)
                    high_wide(s.wide + u + 1, WP - 1)

                def hidden(u, first=False):
                    act.wait_ge(hidden_turned, s.down + u + 1)
                    act.activation(hidden_h[:, 0:FU], bank[6][:, 0:FU], ACT.Copy).then_inc(hidden_high, 1)
                    for p in range(DP):
                        high_down(s.down + u, p, first)

                keep_gathered(0)
                unit(0)
                for g in range(GROUPS):
                    u0 = g * GROUP_UNITS
                    if g:
                        hidden(u0 - 1)
                        unit(u0)
                    hidden(u0, first=s.down + u0 == 0)
                    if g:
                        keep_z(g - 1)
                    unit(u0 + 1)
                    if g + 1 < GROUPS:
                        keep_gathered(g + 1)
                    with act.Fori(u0 + 2, u0 + GROUP_UNITS) as u:
                        hidden(u - 1)
                        unit(u)
                hidden(MOE_UNITS - 1)
                keep_z(GROUPS - 1)

            def gated(s):
                def silu(u, t):
                    if t == 0:
                        act.wait_ge(rows0_done, s.wide + u + 1)
                    else:
                        act.wait_ge(used_w, WP * (s.wide + u + 1))
                    act.activation(y[:, t * FU:(t + 1) * FU], bank[4 + t][:, 0:FU], ACT.Silu).then_inc(silu_done, 1)

                def unit(u, prefetch=True):
                    silu(u, 0)
                    if prefetch:
                        for p in range(WP - 1):
                            high_wide(s.wide + u + 1, p)
                    silu(u, 1)
                    if prefetch:
                        high_wide(s.wide + u + 1, WP - 1)

                def hidden(u, first=False):
                    act.wait_ge(hidden_turned, s.down + u + 1)
                    act.activation(hidden_h[:, :], bank[6][:, :], ACT.Copy).then_inc(hidden_high, 1)
                    for p in range(DP):
                        high_down(s.down + u, p, first)

                unit(0)
                hidden(0, first=s.down == 0)
                unit(1)
                with act.Fori(2, s.units - (1 if s.last else 0)) as u:
                    hidden(u - 1)
                    unit(u)
                if s.last:
                    hidden(s.units - 2)
                    unit(s.units - 1, prefetch=False)
                hidden(s.units - 1)

            def retention(s):
                g = pv(6144)[:, :, 4096:6144]
                for t in range(T):
                    act.wait_ge(taken[t], s.out)
                link(act.activation(g, g, ACT.Silu))
                keep_plain(s.turn, 0)
                keep_plain(s.turn + 1, 8)
                o = pv(6144)
                for j in range(RET_HEADS):
                    for t in range(T):
                        act.wait_ge(ret_done, T * j + t + 1)
                        act.activation(y[:, t * 512:(t + 1) * 512], bank[6 + t][:, :], ACT.Square,
                                       accum_out=stat[:, 16 + T * j + t:17 + T * j + t])
                        act.activation(o[:, t, j * RET_V:(j + 1) * RET_V], bank[6 + t][:, :], ACT.Copy)\
                           .then_inc(ret_taken, 1)
                keep_split(s.turn + 2, 0)
                keep_split(s.turn + 3, 8)

            def keep_bias_rows():
                for j in range(8):
                    act.wait_ge(bias_rows, j + 1)
                    act.activation(proj[:, 512 + j * 384:512 + (j + 1) * 384], bank[6 + j % 2][:, 0:384],
                                   ACT.Copy).then_inc(bias_copied, 1)

            def attention(s):
                keep_plain(s.turn, 0)
                keep_plain(s.turn + 1, 8)

                def exps(i):
                    j = i // s.comps
                    act.wait_ge(maxed, s.soft + i + 1)
                    if j >= 2:
                        act.wait_ge(probs_turned, s.heads + j - 1)
                    for t in range(T):
                        n = P * (t + 1) if s.causal else S
                        e = tmp[:, ((j % 2) * 2 + i % s.comps) * 512 + t * S:][:, 0:n]
                        ins = act.activation(e, proj[:, SOFT0 + (i % 2) * 512 + t * S:][:, 0:n], ACT.Exp,
                                             bias=stat[:, 16 + 2 * i + t:17 + 2 * i + t],
                                             accum_out=stat[:, 48 + 2 * i + t:49 + 2 * i + t])
                    ins.then_inc(exped, 1)

                def keep_probs(j):
                    act.wait_ge(probs_turned, s.heads + j + 1)
                    if j >= 2:
                        act.wait_ge(head_done, s.heads + j - 1)
                    slot = SOFT0 + 1024 + (j % 2) * 512
                    src = bank[6 + j % 2]
                    if s.causal:
                        act.activation(proj[:, slot:slot + S], src[:, 0:S], ACT.Copy)
                        ins = act.activation(proj[:, slot + 384:slot + 512], src[:, 384:512], ACT.Copy)
                    else:
                        ins = act.activation(proj[:, slot:slot + 512], src[:, :], ACT.Copy)
                    ins.then_inc(probs_kept, 1)

                for j in range(s.n_heads):
                    for c in range(s.comps):
                        exps(s.comps * j + c)
                    if j:
                        keep_probs(j - 1)
                keep_probs(s.n_heads - 1)
                keep_split(s.turn + 2, 0)

            def hgrn(s):
                v = pv(4096)
                for t in range(T):
                    act.wait_ge(taken[t], s.out)
                act.activation(v[:, :, 1024:2048], v[:, :, 1024:2048], ACT.Sigmoid).then_inc(hg_sig, 1)
                act.activation(v[:, :, 0:1024], v[:, :, 0:1024], ACT.Silu)
                act.activation(v[:, :, 3072:4096], v[:, :, 3072:4096], ACT.Silu).then_inc(hg_sig, 1)
                act.wait_ge(hg_f, 1)
                act.activation(v[:, :, 1024:2048], v[:, :, 1024:2048], ACT.Ln).then_inc(hg_log, 1)
                keep_plain(s.turn, 0)
                keep_plain(s.turn + 1, 8)
                for lv in range(HG_LEVELS + 1):
                    for b in range(4):
                        act.wait_ge(hg_sums, 4 * lv + b + 1)
                        if lv:
                            act.wait_ge(hg_x, lv)
                        act.activation(y[:, b * 512:(b + 1) * 512], bank[b][:, :], ACT.Exp).then_inc(hg_decay, 1)
                keep_split(s.turn + 2, 0)

            def sgu(s):
                v = pv(2048)
                for t in range(T):
                    act.wait_ge(taken[t], s.out)
                act.activation(v[:, :, 1024:2048], v[:, :, 1024:2048], ACT.Gelu).then_inc(gelus, 1)
                act.activation(v[:, :, 0:1024], v[:, :, 0:1024], ACT.Gelu).then_inc(gelus, 1)
                keep_split(s.turn, 0)

            act.dma_start(hv, dram["x"].rearrange("(t p) d -> p t d", p=P)).then_inc(x_in, 16)
            for p in range(WP):
                high_wide(0, p, first=True)
            act.wait_ge(lam_exp, 1)
            act.activation(lam[:, 0:4], lam[:, 0:4], ACT.Exp).then_inc(lam_exp, 1)
            for s in PLAN:
                if s.kind in ("norm", "between", "finish"):
                    squares_of(s)
                if s.kind == "norm":
                    if s.norm == 1:
                        keep_bias_rows()
                    keep_split(s.turn, s.chunk)
                elif s.kind == "between":
                    act.wait_ge(lb_exp, 1)
                    act.activation(stat[:, 128:160], stat[:, 128:160], ACT.Exp).then_inc(lb_exp, 1)
                elif s.kind == "linear":
                    linear(s)
                elif s.kind == "residual":
                    residual(s)
                elif s.kind == "gated":
                    if s.moe is not None:
                        act.wait_ge(logits_done, 2 * s.moe + 1)
                        act.activation(stat[:, 0:8], stat[:, 0:8], ACT.Exp)
                        act.activation(stat[:, 8:10], stat[:, 8:10], ACT.Exp).then_inc(logits_done, 1)
                        act.wait_ge(counted, s.moe + 1)
                        with act.If(act.value_load(largest[0:1, 0:1], min_val=0, max_val=S) < P + 1):
                            sparse(s)
                        with act.Else():
                            gated(s)
                    else:
                        gated(s)
                elif s.kind == "retention":
                    retention(s)
                elif s.kind == "attention":
                    attention(s)
                elif s.kind == "hgrn":
                    hgrn(s)
                elif s.kind == "sgu":
                    sgu(s)
            act.wait_ge(stored, 1)
            act.dma_start(out.rearrange("(t p) d -> p t d", p=P), yv).then_inc(out_stored, 16)
            act.wait_ge(out_stored, 16)

        @block.vector
        def _(dve):
            step, roots = [0], [0]
            vec = nc.vector

            def link(ins):
                step[0] += 1
                ins.then_inc(v_step, 1)
                dve.wait_ge(v_step, step[0])

            def signal(what):
                vec.memset(stat[:, 190:191], 0.0).then_inc(what, 1)

            def low_wide(n, p):
                dve.wait_ge(split_hw, WP * n + p + 1)
                w = slice(p * PIECE, (p + 1) * PIECE)
                vec.tensor_tensor(low_w[:, w], stage_w[:, w], high_w[:, w].bitcast(F32), ALU.subtract)\
                   .then_inc(split_lw, 1)

            def low_down(n, p):
                dve.wait_ge(split_hd, DP * n + p + 1)
                w = slice(p * PIECE, (p + 1) * PIECE)
                vec.tensor_tensor(low_d[:, w], stage_d[:, w], high_d[:, w].bitcast(F32), ALU.subtract)\
                   .then_inc(split_ld, 1)

            def keep_split(m, chunk):
                for b in range(4):
                    dve.wait_ge(kept_h, kept(m) + b + 1)
                    w = slice((chunk + 2 * b) * S, (chunk + 2 * b + 2) * S)
                    vec.tensor_tensor(xl[:, w], bank[b][:, :], xh[:, w].bitcast(F32), ALU.subtract)\
                       .then_inc(kept_l, 1)

            def keep_plain(m, chunk):
                for b in range(2, 4):
                    dve.wait_ge(turned, 4 * m + b + 1)
                    vec.tensor_copy(qk[:, (chunk + 2 * b) * S:(chunk + 2 * b + 2) * S], bank[b][:, :])\
                       .then_inc(kept_l, 1)

            def rstd(at, n, width):
                vec.tensor_scalar(stat[:, at:at + n], stat[:, at:at + n], 1.0 / width, EPS, ALU.mult, ALU.add)\
                    .then_inc(mean_ready, 1)
                roots[0] += 1
                dve.wait_ge(rooted, roots[0])

            def norm(s, dst):
                mem = s.kind == "norm" and s.src == "mem"
                if mem:
                    dve.wait_ge(mem_in, 16)
                elif s.h == 0:
                    dve.wait_ge(x_in, 16)
                else:
                    dve.wait_ge(h_ready, s.h)
                src = tv if mem else hv
                dve.wait_ge(gain_in, 16 * (s.norm + 1))
                link(vec.tensor_tensor_reduce(yv[:, 1, :], src[:, 1, :], src[:, 1, :], 1.0, 0.0, ALU.mult,
                                              ALU.add, stat[:, 1:2]))
                dve.wait_ge(squares, s.norm + 1)
                rstd(0, 2, D)
                for t in range(T):
                    ins = vec.scalar_tensor_tensor(out=dst[:, t, :], in0=src[:, t, :], scalar=stat[:, t:t + 1],
                                                   in1=gain[:, :], op0=ALU.mult, op1=ALU.mult)
                    ins.then_inc(normed, 1)
                return ins

            def linear(s):
                out_v = pv(s.width)
                if s.norm == 3:
                    dve.wait_ge(skewed, 16)
                with dve.Fori(0, s.blocks) as i:
                    for p in range(WP - 1):
                        low_wide(s.wide + 1 + i, p)
                    dve.wait_ge(used_w, WP * (s.wide + i + 1))
                    vec.tensor_copy(out_v[:, 1, bass.ds(s.col + i * WIDE, WIDE)], bank[5][:, :])\
                       .then_inc(taken[1], 1)
                    low_wide(s.wide + 1 + i, WP - 1)

            def residual(s):
                for half in range(2):
                    for k in range(s.halves):
                        i = half * s.halves + k
                        last = k == s.halves - 1
                        if last:
                            dve.wait_ge(rows0_done, s.wide + i + 1)
                            hs = hv[:, 0, half * WIDE:(half + 1) * WIDE]
                            vec.tensor_tensor(hs, hs, bank[4][:, :], ALU.add).then_inc(taken[0], 1)
                        for p in range(WP - 1):
                            low_wide(s.wide + 1 + i, p)
                        if last:
                            dve.wait_ge(used_w, WP * (s.wide + i + 1))
                            hs = hv[:, 1, half * WIDE:(half + 1) * WIDE]
                            vec.tensor_tensor(hs, hs, bank[5][:, :], ALU.add).then_inc(taken[1], 1)
                        low_wide(s.wide + 1 + i, WP - 1)
                dve.wait_ge(taken[1], s.out + 2)
                signal(h_ready)

            def route(s):
                lg = stat[:, 16:16 + T * ROUTER].rearrange("p (t n) -> p t n", t=T)
                pg = stat[:, 0:8].rearrange("p (t g) -> p t g", t=T)
                dv2 = stat[:, 8:10].rearrange("p (t g) -> p t g", t=T)
                rank = stat[:, 168:176].rearrange("p (t g) -> p t g", t=T)

                def rows(a, g):
                    return tmp[:, a:a + T * g].rearrange("p (t g) -> p t g", t=T)

                m, km, gate, v1, v2, w1, w2 = (rows(2 * i, 1) for i in range(7))
                key, one_g, el, e1, e2, wi, rest = (rows(16 + 8 * i, 4) for i in range(7))
                prod = rows(128, 16)

                def wide(a, g):
                    return a.broadcast_to([P, T, g])

                def best(values, top, one):
                    link(vec.tensor_reduce(top, values, AX.X, ALU.max))
                    link(vec.tensor_tensor(key, values, wide(top, 4), ALU.is_equal))
                    link(vec.tensor_tensor(key, key, rank, ALU.mult))
                    link(vec.tensor_reduce(km, key, AX.X, ALU.max))
                    link(vec.tensor_tensor(one, key, wide(km, 4), ALU.is_equal))

                for t in range(T):
                    for g in range(4):
                        ins = vec.memset(stat[:, 168 + 4 * t + g:169 + 4 * t + g], float(4 - g))
                link(ins)
                dve.wait_ge(late_in, 96)
                dve.wait_ge(used_router, s.moe + 1)
                bias = stat[:, 128 + ROUTER * s.moe:128 + ROUTER * (s.moe + 1)].rearrange("p (t n) -> p t n", t=1)
                link(vec.tensor_tensor(lg, bank[7][:, 0:T * ROUTER].rearrange("p (t n) -> p t n", t=T),
                                       bias.broadcast_to([P, T, ROUTER]), ALU.add))
                best(lg[:, :, 0:4], m, one_g)
                signal(grouped)
                link(vec.tensor_tensor(pg, lg[:, :, 0:4], wide(m, 4), ALU.subtract))
                ev = lg[:, :, 4:ROUTER].rearrange("p t (g e) -> p t e g", g=GROUPS)
                pr = prod.rearrange("p t (e g) -> p t e g", e=EXPERTS)
                for t in range(T):
                    ins = vec.tensor_tensor(pr[:, t], ev[:, t], one_g[:, t:t + 1, :].broadcast_to([P, EXPERTS, GROUPS]),
                                            ALU.mult)
                link(ins)
                link(vec.tensor_reduce(el, pr, AX.X, ALU.add))
                best(el, v1, e1)
                link(vec.tensor_scalar(rest, e1, 3e38, None, ALU.mult))
                link(vec.tensor_tensor(rest, el, rest, ALU.subtract))
                best(rest, v2, e2)
                link(vec.tensor_tensor(dv2, v2, v1, ALU.subtract))
                signal(logits_done)
                dve.wait_ge(logits_done, 2 * s.moe + 2)
                link(vec.tensor_reduce(gate, pg, AX.X, ALU.add))
                link(vec.reciprocal(gate, gate))
                link(vec.tensor_scalar(w1, dv2, 1.0, None, ALU.add))
                link(vec.reciprocal(w1, w1))
                link(vec.tensor_tensor(w1, w1, gate, ALU.mult))
                link(vec.tensor_tensor(w2, w1, dv2, ALU.mult))
                vec.tensor_tensor(e1, e1, wide(w1, 4), ALU.mult)
                link(vec.tensor_tensor(e2, e2, wide(w2, 4), ALU.mult))
                link(vec.tensor_tensor(wi, e1, e2, ALU.add))
                dve.wait_ge(ranked, s.moe + 1)
                link(vec.tensor_scalar(tmp[:, 160:168], bank[7][:, 64:72], -1.0, None, ALU.add))
                link(vec.tensor_reduce(tmp[:, 168:169], bank[7][:, 72:76], AX.X, ALU.max))
                vec.tensor_copy(largest[:, :], tmp[:, 168:169]).then_inc(counted, 1)
                return one_g, wi

            def every_unit(s, one_g, wi):
                way = ways[s.moe]
                cv = comb[:, :].rearrange("p (t g e u) -> p t g e u", t=T, g=GROUPS, e=EXPERTS)
                for t in range(T):
                    for u in range(PER_EXPERT):
                        ins = vec.tensor_tensor(
                            cv[:, t, :, :, u], one_g[:, t, :].rearrange("p (g e) -> p g e", e=1)
                            .broadcast_to([P, GROUPS, EXPERTS]),
                            wi[:, t:t + 1, :].broadcast_to([P, GROUPS, EXPERTS]), ALU.mult)
                ins.then_inc(way.v_step, 1)
                dve.wait_ge(way.v_step, 1)

            def sparse(s):
                way = ways[s.moe]
                for t in range(T):
                    for g in range(GROUPS):
                        ins = vec.tensor_scalar(qk[:, PICK0 + (t * GROUPS + g) * P:][:, 0:P], table[:, IOTA0:IOTA0 + P],
                                                tmp[:, 160 + 4 * t + g:161 + 4 * t + g],
                                                tmp[:, 24 + 4 * t + g:25 + 4 * t + g], ALU.is_equal, ALU.mult)
                ins.then_inc(way.v_step, 1)

                def keep_gathered(g):
                    dve.wait_ge(way.gathered, 3 * g + 2)
                    w = bank[2 * (g % 2)][:, 0:EXPERTS].rearrange("p (e a) -> p e a", a=1)
                    vec.tensor_copy(comb[:, g * GROUP_UNITS:(g + 1) * GROUP_UNITS].rearrange("p (e a) -> p e a", e=EXPERTS),
                                    w.broadcast_to([P, EXPERTS, PER_EXPERT])).then_inc(way.v_step, 1)
                    for i in range(2):
                        dve.wait_ge(way.gathered_h, 2 * g + i + 1)
                        c = KC * (g % 2) + 4 * i
                        vec.tensor_tensor(xlv[:, c:c + 4, 0:P], bank[5 + 2 * i][:, :].rearrange("p (k m) -> p k m", k=4),
                                          xhv[:, c:c + 4, 0:P].bitcast(F32), ALU.subtract).then_inc(way.gathered_l, 1)

                def keep_z(g):
                    dve.wait_ge(used_d, DP * (s.down + GROUP_UNITS * (g + 1)))
                    if g >= 2:
                        dve.wait_ge(way.scattered, 4 * (g - 1))
                    z = Z0 + (g % 2) * D + WIDE
                    vec.tensor_copy(proj[:, z:z + WIDE], bank[2 * (g % 2) + 1][:, :]).then_inc(way.z_right, 1)

                def add(g):
                    for i in range(2 * T):
                        t, half = i // 2, i % 2
                        dve.wait_ge(way.scattered, 4 * g + i + 1)
                        if g:
                            dve.wait_ge(way.added, 4 * (g - 1) + i + 1)
                        hs = hv[:, t, half * WIDE:(half + 1) * WIDE]
                        vec.tensor_tensor(hs, hs, bank[5 + 2 * half][:, :], ALU.add).then_inc(way.added, 1)

                def unit(u):
                    for p in range(WP - 1):
                        low_wide(s.wide + u + 1, p)
                    dve.wait_ge(silu_done, 2 * (s.down + u) + 2)
                    for c in range(2):
                        w = comb[:, u:u + 1] if isinstance(u, int) else comb[:, bass.ds(u, 1)]
                        vec.scalar_tensor_tensor(out=qk[:, GATED0 + FU + c * P:GATED0 + FU + (c + 1) * P],
                                                 in0=qk[:, GATED0 + c * P:GATED0 + (c + 1) * P], scalar=w,
                                                 in1=bank[4][:, FU + c * P:FU + (c + 1) * P], op0=ALU.mult,
                                                 op1=ALU.mult).then_inc(taken[c], 1)
                    low_wide(s.wide + u + 1, WP - 1)

                def hidden(u):
                    dve.wait_ge(hidden_high, s.down + u + 1)
                    vec.tensor_tensor(hidden_l[:, 0:FU], bank[6][:, 0:FU], hidden_h[:, 0:FU].bitcast(F32), ALU.subtract)\
                       .then_inc(hidden_low, 1)
                    for p in range(DP):
                        low_down(s.down + u, p)

                keep_gathered(0)
                dve.wait_ge(way.v_step, 2)
                unit(0)
                for g in range(GROUPS):
                    u0 = g * GROUP_UNITS
                    if g:
                        hidden(u0 - 1)
                        dve.wait_ge(way.v_step, g + 2)
                        unit(u0)
                    hidden(u0)
                    if g:
                        keep_z(g - 1)
                    unit(u0 + 1)
                    if g:
                        add(g - 1)
                    if g + 1 < GROUPS:
                        keep_gathered(g + 1)
                    with dve.Fori(u0 + 2, u0 + GROUP_UNITS) as u:
                        hidden(u - 1)
                        unit(u)
                hidden(MOE_UNITS - 1)
                keep_z(GROUPS - 1)
                add(GROUPS - 1)
                dve.wait_ge(way.added, 4 * GROUPS)

            def gated(s):
                if s.moe is None:
                    dense(s)
                    return
                one_g, wi = route(s)
                dve.wait_ge(counted, s.moe + 1)
                with dve.If(dve.value_load(largest[0:1, 0:1], min_val=0, max_val=S) < P + 1):
                    sparse(s)
                with dve.Else():
                    every_unit(s, one_g, wi)
                    dense(s)
                signal(h_ready)

            def dense(s):
                def gate(u, t):
                    dve.wait_ge(silu_done, 2 * (s.down + u) + t + 1)
                    up, sl = bank[4 + t][:, FU:2 * FU], y[:, t * FU:(t + 1) * FU]
                    o = y[:, 512 + t * FU:512 + (t + 1) * FU]
                    if s.moe is None:
                        ins = vec.tensor_tensor(o, sl, up, ALU.mult)
                    else:
                        w = comb[:, t * MOE_UNITS + u:t * MOE_UNITS + u + 1] if isinstance(u, int) else \
                            comb[:, bass.ds(u + t * MOE_UNITS, 1)]
                        ins = vec.scalar_tensor_tensor(out=o, in0=sl, scalar=w, in1=up, op0=ALU.mult, op1=ALU.mult)
                    ins.then_inc(taken[t], 1)

                def unit(u, prefetch=True):
                    gate(u, 0)
                    if prefetch:
                        for p in range(WP - 1):
                            low_wide(s.wide + u + 1, p)
                    gate(u, 1)
                    if prefetch:
                        low_wide(s.wide + u + 1, WP - 1)

                def hidden(u):
                    dve.wait_ge(hidden_high, s.down + u + 1)
                    vec.tensor_tensor(hidden_l[:, :], bank[6][:, :], hidden_h[:, :].bitcast(F32), ALU.subtract)\
                       .then_inc(hidden_low, 1)
                    for p in range(DP):
                        low_down(s.down + u, p)

                unit(0)
                with dve.Fori(1, s.units - (1 if s.last else 0)) as u:
                    hidden(u - 1)
                    unit(u)
                if s.last:
                    hidden(s.units - 2)
                    unit(s.units - 1, prefetch=False)
                hidden(s.units - 1)
                dve.wait_ge(used_d, DP * (s.down + s.units))
                for t in range(T):
                    for half in range(2):
                        hs = hv[:, t, half * WIDE:(half + 1) * WIDE]
                        ins = vec.tensor_tensor(hs, hs, bank[2 * t + half][:, :], ALU.add)
                if s.moe is None:
                    ins.then_inc(h_ready, 1)

            def lambdas():
                dve.wait_ge(lam_in, 16)
                v = qk[:, 0:512].rearrange("p (l a d) -> p l a d", l=2, a=4)
                for layer in range(2):
                    for c in range(2):
                        ins = vec.tensor_tensor_reduce(qk[:, 512:576], v[:, layer, 2 * c, :], v[:, layer, 2 * c + 1, :],
                                                       1.0, 0.0, ALU.mult, ALU.add,
                                                       lam[:, 2 * layer + c:2 * layer + c + 1])
                        link(ins)
                signal(lam_exp)
                dve.wait_ge(lam_exp, 2)
                for layer in range(2):
                    link(vec.tensor_tensor(lam[:, 2 * layer:2 * layer + 1], lam[:, 2 * layer + 1:2 * layer + 2],
                                           lam[:, 2 * layer:2 * layer + 1], ALU.subtract))
                    link(vec.tensor_scalar(lam[:, 2 * layer:2 * layer + 1], lam[:, 2 * layer:2 * layer + 1],
                                           -lam_init(layer), None, ALU.add))

            def retention(s):
                dve.wait_ge(table_in, 16)
                keep_plain(s.turn, 0)
                keep_plain(s.turn + 1, 8)
                decay = table[:, 0:1024].rearrange("p (j c) -> p j c", j=RET_HEADS)
                for j in range(RET_HEADS):
                    dve.wait_ge(ret_scored, j + 1)
                    if j >= 2:
                        dve.wait_ge(ret_done, 2 * (j - 1))
                    st, b = tmp[:, (j % 2) * 512:], bank[4 + j % 2]
                    vec.tensor_tensor(st[:, 0:256], b[:, 0:256], decay[:, j, :], ALU.mult)
                    vec.tensor_tensor(st[:, 256:384], b[:, 256:384], decay[:, j, 0:128], ALU.mult).then_inc(ret_masked, 1)
                dve.wait_ge(ret_taken, 2 * RET_HEADS)
                signal(table_free)
                rstd(16, 8, RET_V)
                o = pv(6144)
                for j in range(RET_HEADS):
                    for t in range(T):
                        oj = o[:, t, j * RET_V:(j + 1) * RET_V]
                        ins = vec.scalar_tensor_tensor(
                            out=oj, in0=oj, scalar=stat[:, 16 + 2 * j + t:17 + 2 * j + t],
                            in1=o[:, t, 4096 + j * RET_V:4096 + (j + 1) * RET_V], op0=ALU.mult, op1=ALU.mult)
                    if j % 2:
                        ins.then_inc(mixed, 1)
                keep_split(s.turn + 2, 0)
                keep_split(s.turn + 3, 8)

            def rope(col, scratch):
                x = pv(3072)[:, :, col:col + 1024].rearrange("p t (h d) -> p t h d", h=8)
                x1, x2 = x[:, :, :, 0:16], x[:, :, :, 16:32]
                cos, sin = (table[:, o:o + 32].rearrange("p (t h c) -> p t h c", t=T, h=1)
                            .broadcast_to([P, T, 8, 16]) for o in (ROPE0, ROPE0 + 32))
                a, b = (scratch[:, o:o + 256].rearrange("p (t h c) -> p t h c", t=T, h=8) for o in (0, 256))
                vec.tensor_tensor(a, x1, sin, ALU.mult)
                link(vec.tensor_tensor(b, x2, sin, ALU.mult))
                vec.tensor_tensor(x1, x1, cos, ALU.mult)
                link(vec.tensor_tensor(x2, x2, cos, ALU.mult))
                vec.tensor_tensor(x1, x1, b, ALU.subtract)
                link(vec.tensor_tensor(x2, x2, a, ALU.add))

            def attention(s):
                if s.which == "moba":
                    dve.wait_ge(late_in, 96)
                    for t in range(T):
                        dve.wait_ge(taken[t], s.out)
                    rope(0, tmp)
                    rope(1024, tmp)
                if s.which == "diff":
                    dve.wait_ge(unskewed, 16)
                signal(mixed)
                keep_plain(s.turn, 0)
                keep_plain(s.turn + 1, 8)
                H, C = s.n_heads, s.comps

                def masked(i):
                    j = i // C
                    dve.wait_ge(scored, s.soft + i + 1)
                    if i >= 2:
                        dve.wait_ge(exped, s.soft + i - 1)
                    lg, b = proj[:, SOFT0 + (i % 2) * 512:], bank[4 + i % 2]
                    if not s.causal:
                        link(vec.tensor_scalar(lg[:, 0:512], b[:, :], s.scale, None, ALU.mult))
                    else:
                        m = proj[:, BIAS0 + j * S:BIAS0 + (j + 1) * S] if s.which == "diff" else \
                            table[:, CAUSAL0:CAUSAL0 + S]
                        vec.scalar_tensor_tensor(out=lg[:, 0:P], in0=b[:, 0:P], scalar=s.scale, in1=m[:, P:S],
                                                 op0=ALU.mult, op1=ALU.add)
                        link(vec.scalar_tensor_tensor(out=lg[:, S:2 * S], in0=b[:, S:2 * S], scalar=s.scale,
                                                      in1=m[:, :], op0=ALU.mult, op1=ALU.add))
                    for t in range(T):
                        n = P * (t + 1) if s.causal else S
                        ins = vec.tensor_reduce(stat[:, 16 + 2 * i + t:17 + 2 * i + t], lg[:, t * S:t * S + n], AX.X,
                                                ALU.max, negate=True)
                    ins.then_inc(maxed, 1)

                def combine(j):
                    dve.wait_ge(exped, s.soft + 2 * j + 2)
                    link(vec.reciprocal(stat[:, 80 + 4 * j:84 + 4 * j], stat[:, 48 + 4 * j:52 + 4 * j]))
                    link(vec.tensor_scalar(stat[:, 82 + 4 * j:84 + 4 * j], stat[:, 82 + 4 * j:84 + 4 * j],
                                           lam[:, 2 * s.layer:2 * s.layer + 1], None, ALU.mult))
                    for t in range(T):
                        n = P * (t + 1)
                        e0, e1 = (tmp[:, ((j % 2) * 2 + c) * 512 + t * S:][:, 0:n] for c in range(2))
                        link(vec.tensor_scalar(e0, e0, stat[:, 80 + 4 * j + t:81 + 4 * j + t], None, ALU.mult))
                        ins = vec.scalar_tensor_tensor(out=e0, in0=e1, scalar=stat[:, 82 + 4 * j + t:83 + 4 * j + t],
                                                       in1=e0, op0=ALU.mult, op1=ALU.add)
                    ins.then_inc(combined, 1)

                def take(j):
                    dve.wait_ge(head_done, s.heads + j + 1)
                    o = bank[2 + j % 2]
                    if C == 2:
                        ins = vec.tensor_copy(yv[:, :, j * s.dv:(j + 1) * s.dv],
                                              o[:, 0:T * s.dv].rearrange("p (t d) -> p t d", t=T))
                    else:
                        link(vec.reciprocal(stat[:, 80 + 2 * j:82 + 2 * j], stat[:, 48 + 2 * j:50 + 2 * j]))
                        for t in range(T):
                            ins = vec.tensor_scalar(yv[:, t, j * s.dv:(j + 1) * s.dv], o[:, t * s.dv:(t + 1) * s.dv],
                                                    stat[:, 80 + 2 * j + t:81 + 2 * j + t], None, ALU.mult)
                    ins.then_inc(head_taken, 1)

                for j in range(H):
                    for c in range(C):
                        masked(C * j + c)
                    if C == 2:
                        combine(j)
                    if j >= 2:
                        take(j - 2)
                take(H - 2)
                take(H - 1)
                if s.which == "diff":
                    group_norm(table[:, 1024 + s.layer * P:1024 + (s.layer + 1) * P], 1.0 - lam_init(s.layer),
                               s.heads + H)
                dve.wait_ge(head_taken, s.heads + H)
                signal(mixed)
                keep_split(s.turn + 2, 0)

            def group_norm(g, factor, taken_count=None):
                if taken_count is not None:
                    dve.wait_ge(head_taken, taken_count)
                y16 = y[:, :].rearrange("p (n d) -> p n d", n=16)
                t16 = tmp[:, :].rearrange("p (n d) -> p n d", n=16)
                link(vec.tensor_tensor(tmp[:, :], y[:, :], y[:, :], ALU.mult))
                link(vec.tensor_reduce(stat[:, 16:32], t16, AX.X, ALU.add))
                rstd(16, 16, P)
                if factor != 1.0:
                    link(vec.tensor_scalar(stat[:, 16:32], stat[:, 16:32], factor, None, ALU.mult))
                link(vec.tensor_tensor(y16, y16, stat[:, 16:32].rearrange("p (n a) -> p n a", a=1)
                                       .broadcast_to([P, 16, P]), ALU.mult))
                link(vec.tensor_tensor(y16, y16, g.rearrange("p (a d) -> p a d", a=1).broadcast_to([P, 16, P]),
                                       ALU.mult))

            def lower_bound():
                lb = stat[:, 128:160].rearrange("p (k l) -> p k l", l=4)
                dve.wait_ge(lb_in, 16)
                link(vec.tensor_reduce(stat[:, 176:184], lb, AX.X, ALU.max))
                vec.tensor_tensor(lb, lb, stat[:, 176:184].rearrange("p (k l) -> p k l", l=1)
                                  .broadcast_to([P, 8, 4]), ALU.subtract).then_inc(lb_exp, 1)
                dve.wait_ge(lb_exp, 2)
                link(vec.tensor_reduce(stat[:, 176:184], lb, AX.X, ALU.add))
                link(vec.reciprocal(stat[:, 176:184], stat[:, 176:184]))
                link(vec.tensor_tensor(lb, lb, stat[:, 176:184].rearrange("p (k l) -> p k l", l=1)
                                       .broadcast_to([P, 8, 4]), ALU.mult))
                link(vec.tensor_tensor(stat[:, 176:184], lb[:, :, 0], lb[:, :, 1], ALU.add))
                link(vec.tensor_tensor(stat[:, 176:184], stat[:, 176:184], lb[:, :, 0], ALU.subtract))
                signal(lb_ready)

            def keep_bound():
                for b in range(2):
                    dve.wait_ge(lb_spread, b + 1)
                    ins = vec.tensor_copy(table[:, b * 512:(b + 1) * 512], bank[6 + b][:, :])
                link(ins)

            def hgrn(s):
                v = pv(4096)
                f, lb = v[:, :, 1024:2048], table[:, 0:1024].rearrange("p (t n) -> p t n", t=1).broadcast_to([P, T, D])
                keep_bound()
                dve.wait_ge(late_in, 96)
                dve.wait_ge(hg_sig, 1)
                link(vec.tensor_tensor(tv, f, lb, ALU.mult))
                link(vec.tensor_tensor(f, f, tv, ALU.subtract))
                link(vec.tensor_tensor(f, f, lb, ALU.add))
                link(vec.tensor_scalar(yv, f, -1.0, 1.0, ALU.mult, ALU.add))
                vec.tensor_scalar(f, f, 1e-19, None, ALU.max).then_inc(hg_f, 1)
                dve.wait_ge(hg_sig, 2)
                signal(mixed)
                keep_plain(s.turn, 0)
                keep_plain(s.turn + 1, 8)
                at_b = [at_of(b) for b in range(4)]
                for b in range(4):
                    dve.wait_ge(hg_prod, b + 1)
                    vec.tensor_tensor(at_b[b], bank[4 + b][:, :].rearrange("p (n m) -> p n m", n=4),
                                      ident[:, :].rearrange("p (n m) -> p n m", n=1).broadcast_to([P, 4, P]),
                                      ALU.mult).then_inc(hg_kept, 1)
                qf, kf = qk[:, 0:2048], qk[:, 2048:4096]
                for lv in range(HG_LEVELS):
                    L = 1 << lv
                    dve.wait_ge(hg_decay, 4 * (lv + 1))
                    dve.wait_ge(hg_prod, 4 * (lv + 1))
                    e, x, q_, k_ = (a.rearrange("p (n b l) -> p n b l", b=2, l=L)
                                    for a in (y[:, :], tmp[:, :], qf, kf))
                    vec.tensor_tensor(x[:, :, 1], e[:, :, 1], q_[:, :, 1], ALU.mult)
                    vec.tensor_tensor(x[:, :, 0], e[:, :, 0], k_[:, :, 0], ALU.mult).then_inc(hg_x, 1)
                    mask = proj[:, MASK0 + lv * P:MASK0 + (lv + 1) * P].bitcast(U32)\
                        .rearrange("p (n m) -> p n m", n=1).broadcast_to([P, 4, P])
                    for b in range(4):
                        dve.wait_ge(hg_prod, 4 * (lv + 1) + b + 1)
                        dve.wait_ge(hg_kept, 4 * (lv + 1) - 3 + b)
                        vec.copy_predicated(at_b[b], mask,
                                            bank[4 + b][:, :].rearrange("p (n m) -> p n m", n=4)).then_inc(hg_kept, 1)
                dve.wait_ge(hg_decay, 4 * (HG_LEVELS + 1))
                dve.wait_ge(hg_prod, 4 * (HG_LEVELS + 1))
                e, x, q_, k_ = (a.rearrange("p (n t l) -> p n t l", t=T, l=P) for a in (y[:, :], tmp[:, :], qf, kf))
                vec.tensor_tensor(x[:, :, 1], e[:, :, 1], q_[:, :, 1], ALU.mult)
                vec.tensor_tensor(x[:, :, 0], e[:, :, 0], k_[:, :, 0], ALU.mult).then_inc(hg_x, 1)
                for b in range(2):
                    dve.wait_ge(hg_prod, 4 * (HG_LEVELS + 1) + b + 1)
                    ins = vec.tensor_copy(table[:, b * 512:(b + 1) * 512], bank[4 + b][:, :])
                ins.then_inc(hg_kept, 1)
                for b in range(4):
                    dve.wait_ge(hg_out, b + 1)
                    t, half = b // 2, b % 2
                    ins = vec.tensor_copy(yv[:, t, half * 512:(half + 1) * 512], bank[b][:, :])
                link(ins)
                group_norm(table[:, 1280:1408], 1.0)
                vec.tensor_tensor(yv, yv, v[:, :, 3072:4096], ALU.mult).then_inc(mixed, 1)
                keep_split(s.turn + 2, 0)

            def sgu(s):
                u, g = pv(2048)[:, :, 0:1024], pv(2048)[:, :, 1024:2048]
                dve.wait_ge(sg_w_in, 48)
                w = proj[:, 4096:5120].rearrange("p (g t) -> p g t", g=8)
                link(vec.tensor_tensor(w, w, tril_mask(), ALU.mult))
                dve.wait_ge(gelus, 1)
                link(vec.tensor_tensor(tv, g, g, ALU.mult))
                link(vec.tensor_reduce(stat[:, 0:2], tv, AX.X, ALU.add))
                rstd(0, 2, D)
                for t in range(T):
                    ins = vec.scalar_tensor_tensor(out=g[:, t, :], in0=g[:, t, :], scalar=stat[:, t:t + 1],
                                                   in1=proj[:, 5120:6144], op0=ALU.mult, op1=ALU.mult)
                ins.then_inc(sg_w_ready, 1)
                dve.wait_ge(gelus, 2)
                for grp in range(8):
                    dve.wait_ge(sg_mixed, grp // 2 + 1)
                    c = slice(grp * P, (grp + 1) * P)
                    for t in range(T):
                        b = bank[4 + grp // 2][:, (grp % 2) * S + t * P:][:, 0:P]
                        ins = vec.scalar_tensor_tensor(out=yv[:, t, c], in0=b, scalar=stat[:, 128 + grp:129 + grp],
                                                       in1=u[:, t, c], op0=ALU.add, op1=ALU.mult)
                ins.then_inc(mixed, 1)
                keep_split(s.turn, 0)

            def tril_mask():
                m = proj[:, CUM0 + (HG_LEVELS + 1) * P:CUM0 + (HG_LEVELS + 2) * P]
                return m.rearrange("p (a t) -> p a t", a=1).broadcast_to([P, 8, P])

            for p in range(WP):
                low_wide(0, p)
            lambdas()
            for s in PLAN:
                if s.kind == "norm":
                    norm(s, yv)
                    keep_split(s.turn, s.chunk)
                elif s.kind == "between":
                    norm(s, hv)
                    dve.wait_ge(normed, 2 * (s.norm + 1))
                    signal(h_ready)
                    lower_bound()
                elif s.kind == "finish":
                    norm(s, yv)
                    dve.wait_ge(normed, 2 * (s.norm + 1))
                    signal(stored)
                elif s.kind == "linear":
                    linear(s)
                elif s.kind == "residual":
                    residual(s)
                elif s.kind == "gated":
                    gated(s)
                elif s.kind == "retention":
                    retention(s)
                elif s.kind == "attention":
                    attention(s)
                elif s.kind == "hgrn":
                    hgrn(s)
                elif s.kind == "sgu":
                    sgu(s)

        @block.tensor
        def _(pe):
            def three(o, hi, lo, wh, wl, start, stop):
                pe.matmul(o, hi, wh, start=start, stop=False)
                pe.matmul(o, hi, wl, start=False, stop=False)
                return pe.matmul(o, lo, wh, start=False, stop=stop)

            def wide_block(n, q, chunk, start=True, stop=True):
                for t in range(T):
                    if start and not (isinstance(q, int) and q == 0):
                        pe.wait_ge(taken[t], q)
                    for p in range(WP):
                        if t == 0:
                            pe.wait_ge(split_lw, WP * n + p + 1)
                        for k in range(KP):
                            c = KP * p + k
                            w = slice(c * WIDE, (c + 1) * WIDE)
                            x = slice(t * P, (t + 1) * P)
                            mm = three(bank[4 + t][:, :], xhv[:, chunk + c, x], xlv[:, chunk + c, x],
                                       high_w[:, w], low_w[:, w], start and c == 0, stop and c == KC - 1)
                        if t == T - 1:
                            mm.then_inc(used_w, 1)
                        elif p == WP - 1:
                            mm.then_inc(rows0_done, 1)

            def turn(m, src):
                if m:
                    pe.wait_ge(kept_h, kept(m))
                    pe.wait_ge(kept_l, kept(m))
                for b in range(4):
                    for c in range(2):
                        for t in range(T):
                            k = 2 * b + c
                            mm = pe.transpose(bank[b][:, c * S + t * P:c * S + (t + 1) * P],
                                              src[:, t, k * P:(k + 1) * P], ident[:, :])
                    mm.then_inc(turned, 1)

            def wait_kept(m):
                pe.wait_ge(kept_h, kept(m + 1))
                pe.wait_ge(kept_l, kept(m + 1))

            def linear(s):
                if s.out == 0:
                    wide_block(s.wide, 0, s.chunk)
                    with pe.Fori(1, s.blocks) as i:
                        wide_block(s.wide + i, s.out + i, s.chunk)
                else:
                    with pe.Fori(0, s.blocks) as i:
                        wide_block(s.wide + i, s.out + i, s.chunk)

            def residual(s):
                for half in range(2):
                    for k in range(s.halves):
                        wide_block(s.wide + half * s.halves + k, s.out + half, KC * k, k == 0, k == s.halves - 1)

            def router(s):
                for t in range(T):
                    for i, part in enumerate((xhv, xlv)):
                        for k in range(KC):
                            w = table[:, ROUTER0 + (s.moe * KC + k) * ROUTER:][:, 0:ROUTER]
                            mm = pe.matmul(bank[7][:, t * ROUTER:(t + 1) * ROUTER],
                                           part[:, k, t * P:(t + 1) * P].bitcast(F32), w,
                                           start=i == 0 and k == 0, stop=i == 1 and k == KC - 1)
                mm.then_inc(used_router, 1)
                pe.wait_ge(grouped, s.moe + 1)
                upto = proj[:, CUM0 + (HG_LEVELS + 1) * P:CUM0 + (HG_LEVELS + 2) * P]
                ones = table[:, ONE0:ONE0 + 1].broadcast_to([P, P])
                one_g = [tmp[:, 24 + 4 * t:28 + 4 * t] for t in range(T)]
                pe.matmul(bank[7][:, 64:68], upto, one_g[0], start=True, stop=True)
                pe.matmul(bank[7][:, 68:72], upto, one_g[1], start=True, stop=False)
                pe.matmul(bank[7][:, 68:72], ones, one_g[0], start=False, stop=True)
                pe.matmul(bank[7][:, 72:76], ones, one_g[0], start=True, stop=False)
                pe.matmul(bank[7][:, 72:76], ones, one_g[1], start=False, stop=True).then_inc(ranked, 1)

            def sparse(s):
                way = ways[s.moe]

                def gather(g):
                    pick = [qk[:, PICK0 + (t * GROUPS + g) * P:][:, 0:P] for t in range(T)]
                    for t in range(T):
                        mm = pe.transpose(bank[6][:, S + t * P:S + (t + 1) * P], pick[t], ident[:, :])
                    mm.then_inc(way.gathered, 1)
                    if g >= 2:
                        pe.wait_ge(way.added, 4 * (g - 1))
                    for t in range(T):
                        pe.matmul(bank[2 * (g % 2)][:, 0:EXPERTS], pick[t], tmp[:, WI0 + 4 * t:WI0 + 4 * t + 4],
                                  start=t == 0, stop=t == T - 1)
                    for k in range(KC):
                        for t in range(T):
                            mm = pe.matmul(bank[5 + 2 * (k // 4)][:, (k % 4) * P:(k % 4 + 1) * P],
                                           yv[:, t, k * P:(k + 1) * P], pick[t], start=t == 0, stop=t == T - 1)
                        if k % 4 == 3:
                            mm.then_inc(way.gathered, 1)

                def scatter(g):
                    pe.wait_ge(way.z_left, g + 1)
                    pe.wait_ge(way.z_right, g + 1)
                    for i in range(2 * T):
                        t, half = i // 2, i % 2
                        if i >= 2:
                            pe.wait_ge(way.added, 4 * g + i - 1)
                        z = Z0 + (g % 2) * D + half * WIDE
                        pe.matmul(bank[5 + 2 * half][:, :], qk[:, SLOT0 + g * S + t * P:][:, 0:P], proj[:, z:z + WIDE],
                                  start=True, stop=True).then_inc(way.scattered, 1)

                def unit(u, g):
                    n = s.wide + u
                    for t in range(T):
                        pe.wait_ge(taken[t], s.out + u)
                    for p in range(WP):
                        pe.wait_ge(split_lw, WP * n + p + 1)
                        for k in range(KP):
                            c = KP * p + k
                            w, x = slice(c * WIDE, (c + 1) * WIDE), KC * (g % 2) + c
                            mm = three(bank[4][:, :], xhv[:, x, 0:P], xlv[:, x, 0:P], high_w[:, w], low_w[:, w],
                                       c == 0, c == KC - 1)
                            if c == KC - 2:
                                mm.then_inc(rows0_done, 1)
                        mm.then_inc(used_w, 1)

                def turn_hidden(u):
                    for t in range(T):
                        pe.wait_ge(taken[t], s.out + u + 1)
                    for c in range(DP):
                        o = GATED0 + FU + c * P
                        mm = pe.transpose(bank[6][:, c * P:(c + 1) * P], qk[:, o:o + P], ident[:, :])
                    mm.then_inc(hidden_turned, 1)

                def down(u, g, first=False, last=False):
                    pe.wait_ge(hidden_low, s.down + u + 1)
                    for p in range(DP):
                        pe.wait_ge(split_ld, DP * (s.down + u) + p + 1)
                        for half in range(2):
                            x = slice(p * P, (p + 1) * P)
                            w = slice(p * PIECE + half * WIDE, p * PIECE + (half + 1) * WIDE)
                            mm = three(bank[2 * (g % 2) + half][:, :], hidden_h[:, x], hidden_l[:, x],
                                       high_d[:, w], low_d[:, w], first and p == 0, last and p == DP - 1)
                        mm.then_inc(used_d, 1)

                pe.wait_ge(way.v_step, 1)
                gather(0)
                pe.wait_ge(way.gathered_l, 2)
                unit(0, 0)
                turn_hidden(0)
                for g in range(GROUPS):
                    u0 = g * GROUP_UNITS
                    if g:
                        pe.wait_ge(way.gathered_l, 2 * (g + 1))
                        unit(u0, g)
                        down(u0 - 1, g - 1, last=True)
                        turn_hidden(u0)
                    unit(u0 + 1, g)
                    down(u0, g, first=True)
                    turn_hidden(u0 + 1)
                    if g:
                        scatter(g - 1)
                    if g + 1 < GROUPS:
                        if g == 0:
                            pe.wait_ge(way.gathered_l, 2)
                        gather(g + 1)
                    with pe.Fori(u0 + 2, u0 + GROUP_UNITS) as u:
                        unit(u, g)
                        down(u - 1, g)
                        turn_hidden(u)
                down(MOE_UNITS - 1, GROUPS - 1, last=True)
                scatter(GROUPS - 1)

            def gated(s):
                if s.moe is None:
                    dense(s)
                    return
                pe.wait_ge(late_in, 96)
                router(s)
                pe.wait_ge(counted, s.moe + 1)
                with pe.If(pe.value_load(largest[0:1, 0:1], min_val=0, max_val=S) < P + 1):
                    sparse(s)
                with pe.Else():
                    dense(s)

            def dense(s):
                def turn_hidden(u):
                    for t in range(T):
                        pe.wait_ge(taken[t], s.out + u + 1)
                    for c in range(DP):
                        for t in range(T):
                            mm = pe.transpose(bank[6][:, c * S + t * P:c * S + (t + 1) * P],
                                              y[:, 512 + t * FU + c * P:512 + t * FU + (c + 1) * P], ident[:, :])
                    mm.then_inc(hidden_turned, 1)

                def down(u, first=False, last=False):
                    pe.wait_ge(hidden_low, s.down + u + 1)
                    for p in range(DP):
                        pe.wait_ge(split_ld, DP * (s.down + u) + p + 1)
                        for t in range(T):
                            for half in range(2):
                                x = slice(p * S + t * P, p * S + (t + 1) * P)
                                w = slice(p * PIECE + half * WIDE, p * PIECE + (half + 1) * WIDE)
                                mm = three(bank[2 * t + half][:, :], hidden_h[:, x], hidden_l[:, x],
                                           high_d[:, w], low_d[:, w], first and p == 0, last and p == DP - 1)
                        mm.then_inc(used_d, 1)

                wide_block(s.wide, s.out, 0)
                turn_hidden(0)
                wide_block(s.wide + 1, s.out + 1, 0)
                down(0, first=True)
                turn_hidden(1)
                with pe.Fori(2, s.units) as u:
                    wide_block(s.wide + u, s.out + u, 0)
                    down(u - 1)
                    turn_hidden(u)
                down(s.units - 1, last=True)

            def retention(s):
                v = pv(6144)
                pe.wait_ge(rotated, 1)
                turn(s.turn, v[:, :, 0:1024])
                pe.wait_ge(rotated, 2)
                turn(s.turn + 1, v[:, :, 1024:2048])
                wait_kept(s.turn + 1)

                def scores(j):
                    if j >= 2:
                        pe.wait_ge(ret_masked, j - 1)
                    b = bank[4 + j % 2]
                    for mt in range(T):
                        for c in range(2):
                            mm = pe.matmul(b[:, mt * S:mt * S + S - mt * P],
                                           qkv[:, 8 + 2 * j + c, mt * P:(mt + 1) * P],
                                           qkv[:, 2 * j + c, mt * P:S], start=c == 0, stop=c == 1)
                    mm.then_inc(ret_scored, 1)

                def heads(j):
                    pe.wait_ge(ret_masked, j + 1)
                    st = tmp[:, (j % 2) * 512:]
                    vj = [v[:, t, 2048 + j * RET_V:2048 + (j + 1) * RET_V] for t in range(T)]
                    if j:
                        pe.wait_ge(ret_taken, 2 * j - 1)
                    pe.matmul(bank[6][:, :], st[:, 0:P], vj[0], start=True, stop=True).then_inc(ret_done, 1)
                    if j:
                        pe.wait_ge(ret_taken, 2 * j)
                    pe.matmul(bank[7][:, :], st[:, P:S], vj[0], start=True, stop=False)
                    pe.matmul(bank[7][:, :], st[:, S:S + P], vj[1], start=False, stop=True).then_inc(ret_done, 1)

                scores(0)
                for j in range(RET_HEADS):
                    if j + 1 < RET_HEADS:
                        scores(j + 1)
                    heads(j)
                pe.wait_ge(mixed, 1)
                turn(s.turn + 2, v[:, :, 0:1024])
                pe.wait_ge(mixed, 2)
                turn(s.turn + 3, v[:, :, 1024:2048])
                wait_kept(s.turn + 3)

            def bias_table():
                pe.wait_ge(late_in, 96)
                pe.wait_ge(ret_taken, 2 * RET_HEADS)
                for j in range(8):
                    if j >= 2:
                        pe.wait_ge(bias_copied, j - 1)
                    pe.matmul(bank[6 + j % 2][:, 0:384], proj[0:33, 384 + j:385 + j].broadcast_to([33, P]),
                              proj[0:33, 0:384], start=True, stop=True).then_inc(bias_rows, 1)

            def attention(s):
                v = pv(s.width)
                pe.wait_ge(mixed, s.mixed + 1)
                for t in range(T):
                    pe.wait_ge(taken[t], s.out)
                turn(s.turn, v[:, :, 0:1024])
                turn(s.turn + 1, v[:, :, 1024:2048])
                wait_kept(s.turn + 1)
                H, C, dv = s.n_heads, s.comps, s.dv

                def scores(i):
                    j, c = i // C, i % C
                    if i >= 2:
                        pe.wait_ge(maxed, s.soft + i - 1)
                    r = slice(c * 64, (c + 1) * 64) if C == 2 else slice(0, P)
                    for t in range(T):
                        n = P * (t + 1) if s.causal else S
                        for k in range(s.chunks):
                            mm = pe.matmul(bank[4 + i % 2][:, t * S:t * S + n],
                                           qkv[r, s.chunks * j + k, t * P:(t + 1) * P],
                                           qkv[r, 8 + s.chunks * j + k, 0:n], start=k == 0, stop=k == s.chunks - 1)
                    mm.then_inc(scored, 1)

                def turn_probs(j):
                    if C == 2:
                        pe.wait_ge(combined, 8 * s.layer + j + 1)
                    else:
                        pe.wait_ge(exped, s.soft + j + 1)
                    if j >= 2:
                        pe.wait_ge(probs_kept, s.heads + j - 1)
                    for kt in range(T):
                        for t in range(T):
                            if s.causal and kt > t:
                                continue
                            e = tmp[:, (j % 2) * 1024 + t * S + kt * P:][:, 0:P]
                            mm = pe.transpose(bank[6 + j % 2][:, kt * S + t * P:kt * S + (t + 1) * P], e, ident[:, :])
                    mm.then_inc(probs_turned, 1)

                def head(j):
                    pe.wait_ge(probs_kept, s.heads + j + 1)
                    if j >= 2:
                        pe.wait_ge(head_taken, s.heads + j - 1)
                    slot = proj[:, SOFT0 + 1024 + (j % 2) * 512:]
                    for t in range(T):
                        kts = range(t + 1) if s.causal else range(T)
                        for kt in kts:
                            mm = pe.matmul(bank[2 + j % 2][:, t * dv:(t + 1) * dv],
                                           slot[:, kt * S + t * P:kt * S + (t + 1) * P],
                                           v[:, kt, 2048 + j * dv:2048 + (j + 1) * dv],
                                           start=kt == 0, stop=kt == kts[-1])
                    mm.then_inc(head_done, 1)

                for j in range(H):
                    for c in range(C):
                        scores(C * j + c)
                    if j:
                        turn_probs(j - 1)
                    if j >= 2:
                        head(j - 2)
                turn_probs(H - 1)
                head(H - 2)
                head(H - 1)
                pe.wait_ge(mixed, s.mixed + 2)
                turn(s.turn + 2, yv)
                wait_kept(s.turn + 2)

            def spread_bound():
                pe.wait_ge(lb_ready, 1)
                for j in range(8):
                    mm = pe.matmul(bank[6 + j // 4][:, (j % 4) * P:(j % 4 + 1) * P],
                                   stat[:, 176 + j:177 + j].broadcast_to([P, P]), ident[:, :], start=True, stop=True)
                    if j % 4 == 3:
                        mm.then_inc(lb_spread, 1)

            def hgrn(s):
                v = pv(4096)
                spread_bound()
                pe.wait_ge(mixed, s.mixed + 1)
                turn(s.turn, v[:, :, 0:1024])
                turn(s.turn + 1, yv)
                wait_kept(s.turn + 1)
                pe.wait_ge(hg_log, 1)

                def sums(lv):
                    for j in range(8):
                        if lv and j % 2 == 0:
                            pe.wait_ge(hg_decay, 4 * (lv - 1) + j // 2 + 1)
                        for t in range(T):
                            m = lv if lv < HG_LEVELS else HG_LEVELS + t
                            mm = pe.matmul(bank[j // 2][:, (j % 2) * S + t * P:(j % 2) * S + (t + 1) * P],
                                           v[:, t, 1024 + j * P:1024 + (j + 1) * P],
                                           proj[:, CUM0 + m * P:CUM0 + (m + 1) * P], start=True, stop=True)
                        if j % 2:
                            mm.then_inc(hg_sums, 1)

                def products(lv):
                    if lv:
                        pe.wait_ge(hg_x, lv)
                    for n in range(16):
                        if n % 4 == 0 and lv:
                            pe.wait_ge(hg_kept, 4 * (lv - 1) + n // 4 + 1)
                        j, t = n // 2, n % 2
                        c = slice(j * S + t * P, j * S + (t + 1) * P)
                        a, b = (tmp[:, c], tmp[:, c]) if lv else (qk[:, 2048 + j * S + t * P:][:, 0:P], qk[:, c])
                        mm = pe.matmul(bank[4 + n // 4][:, (n % 4) * P:(n % 4 + 1) * P], a, b, start=True, stop=True)
                        if n % 4 == 3:
                            mm.then_inc(hg_prod, 1)

                sums(0)
                products(0)
                for lv in range(HG_LEVELS):
                    sums(lv + 1)
                    products(lv + 1)
                pe.wait_ge(hg_x, HG_LEVELS + 1)
                for j in range(8):
                    if j % 4 == 0:
                        pe.wait_ge(hg_kept, 4 * HG_LEVELS + j // 4 + 1)
                    mm = pe.matmul(bank[4 + j // 4][:, (j % 4) * P:(j % 4 + 1) * P], tmp[:, j * S:j * S + P],
                                   tmp[:, j * S + P:(j + 1) * S], start=True, stop=True)
                    if j % 4 == 3:
                        mm.then_inc(hg_prod, 1)
                pe.wait_ge(hg_kept, 4 * (HG_LEVELS + 1) + 1)
                for t in range(T):
                    for j in range(8):
                        o = bank[2 * t + j // 4][:, (j % 4) * P:(j % 4 + 1) * P]
                        at = at_of(j // 2)[:, (j % 2) * 2 + t, :]
                        mm = pe.matmul(o, at, v[:, t, 2048 + j * P:2048 + (j + 1) * P], start=True, stop=t == 0)
                        if t:
                            mm = pe.matmul(o, table[:, j * P:(j + 1) * P], v[:, 0, 2048 + j * P:2048 + (j + 1) * P],
                                           start=False, stop=True)
                        if j % 4 == 3:
                            mm.then_inc(hg_out, 1)
                pe.wait_ge(mixed, s.mixed + 2)
                turn(s.turn + 2, yv)
                wait_kept(s.turn + 2)

            def sgu(s):
                pe.wait_ge(sg_w_ready, 1)
                pe.wait_ge(taken[0], s.out)
                pe.wait_ge(taken[1], s.out)
                for grp in range(8):
                    for t in range(T):
                        mm = pe.matmul(bank[4 + grp // 2][:, (grp % 2) * S + t * P:(grp % 2) * S + (t + 1) * P],
                                       proj[:, 4096 + grp * P:4096 + (grp + 1) * P],
                                       pv(2048)[:, t, 1024 + grp * P:1024 + (grp + 1) * P], start=True, stop=True)
                    if grp % 2:
                        mm.then_inc(sg_mixed, 1)
                pe.wait_ge(mixed, s.mixed + 1)
                turn(s.turn, yv)
                wait_kept(s.turn)

            pe.wait_ge(ident_in, 16)
            for s in PLAN:
                if s.kind == "norm":
                    if s.norm == 1:
                        bias_table()
                    pe.wait_ge(normed, 2 * (s.norm + 1))
                    turn(s.turn, yv)
                    wait_kept(s.turn)
                elif s.kind == "linear":
                    linear(s)
                elif s.kind == "residual":
                    residual(s)
                elif s.kind == "gated":
                    gated(s)
                elif s.kind == "retention":
                    retention(s)
                elif s.kind == "attention":
                    attention(s)
                elif s.kind == "hgrn":
                    hgrn(s)
                elif s.kind == "sgu":
                    sgu(s)


def _wide(w):
    n = w.shape[1] // WIDE
    return w.reshape(WP, KP, P, n, WIDE).transpose(3, 0, 2, 1, 4).reshape(n, WP, P, PIECE)


def _gated(gate, up):
    n = gate.shape[1] // FU
    both = np.concatenate([gate.reshape(D, n, FU), up.reshape(D, n, FU)], axis=2)
    return _wide(both.reshape(D, n * WIDE))


def _out(w):
    m = w.shape[0] // D
    return np.concatenate([_wide(w[k * D:(k + 1) * D, c * WIDE:(c + 1) * WIDE]) for c in range(2) for k in range(m)])


def _streams(a):
    wide, down = [], []

    def moe(layer):
        for g in range(GROUPS):
            for e in range(EXPERTS):
                wide.append(_gated(a["expert_w_gate"][layer, g, e], a["expert_w_up"][layer, g, e]))
                down.append(a["expert_w_down"][layer, g, e].reshape(-1, DP, P, PIECE))

    wide += [_wide(a["ret_w_in"][0]), _out(a["ret_w_out"][0])]
    moe(0)
    wide += [_wide(a["w_kv"]), _wide(a["w_q"][0]), _out(a["w_o"][0])]
    moe(1)
    for i in range(4):
        mix = ("da", "hg", "sg")[i % 3]
        wide += [_wide(a[mix + "_w_in_2"][i // 3]), _out(a[mix + "_w_out_2"][i // 3])]
        wide += [_wide(a["ca_w_q_2"][i]), _wide(a["ca_w_kv_2"][i]), _out(a["ca_w_o_2"][i])]
        gu = a["ffn_w_gu_2"][i]
        wide.append(_gated(gu[:, :D_FF], gu[:, D_FF:]))
        down.append(a["ffn_w_down_2"][i].reshape(-1, DP, P, PIECE))
    return np.concatenate(wide), np.concatenate(down)


def _rope_table(dim, theta):
    half = dim // 2
    inv = (1.0 / (np.float32(theta) ** (np.arange(half, dtype=np.float32) / np.float32(half)))).astype(np.float32)
    ang = np.arange(S, dtype=np.float32)[:, None] * inv[None, :]

    def lay(x):
        return x.astype(np.float32).reshape(T, P, half).transpose(1, 0, 2).reshape(P, T * half)
    return lay(np.cos(ang)), lay(np.sin(ang))


def _constants():
    f = np.float32
    p = np.arange(P)[:, None]
    c = np.arange(S)[None, :]
    gamma = np.log1p(-np.power(2.0, -5.0 - np.arange(RET_HEADS)))
    decay = [np.where(c >= p, np.exp(g * np.maximum(c - p, 0)), 0.0) * RET_QK ** -0.5 for g in gamma]
    ret = np.concatenate([*decay, *_rope_table(RET_QK, 10000.0)], axis=1).astype(f)
    causal = np.where(c <= p + P, 0.0, NEG)
    iota_one = np.concatenate([np.tile(np.arange(P), (P, 1)), np.ones((P, 1))], axis=1)
    small = np.concatenate([np.zeros((P, CAUSAL0)), causal, *_rope_table(32, 500000.0), iota_one], axis=1).astype(f)
    s, t = np.arange(P)[:, None], np.arange(P)[None, :]
    sums, masks = [], []
    for lv in range(HG_LEVELS):
        L = 1 << lv
        mid = (t // (2 * L)) * 2 * L + L - 1
        second = t > mid
        sums.append(np.where(second, (s > mid) & (s <= t), (s > t) & (s <= mid)))
        masks.append((s // (2 * L) == t // (2 * L)) & (s <= mid) & second)
    sums += [s > t, s <= t]
    hg = np.concatenate(sums + masks, axis=1).astype(f)
    dist = 255 - np.arange(384)
    n = np.maximum(dist, 0)
    nf = np.maximum(n, 16).astype(f)
    large = np.minimum(16 + (np.log(nf / f(16)) / f(math.log(8.0)) * f(16)).astype(np.int32), 31)
    bucket = np.where(n < 16, n, large)
    buckets = np.zeros((33, 384), f)
    buckets[bucket, np.arange(384)] = dist >= 0
    buckets[32] = np.where(dist < 0, NEG, 0.0)
    return ret, small, hg, buckets


def kernel(**inputs):
    import concourse.bacc as bacc
    from concourse.bass_utils import run_bass_kernel_spmd

    a = {k: np.asarray(v) for k, v in inputs.items()}
    f = np.float32
    ret, small, hg, buckets = _constants()
    router = np.concatenate([a["router_group_w"], a["router_expert_w"].transpose(0, 2, 1, 3).reshape(2, D, -1)], axis=2)
    small[:, ROUTER0:CAUSAL0] = router.reshape(2, KC, P, ROUTER).transpose(2, 0, 1, 3).reshape(P, -1)
    gains = [a["ret_norm"][0], a["ffn_norm"][0], a["kv_norm"], a["attn_norm"][0], a["ffn_norm"][1], a["final_norm"],
             a["norm_mem_2"]]
    for i in range(4):
        gains += [a["norm_mix_2"][i], a["norm_cross_2"][i], a["norm_ffn_2"][i]]
    gains.append(a["norm_final_2"])
    wide, down = _streams(a)
    rel = np.ones((33, 8), f)
    rel[:32] = a["rel_bias_2"].T
    arrays = {
        "x": a["x"][0], "mem": a["mem_2"][0], "wide": wide, "down": down, "gains": np.stack(gains),
        "ident": np.eye(P, dtype=f), "ret_table": ret, "small_table": small, "hg_consts": hg, "buckets": buckets,
        "rel_bias": rel,
        "head_gains": np.concatenate([a["da_subln_2"].reshape(-1), a["hg_onorm_2"].reshape(-1)])[None],
        "router_bias": np.concatenate([np.concatenate([a["router_group_b"][i], a["router_expert_b"][i].reshape(-1)])
                                       for i in range(2)])[None],
        "lambdas": np.stack([a["da_" + n + "_2"] for n in ("lq1", "lk1", "lq2", "lk2")], axis=1).reshape(1, -1),
        "lower_bounds": a["hg_lower_bounds_2"].reshape(4, 8, P).transpose(2, 1, 0).reshape(P, 32),
        "sg_w": a["sg_w_s_2"][0].transpose(2, 0, 1).reshape(P, -1), "sg_gain": a["sg_vnorm_2"],
        "sg_bias": a["sg_b_s_2"][0].T,
    }
    nc = bacc.Bacc("TRN2", target_bir_lowering=False, num_devices=1)
    dram = {}
    for name, v in arrays.items():
        arrays[name] = np.ascontiguousarray(v)
        dram[name] = nc.dram_tensor("in_" + name, v.shape, F32, kind="ExternalInput").ap()
    out = nc.dram_tensor("out_h", (S, D), F32, kind="ExternalOutput").ap()
    build(nc, dram, out)
    r = run_bass_kernel_spmd(nc, [{"in_" + k: v for k, v in arrays.items()}], core_ids=[0])
    return r.results[0]["out_h"].reshape(1, S, D)
```

```python
from contextlib import ExitStack
import math

import concourse.bass as bass
import numpy as np
from concourse import mybir

F32 = mybir.dt.float32
F32R = mybir.dt.float32r
U32 = mybir.dt.uint32
ALU = mybir.AluOpType
ACT = mybir.ActivationFunctionType
AX = mybir.AxisListType

P = 128
S = 256
T = S // P
D = 1024
KC = D // P
EPS = 1e-6
WIDE = 512
PIECE = 1024
WP = KC * WIDE // PIECE
KP = KC // WP
FU = 256
DP = FU // P
D_FF = int(math.ceil(8 * D / 3 / 256)) * 256
FFN_UNITS = D_FF // FU
GROUPS, EXPERTS, D_EXPERT = 4, 4, D // 2
MOE_UNITS = GROUPS * EXPERTS * D_EXPERT // FU
PER_EXPERT = D_EXPERT // FU
ROUTER = GROUPS + GROUPS * EXPERTS
RET_HEADS, RET_QK, RET_V = 4, 256, 512
HG_LEVELS = 7
NEG = -1e30

SOFT0 = 6144
BIAS0 = 8192
CUM0 = 10240
MASK0 = CUM0 + (HG_LEVELS + 2) * P
ROUTER0, CAUSAL0, ROPE0, IOTA0, ONE0 = 0, 320, 576, 640, 768
SLOT0, PICK0, GATED0 = 0, 1024, 2048
WI0 = 56
HEADS0 = 144
Z0 = 4096
GROUP_UNITS = MOE_UNITS // GROUPS


COUNTED = ("wide", "out", "down", "turn", "norm", "h", "soft", "heads", "mixed")


class Stage:

    def __init__(self, kind, count, chunk=0, src="h", blocks=0, width=0, col=0, halves=1, units=0, moe=None,
                 last=False, func="", fused=False, hook=False, early=False, n_heads=0, comps=1, chunks=1, dv=0, causal=False, scale=1.0, which="", layer=0):
        self.kind = kind
        self.wide, self.out, self.down, self.turn, self.norm, self.h, self.soft, self.heads, self.mixed = (
            count[k] for k in COUNTED)
        self.chunk, self.src, self.blocks, self.width, self.col = chunk, src, blocks, width, col
        self.halves, self.units, self.moe, self.last = halves, units, moe, last
        self.func, self.fused, self.hook, self.early = func, fused, hook, early
        self.n_heads, self.comps, self.chunks, self.dv = n_heads, comps, chunks, dv
        self.causal, self.scale, self.which, self.layer = causal, scale, which, layer


def plan():
    c = dict.fromkeys(COUNTED, 0)
    stages = []

    def add(kind, turns="", what=(), **counted):
        stages.append(Stage(kind, c, **dict(what)))
        for k, v in counted.items():
            c[k] += v
        for m in turns:
            c["turn"] += 1
            TURNS.append(m)

    def prenorm(src="h"):
        fused = src == "h" and stages[-1].kind in ("residual", "gated") and stages[-1].moe is None
        add("prenorm", what=dict(src=src, fused=fused), norm=1)

    def turn(src, mode, chunk=0, hook=False):
        early = stages[-1].kind == "prenorm" and stages[-1].fused
        add("turn", mode, dict(src=src, chunk=chunk, hook=hook, early=early))

    def linear(blocks, width, col=0, chunk=0, func=""):
        add("linear", what=dict(blocks=blocks, width=width, col=col, chunk=chunk, func=func), wide=blocks, out=blocks)

    def residual(halves=1):
        add("residual", what=dict(halves=halves), wide=2 * halves, out=2, h=1)

    def gated(units, moe, last=False):
        add("gated", what=dict(units=units, moe=moe, last=last), wide=units, out=units, down=units, h=1)

    def softmax(heads, comps, chunks, dv, causal, scale, width, which, layer):
        add("attention", what=dict(n_heads=heads, comps=comps, chunks=chunks, dv=dv, causal=causal,
                                   scale=scale, width=width, which=which, layer=layer),
            soft=heads * comps, heads=heads, mixed=2)
        turn("y", "s", hook=True)

    add("setup")
    prenorm()
    turn("norm", "s", hook=True)
    linear(6, 6144)
    turn("q rotated", "p")
    linear(2, 6144, col=6 * WIDE)
    turn("k rotated", "p", chunk=KC)
    linear(4, 6144, col=8 * WIDE, func="silu")
    add("retention", "ss", mixed=2)
    residual(2)
    prenorm()
    add("bias")
    turn("norm", "s")
    gated(MOE_UNITS, 0)
    prenorm()
    turn("norm", "s", hook=True)
    prenorm()
    linear(2, 3072, col=1024)
    turn("norm", "s", chunk=KC, hook=True)
    add("rope", what=dict(col=1024), mixed=1)
    linear(2, 3072, chunk=KC)
    turn("k roped", "p", chunk=KC)
    add("rope", what=dict(col=0), mixed=1)
    linear(1, 3072, col=2048)
    turn("q roped", "p")
    linear(1, 3072, col=2560)
    softmax(8, 1, 1, 128, True, 128.0 ** -0.5, 3072, "moba", 0)
    residual()
    prenorm()
    turn("norm", "s")
    gated(MOE_UNITS, 1)
    add("between", norm=1, h=1)
    for layer in range(4):
        prenorm()
        turn("norm", "s", hook=True)
        if layer % 3 == 0:
            if layer == 0:
                prenorm(src="mem")
                linear(2, 3072)
                turn("norm", "s", chunk=KC)
                linear(2, 3072, col=1024)
            else:
                linear(4, 3072)
            turn("q", "p")
            linear(1, 3072, col=2048)
            turn("k", "p", chunk=KC)
            linear(1, 3072, col=2560)
            softmax(8, 2, 1, 128, True, 64.0 ** -0.5, 3072, "diff", layer // 3)
        elif layer == 1:
            linear(2, 4096, func="silu")
            linear(2, 4096, col=1024, func="sigmoid")
            add("gates", mixed=1)
            linear(1, 4096, col=2048)
            turn("q", "p")
            linear(1, 4096, col=2560)
            turn("gates", "p", chunk=KC)
            linear(2, 4096, col=3072, func="silu")
            add("hgrn", mixed=2)
            turn("y", "s", hook=True)
        else:
            linear(2, 2048, col=1024, func="gelu")
            add("values")
            linear(2, 2048, func="gelu")
            add("sgu", mixed=2)
            turn("y", "s", hook=True)
        residual()
        prenorm()
        linear(2, 3072, col=1024, chunk=KC)
        turn("norm", "s", hook=True)
        linear(2, 3072)
        turn("k", "p", chunk=KC)
        linear(1, 3072, col=2048, chunk=KC)
        turn("q", "p")
        linear(1, 3072, col=2560, chunk=KC)
        softmax(4, 1, 2, 256, False, 256.0 ** -0.5, 3072, "cross", layer)
        residual()
        prenorm()
        turn("norm", "s", hook=True)
        gated(FFN_UNITS, None, last=layer == 3)
    add("finish", norm=1)
    return stages, c


TURNS = []
PLAN, TOTAL = plan()


def kept(m):
    n = sum(4 if k == "s" else 2 for k in TURNS[:m])
    return n


def after(s):
    return PLAN[PLAN.index(s) + 1]


def lam_init(layer):
    return 0.8 - 0.6 * math.exp(-0.3 * 3 * layer)


def build(nc, dram, out):
    ctx = ExitStack()
    with ctx:
        def sb(name, words, dt=F32):
            return ctx.enter_context(nc.sbuf_tensor(name, [P, words], dt))

        def sem(name):
            return ctx.enter_context(nc.semaphore(name))

        stage_w = sb("stage_w", WP * PIECE)
        stage_d = sb("stage_d", DP * PIECE)
        high_w, low_w = sb("high_w", WP * PIECE, F32R), sb("low_w", WP * PIECE, F32R)
        high_d, low_d = sb("high_d", DP * PIECE, F32R), sb("low_d", DP * PIECE, F32R)
        xh = sb("xh", 2 * KC * S, F32R)
        xl = sb("xl", 2 * KC * S, F32R)
        h = sb("h", T * D)
        proj = sb("proj", T * 6144)
        qk = sb("qk", 2 * KC * S)
        y = sb("y", T * D)
        tmp = sb("tmp", T * D)
        table = sb("table", 1536)
        gain = sb("gain", D)
        hidden_h, hidden_l = sb("hidden_h", T * FU, F32R), sb("hidden_l", T * FU, F32R)
        ident = sb("ident", P)
        stat = sb("stat", 192)
        comb = sb("comb", T * MOE_UNITS)
        lam = sb("lam", 4)
        largest = sb("largest", 1, mybir.dt.int32)
        minus_half = sb("minus_half", 1)
        xhv = xh[:, :].rearrange("p (k s) -> p k s", k=2 * KC)
        xlv = xl[:, :].rearrange("p (k s) -> p k s", k=2 * KC)
        qkv = qk[:, :].rearrange("p (k s) -> p k s", k=2 * KC)
        hv = h[:, :].rearrange("p (t d) -> p t d", t=T)
        yv = y[:, :].rearrange("p (t d) -> p t d", t=T)
        tv = tmp[:, :].rearrange("p (t d) -> p t d", t=T)

        def pv(width):
            return proj[:, 0:T * width].rearrange("p (t n) -> p t n", t=T)

        bank = [ctx.enter_context(nc.psum_tensor(f"bank{b}", [P, 512], F32)) for b in range(8)]
        skew = nc.dram_tensor("skew", (8 * P * 385,), F32).ap()

        def at_of(b):
            at = (b // 2) * 4096 + (b % 2) * 512
            return proj[:, at:at + 512].rearrange("p (n m) -> p n m", n=4)

        def part(v, b, chunk):
            c, t = chunk + 4 * (b % 2), b // 2
            return v[:, c:c + 4, t * P:(t + 1) * P]

        def part_bank(b):
            return bank[b][:, :].rearrange("p (k m) -> p k m", k=4)

        def hidden_of(s, u):
            if isinstance(u, int) and u == s.units - 1:
                return xh[:, 0:T * FU], xl[:, 0:T * FU]
            return hidden_h[:, :], hidden_l[:, :]

        def columns(s, i):
            return slice(s.col, s.col + WIDE) if s.blocks == 1 else bass.ds(s.col + i * WIDE, WIDE)

        landed_w = [sem(f"landed_w{p}") for p in range(WP)]
        landed_d = [sem(f"landed_d{p}") for p in range(DP)]
        split_hw, split_lw = sem("split_hw"), sem("split_lw")
        split_hd, split_ld = sem("split_hd"), sem("split_ld")
        used_w, used_d = sem("used_w"), sem("used_d")
        rows0_done = sem("rows0_done")
        taken = [sem("taken0"), sem("taken1")]
        turned, kept_h, kept_l = sem("turned"), sem("kept_h"), sem("kept_l")
        x_in, gain_in, mem_in, table_in = [sem("x_in0"), sem("x_in1")], sem("gain_in"), sem("mem_in"), sem("table_in")
        ident_in, lam_in, late_in = sem("ident_in"), sem("lam_in"), sem("late_in")
        mean_ready, rooted = sem("mean_ready"), sem("rooted")
        h_ready, down0_done = [sem("h_ready0"), sem("h_ready1")], sem("down0_done")
        squares, normed = sem("squares"), sem("normed")
        mixed = sem("mixed")
        silu_done, hidden_turned, hidden_high, hidden_low = (
            sem("silu_done"), sem("hidden_turned"), sem("hidden_high"), sem("hidden_low"))
        logits_done = sem("logits_done")
        v_step, s_step, g_step = sem("v_step"), sem("s_step"), sem("g_step")
        scored, maxed, exped, combined = sem("scored"), sem("maxed"), sem("exped"), sem("combined")
        probs_turned, probs_kept = sem("probs_turned"), sem("probs_kept")
        head_done, head_taken = sem("head_done"), sem("head_taken")
        rotated, used_router = sem("rotated"), sem("used_router")
        ret_scored, ret_masked, ret_done, ret_taken = (
            sem("ret_scored"), sem("ret_masked"), sem("ret_done"), sem("ret_taken"))
        bias_rows, bias_copied, skewed, unskewed = (
            sem("bias_rows"), sem("bias_copied"), sem("skewed"), sem("unskewed"))
        lam_exp, lb_in, lb_exp, lb_ready, lb_spread = (
            sem("lam_exp"), sem("lb_in"), sem("lb_exp"), sem("lb_ready"), sem("lb_spread"))
        hg_taken = sem("hg_taken")
        hg_f, hg_log, hg_sums, hg_decay, hg_x, hg_prod, hg_kept, hg_out = (
            sem("hg_f"), sem("hg_log"), sem("hg_sums"), sem("hg_decay"), sem("hg_x"),
            sem("hg_prod"), sem("hg_kept"), sem("hg_out"))
        sg_w_in, sg_w_ready, sg_mixed = (
            sem("sg_w_in"), sem("sg_w_ready"), sem("sg_mixed"))
        stored, out_stored = sem("stored"), sem("out_stored")
        table_free = sem("table_free")

        grouped, ranked, counted = sem("grouped"), sem("ranked"), sem("counted")

        class Way:
            def __init__(self, n):
                self.gathered, self.gathered_h, self.gathered_l = (
                    sem(f"gathered{n}"), sem(f"gathered_h{n}"), sem(f"gathered_l{n}"))
                self.slots_kept, self.z_left, self.z_right = (
                    sem(f"slots_kept{n}"), sem(f"z_left{n}"), sem(f"z_right{n}"))
                self.scattered, self.added, self.v_step = sem(f"scattered{n}"), sem(f"added{n}"), sem(f"way_v{n}")

        ways = [Way(n) for n in range(2)]
        def down0(s):
            return sum(p.kind == "gated" and p.moe is None for p in PLAN[:PLAN.index(s)]) + 1

        block = ctx.enter_context(nc.Block())

        @block.sync
        def _(sp):
            def load_wide(n, first=False):
                for p in range(WP):
                    if not first:
                        sp.wait_ge(split_lw, 4 * (n - 1) + p + 1)
                    src = dram["wide"][bass.ds(n, 1), p, :, :].rearrange("a p n -> p (a n)")
                    sp.dma_start(stage_w[:, p * PIECE:(p + 1) * PIECE], src).then_inc(landed_w[p], 16)

            def load_down(n, first=False):
                for p in range(DP):
                    if not first:
                        sp.wait_ge(split_ld, DP * (n - 1) + p + 1)
                    src = dram["down"][bass.ds(n, 1), p, :, :].rearrange("a p n -> p (a n)")
                    sp.dma_start(stage_d[:, p * PIECE:(p + 1) * PIECE], src).then_inc(landed_d[p], 16)

            for t in range(T):
                sp.dma_start(hv[:, t, :], dram["x"][t * P:(t + 1) * P, :]).then_inc(x_in[t], 16)
                if t == 0:
                    sp.dma_start(ident[:, :], dram["ident"]).then_inc(ident_in, 16)
            load_wide(0, first=True)
            for s in PLAN:
                if s.kind in ("linear", "residual"):
                    blocks = s.blocks if s.kind == "linear" else 2 * s.halves
                    if blocks == 1:
                        load_wide(s.wide + 1)
                    else:
                        with sp.Fori(1, blocks + 1) as i:
                            load_wide(s.wide + i)
                elif s.kind == "gated":
                    load_wide(s.wide + 1)
                    load_down(s.down, first=s.down == 0)
                    with sp.Fori(1, s.units - 1) as i:
                        load_wide(s.wide + 1 + i)
                        load_down(s.down + i)
                    if not s.last:
                        load_wide(s.wide + s.units)
                    load_down(s.down + s.units - 1)

        @block.gpsimd
        def _(pool):
            step, roots = [0], [0]

            def link(ins):
                step[0] += 1
                ins.then_inc(g_step, 1)
                pool.wait_ge(g_step, step[0])

            def root(at, n):
                roots[0] += 1
                pool.wait_ge(mean_ready, roots[0])
                nc.gpsimd.tensor_tensor(stat[:, at:at + n], stat[:, at:at + n],
                                        minus_half[:, :].broadcast_to([P, n]), ALU.pow).then_inc(rooted, 1)

            def load_gain(n):
                if n:
                    pool.wait_ge(normed, 2 * n)
                pool.dma_start(gain[:, :], dram["gains"][n:n + 1, :].broadcast_to([P, D])).then_inc(gain_in, 16)

            def setup():
                link(nc.gpsimd.memset(minus_half[:, :], -0.5))
                load_gain(0)
                pool.dma_start(qk[:, 0:512], dram["lambdas"].broadcast_to([P, 512])).then_inc(lam_in, 16)
                pool.dma_start(table[:, :], dram["ret_table"]).then_inc(table_in, 16)

            def rotate(col):
                x = pv(6144)[:, :, col:col + 1024].rearrange("p t (h a c) -> p t h a c", h=RET_HEADS, a=2)
                x1, x2 = x[:, :, :, 0, :], x[:, :, :, 1, :]
                cos, sin = (table[:, o:o + S].rearrange("p (t h c) -> p t h c", t=T, h=1)
                            .broadcast_to([P, T, RET_HEADS, P]) for o in (1024, 1280))
                a, b = (tmp[:, o:o + 1024].rearrange("p (t h c) -> p t h c", t=T, h=RET_HEADS)
                        for o in (0, 1024))
                eng = nc.gpsimd
                link(eng.tensor_tensor(a, x1, sin, ALU.mult))
                link(eng.tensor_tensor(b, x2, sin, ALU.mult))
                link(eng.tensor_tensor(x1, x1, cos, ALU.mult))
                link(eng.tensor_tensor(x2, x2, cos, ALU.mult))
                link(eng.tensor_tensor(x1, x1, b, ALU.subtract))
                return eng.tensor_tensor(x2, x2, a, ALU.add)

            def retention():
                pool.wait_ge(table_in, 16)
                for n in range(2):
                    for t in range(T):
                        pool.wait_ge(taken[t], 2 * (n + 1))
                    rotate(n * 1024).then_inc(rotated, 1)
                    pool.wait_ge(rotated, n + 1)

            def after_retention(s):
                pool.wait_ge(table_free, 1)
                pool.wait_ge(turned, 4 * (s.turn + 2))
                for dst, src in ((table[:, 0:ONE0 + 1], dram["small_table"]),
                                 (table[:, 1024:1408], dram["head_gains"].broadcast_to([P, 3 * P])),
                                 (proj[0:33, 0:384], dram["buckets"]),
                                 (proj[0:33, 384:392], dram["rel_bias"]),
                                 (proj[:, CUM0:MASK0 + HG_LEVELS * P], dram["hg_consts"]),
                                 (stat[:, 128:168], dram["router_bias"].broadcast_to([P, 2 * ROUTER]))):
                    pool.dma_start(dst, src).then_inc(late_in, 16)

            def skew_bias():
                pool.wait_ge(bias_copied, 8)
                rows = proj[:, 512:512 + 8 * 384].rearrange("p (h j) -> p h j", h=8)
                pool.dma_start(skew.rearrange("(h p j) -> p h j", h=8, j=385)[:, :, 0:384], rows).then_inc(skewed, 16)
                pool.wait_ge(skewed, 16)
                back = bass.AP(skew.tensor, 127, [[384, P], [P * 385, 8], [1, S]])
                pool.dma_start(proj[:, BIAS0:BIAS0 + 8 * S].rearrange("p (h k) -> p h k", h=8), back)\
                    .then_inc(unskewed, 16)

            for s in PLAN:
                if s.kind in ("prenorm", "between", "finish"):
                    for t in range(T):
                        root(t, 1)
                elif s.kind == "values":
                    root(0, T)
                elif s.kind == "hgrn" or s.kind == "attention" and s.which == "diff":
                    root(HEADS0, 16)
                if s.kind == "setup":
                    setup()
                elif s.kind == "turn" and s.src == "q rotated":
                    load_gain(1)
                    retention()
                elif s.kind == "retention":
                    root(16, T * RET_HEADS)
                    after_retention(s)
                elif s.kind in ("prenorm", "between") and s.norm >= 1:
                    load_gain(s.norm + 1)
                elif s.kind == "bias":
                    skew_bias()
                if s.kind == "between":
                    pool.dma_start(tv, dram["mem"].rearrange("(t p) d -> p t d", p=P)).then_inc(mem_in, 16)
                    pool.dma_start(stat[:, 128:160], dram["lower_bounds"]).then_inc(lb_in, 16)
                if s.kind == "linear" and s.width == 2048 and s.col:
                    pool.dma_start(proj[:, 4096:5120], dram["sg_w"]).then_inc(sg_w_in, 16)
                    pool.dma_start(proj[:, 5120:6144], dram["sg_gain"].broadcast_to([P, D])).then_inc(sg_w_in, 16)
                    pool.dma_start(stat[:, 128:136], dram["sg_bias"]).then_inc(sg_w_in, 16)

        @block.scalar
        def _(act):
            step = [0]

            def link(ins):
                step[0] += 1
                ins.then_inc(s_step, 1)
                act.wait_ge(s_step, step[0])

            def high_wide(n, p, first=False):
                act.wait_ge(landed_w[p], 16 * (n + 1))
                if not first:
                    act.wait_ge(used_w, WP * (n - 1) + p + 1)
                w = slice(p * PIECE, (p + 1) * PIECE)
                act.activation(high_w[:, w], stage_w[:, w], ACT.Copy).then_inc(split_hw, 1)

            def high_down(n, p, first=False):
                act.wait_ge(landed_d[p], 16 * (n + 1))
                if not first:
                    act.wait_ge(used_d, DP * (n - 1) + p + 1)
                w = slice(p * PIECE, (p + 1) * PIECE)
                act.activation(high_d[:, w], stage_d[:, w], ACT.Copy).then_inc(split_hd, 1)

            def keep_split(m, chunk, banks=range(4)):
                for b in banks:
                    act.wait_ge(turned, 4 * m + b + 1)
                    act.activation(part(xhv, b, chunk), part_bank(b), ACT.Copy).then_inc(kept_h, 1)

            def keep_plain(m, chunk):
                for b in range(2):
                    act.wait_ge(turned, 4 * m + b + 1)
                    act.activation(part(qkv, b, chunk), part_bank(b), ACT.Copy).then_inc(kept_h, 1)

            def square(s, t):
                mem = s.src == "mem"
                if mem:
                    act.wait_ge(mem_in, 16)
                elif s.h == 0:
                    act.wait_ge(x_in[t], 16)
                else:
                    act.wait_ge(h_ready[t], s.h)
                act.activation(yv[:, t, :], (tv if mem else hv)[:, t, :], ACT.Square, accum_out=stat[:, t:t + 1])\
                    .then_inc(squares, 1)

            def linear(s):
                out_v = pv(s.width)
                func = {"": ACT.Copy, "silu": ACT.Silu, "sigmoid": ACT.Sigmoid, "gelu": ACT.Gelu}[s.func]
                if s.norm == 4 and s.width == 3072:
                    act.wait_ge(skewed, 16)

                def one(i):
                    act.wait_ge(rows0_done, s.wide + i + 1)
                    act.activation(out_v[:, 0, columns(s, i)], bank[4][:, :], func).then_inc(taken[0], 1)
                    for p in range(WP - 1):
                        high_wide(s.wide + 1 + i, p)
                    if s.func:
                        act.wait_ge(used_w, WP * (s.wide + i + 1))
                        act.activation(out_v[:, 1, columns(s, i)], bank[5][:, :], func).then_inc(taken[1], 1)
                    high_wide(s.wide + 1 + i, WP - 1)

                if s.blocks == 1:
                    one(0)
                else:
                    with act.Fori(0, s.blocks) as i:
                        one(i)

            def residual(s):
                nxt = after(s)
                n = 2 * s.halves
                with act.Fori(0, n - 1) as i:
                    for p in range(WP):
                        high_wide(s.wide + 1 + i, p)
                square(nxt, 0)
                for p in range(WP - 1):
                    high_wide(s.wide + n, p)
                keep_early(nxt)
                high_wide(s.wide + n, WP - 1)
                square(nxt, 1)

            def keep_early(s):
                if after(s).early:
                    keep_split(after(s).turn, after(s).chunk, range(2))

            def sparse(s):
                way = ways[s.moe]

                def keep_gathered(g):
                    act.wait_ge(way.gathered, 3 * g + 1)
                    act.activation(qk[:, SLOT0 + g * S:SLOT0 + (g + 1) * S], bank[6][:, S:2 * S], ACT.Copy)\
                        .then_inc(way.slots_kept, 1)
                    for i in range(2):
                        act.wait_ge(way.gathered, 3 * g + i + 2)
                        c = KC * (g % 2) + 4 * i
                        act.activation(xhv[:, c:c + 4, 0:P], bank[5 + 2 * i][:, :].rearrange("p (k m) -> p k m", k=4),
                                       ACT.Copy).then_inc(way.gathered_h, 1)

                def keep_z(g):
                    act.wait_ge(used_d, DP * (s.down + GROUP_UNITS * (g + 1)))
                    if g >= 2:
                        act.wait_ge(way.scattered, 4 * (g - 1))
                    z = Z0 + (g % 2) * D
                    act.activation(proj[:, z:z + WIDE], bank[2 * (g % 2)][:, :], ACT.Copy).then_inc(way.z_left, 1)

                def unit(u, prefetch=True):
                    if prefetch:
                        for p in range(WP - 1):
                            high_wide(s.wide + u + 1, p)
                    act.wait_ge(used_w, WP * (s.wide + u + 1))
                    act.activation(qk[:, GATED0:GATED0 + FU], bank[4][:, 0:FU], ACT.Silu).then_inc(silu_done, 2)
                    high_wide(s.wide + u + 1, WP - 1)

                def hidden(u, first=False):
                    act.wait_ge(hidden_turned, s.down + u + 1)
                    act.activation(hidden_h[:, 0:FU], bank[6][:, 0:FU], ACT.Copy).then_inc(hidden_high, 1)
                    for p in range(DP):
                        high_down(s.down + u, p, first)

                keep_gathered(0)
                unit(0)
                for g in range(GROUPS):
                    u0 = g * GROUP_UNITS
                    if g:
                        hidden(u0 - 1)
                        unit(u0)
                    hidden(u0, first=s.down + u0 == 0)
                    if g:
                        keep_z(g - 1)
                    unit(u0 + 1)
                    if g + 1 < GROUPS:
                        keep_gathered(g + 1)
                    with act.Fori(u0 + 2, u0 + GROUP_UNITS) as u:
                        hidden(u - 1)
                        unit(u)
                hidden(MOE_UNITS - 1)
                keep_z(GROUPS - 1)

            def gated(s):
                def silu(u, t):
                    if t == 0:
                        act.wait_ge(rows0_done, s.wide + u + 1)
                    else:
                        act.wait_ge(used_w, WP * (s.wide + u + 1))
                    act.activation(y[:, t * FU:(t + 1) * FU], bank[4 + t][:, 0:FU], ACT.Silu).then_inc(silu_done, 1)

                def unit(u, prefetch=True):
                    silu(u, 0)
                    if prefetch:
                        for p in range(WP - 1):
                            high_wide(s.wide + u + 1, p)
                    silu(u, 1)
                    if prefetch:
                        high_wide(s.wide + u + 1, WP - 1)

                def hidden(u, first=False):
                    act.wait_ge(hidden_turned, s.down + u + 1)
                    hh = hidden_of(s, u)[0]
                    act.activation(hh, bank[6][:, :], ACT.Copy).then_inc(hidden_high, 1)
                    for p in range(DP):
                        high_down(s.down + u, p, first)

                unit(0)
                hidden(0, first=s.down == 0)
                unit(1)
                with act.Fori(2, s.units - (1 if s.last else 0)) as u:
                    hidden(u - 1)
                    unit(u)
                if s.last:
                    hidden(s.units - 2)
                    unit(s.units - 1, prefetch=False)
                hidden(s.units - 1)
                if s.moe is None and after(s).kind == "prenorm":
                    square(after(s), 0)
                    keep_early(after(s))
                    square(after(s), 1)

            def retention(s):
                o = pv(6144)
                for j in range(RET_HEADS):
                    for t in range(T):
                        act.wait_ge(ret_done, T * j + t + 1)
                        act.activation(y[:, t * 512:(t + 1) * 512], bank[6 + t][:, :], ACT.Square,
                                       accum_out=stat[:, 16 + T * j + t:17 + T * j + t])
                        act.activation(o[:, t, j * RET_V:(j + 1) * RET_V], bank[6 + t][:, :], ACT.Copy)\
                           .then_inc(ret_taken, 1)
                keep_split(s.turn, 0)
                keep_split(s.turn + 1, 8)

            def keep_bias_rows():
                for j in range(8):
                    act.wait_ge(bias_rows, j + 1)
                    act.activation(proj[:, 512 + j * 384:512 + (j + 1) * 384], bank[6 + j % 2][:, 0:384],
                                   ACT.Copy).then_inc(bias_copied, 1)

            def attention(s):
                def exps(i):
                    j = i // s.comps
                    act.wait_ge(maxed, s.soft + i + 1)
                    if j >= 2:
                        act.wait_ge(probs_turned, s.heads + j - 1)
                    for t in range(T):
                        n = P * (t + 1) if s.causal else S
                        e = tmp[:, ((j % 2) * 2 + i % s.comps) * 512 + t * S:][:, 0:n]
                        ins = act.activation(e, proj[:, SOFT0 + (i % 2) * 512 + t * S:][:, 0:n], ACT.Exp,
                                             bias=stat[:, 16 + 2 * i + t:17 + 2 * i + t],
                                             accum_out=stat[:, 48 + 2 * i + t:49 + 2 * i + t])
                    ins.then_inc(exped, 1)

                def keep_probs(j):
                    act.wait_ge(probs_turned, s.heads + j + 1)
                    if j >= 2:
                        act.wait_ge(head_done, s.heads + j - 1)
                    slot = SOFT0 + 1024 + (j % 2) * 512
                    src = bank[6 + j % 2]
                    if s.causal:
                        act.activation(proj[:, slot:slot + S], src[:, 0:S], ACT.Copy)
                        ins = act.activation(proj[:, slot + 384:slot + 512], src[:, 384:512], ACT.Copy)
                    else:
                        ins = act.activation(proj[:, slot:slot + 512], src[:, :], ACT.Copy)
                    ins.then_inc(probs_kept, 1)

                def take(j):
                    act.wait_ge(head_done, s.heads + j + 1)
                    o = bank[2 + j % 2]
                    for t in range(T):
                        n = HEADS0 + 8 * t + j
                        act.activation(table[:, (j % 4) * S + t * P:][:, 0:P], o[:, t * P:(t + 1) * P], ACT.Square,
                                       accum_out=stat[:, n:n + 1])
                    act.activation(yv[:, :, j * P:(j + 1) * P], o[:, 0:S].rearrange("p (t d) -> p t d", t=T),
                                   ACT.Copy).then_inc(head_taken, 1)

                H = s.n_heads
                for j in range(H):
                    for c in range(s.comps):
                        exps(s.comps * j + c)
                    if j:
                        keep_probs(j - 1)
                    if s.comps == 2 and j >= 3:
                        take(j - 3)
                keep_probs(H - 1)
                if s.comps == 2:
                    for j in range(H - 3, H):
                        take(j)

            def gates(s):
                f = pv(4096)[:, :, 1024:2048]
                act.wait_ge(hg_f, 1)
                act.activation(f, f, ACT.Ln).then_inc(hg_log, 1)

            def hgrn(s):
                for lv in range(HG_LEVELS + 1):
                    for b in range(4):
                        act.wait_ge(hg_sums, 4 * lv + b + 1)
                        if lv:
                            act.wait_ge(hg_x, lv)
                        act.activation(y[:, b * 512:(b + 1) * 512], bank[b][:, :], ACT.Exp).then_inc(hg_decay, 1)
                act.wait_ge(hg_x, HG_LEVELS + 1)
                for b in range(4):
                    act.wait_ge(hg_out, b + 1)
                    for n in range(4 * b, 4 * b + 4):
                        act.activation(tmp[:, n * P:(n + 1) * P], bank[b][:, (n % 4) * P:(n % 4 + 1) * P], ACT.Square,
                                       accum_out=stat[:, HEADS0 + n:HEADS0 + n + 1])
                    act.activation(y[:, b * 512:(b + 1) * 512], bank[b][:, :], ACT.Copy).then_inc(hg_taken, 1)

            for p in range(WP):
                high_wide(0, p, first=True)
            for s in PLAN:
                if s.kind in ("prenorm", "between", "finish") and not s.fused:
                    for t in range(T):
                        square(s, t)
                if s.kind == "turn":
                    if TURNS[s.turn] == "s":
                        keep_split(s.turn, s.chunk, range(2 if s.early else 0, 4))
                    else:
                        keep_plain(s.turn, s.chunk)
                    if s.turn == 0:
                        act.wait_ge(lam_exp, 1)
                        act.activation(lam[:, 0:4], lam[:, 0:4], ACT.Exp).then_inc(lam_exp, 1)
                elif s.kind == "bias":
                    keep_bias_rows()
                elif s.kind == "prenorm" and s.src == "mem":
                    act.wait_ge(lb_exp, 1)
                    act.activation(stat[:, 128:160], stat[:, 128:160], ACT.Exp).then_inc(lb_exp, 1)
                elif s.kind == "linear":
                    linear(s)
                elif s.kind == "residual":
                    residual(s)
                elif s.kind == "gated":
                    if s.moe is not None:
                        act.wait_ge(logits_done, 2 * s.moe + 1)
                        act.activation(stat[:, 0:8], stat[:, 0:8], ACT.Exp)
                        act.activation(stat[:, 8:10], stat[:, 8:10], ACT.Exp).then_inc(logits_done, 1)
                        act.wait_ge(counted, s.moe + 1)
                        with act.If(act.value_load(largest[0:1, 0:1], min_val=0, max_val=S) < P + 1):
                            sparse(s)
                        with act.Else():
                            gated(s)
                    else:
                        gated(s)
                elif s.kind == "retention":
                    retention(s)
                elif s.kind == "attention":
                    attention(s)
                elif s.kind == "gates":
                    gates(s)
                elif s.kind == "hgrn":
                    hgrn(s)
            act.wait_ge(stored, 1)
            act.dma_start(out.rearrange("(t p) d -> p t d", p=P), yv).then_inc(out_stored, 16)
            act.wait_ge(out_stored, 16)

        @block.vector
        def _(dve):
            step, roots = [0], [0]
            vec = nc.vector

            def link(ins):
                step[0] += 1
                ins.then_inc(v_step, 1)
                dve.wait_ge(v_step, step[0])

            def signal(what, at=190):
                vec.memset(stat[:, at:at + 1], 0.0).then_inc(what, 1)

            def low_wide(n, p):
                dve.wait_ge(split_hw, WP * n + p + 1)
                w = slice(p * PIECE, (p + 1) * PIECE)
                vec.tensor_tensor(low_w[:, w], stage_w[:, w], high_w[:, w].bitcast(F32), ALU.subtract)\
                   .then_inc(split_lw, 1)

            def low_down(n, p):
                dve.wait_ge(split_hd, DP * n + p + 1)
                w = slice(p * PIECE, (p + 1) * PIECE)
                vec.tensor_tensor(low_d[:, w], stage_d[:, w], high_d[:, w].bitcast(F32), ALU.subtract)\
                   .then_inc(split_ld, 1)

            def keep_split(m, chunk, banks=range(4)):
                for b in banks:
                    dve.wait_ge(kept_h, kept(m) + b + 1)
                    vec.tensor_tensor(part(xlv, b, chunk), part_bank(b), part(xhv, b, chunk).bitcast(F32),
                                      ALU.subtract).then_inc(kept_l, 1)

            def keep_plain(m, chunk):
                for b in range(2, 4):
                    dve.wait_ge(turned, 4 * m + b + 1)
                    vec.tensor_copy(part(qkv, b, chunk), part_bank(b)).then_inc(kept_l, 1)

            def rstd(at, n, width):
                vec.tensor_scalar(stat[:, at:at + n], stat[:, at:at + n], 1.0 / width, EPS, ALU.mult, ALU.add)\
                    .then_inc(mean_ready, 1)
                roots[0] += 1
                dve.wait_ge(rooted, roots[0])

            def mean(s, t):
                dve.wait_ge(squares, 2 * s.norm + t + 1)
                vec.tensor_scalar(stat[:, t:t + 1], stat[:, t:t + 1], 1.0 / D, EPS, ALU.mult, ALU.add)\
                    .then_inc(mean_ready, 1)

            def scale(s, t):
                roots[0] += 1
                dve.wait_ge(rooted, roots[0])
                dve.wait_ge(gain_in, 16 * (s.norm + 1))
                if s.src == "mem":
                    dve.wait_ge(mem_in, 16)
                elif s.h == 0:
                    dve.wait_ge(x_in[t], 16)
                else:
                    dve.wait_ge(h_ready[t], s.h)
                src, dst = tv if s.src == "mem" else hv, hv if s.kind == "between" else yv
                vec.scalar_tensor_tensor(out=dst[:, t, :], in0=src[:, t, :], scalar=stat[:, t:t + 1],
                                         in1=gain[:, :], op0=ALU.mult, op1=ALU.mult).then_inc(normed, 1)

            def norm(s):
                for t in range(T):
                    mean(s, t)
                for t in range(T):
                    scale(s, t)

            def linear(s):
                out_v = pv(s.width)
                if s.norm == 4 and s.width == 3072:
                    dve.wait_ge(skewed, 16)

                def one(i):
                    for p in range(WP - 1):
                        low_wide(s.wide + 1 + i, p)
                    if not s.func:
                        dve.wait_ge(used_w, WP * (s.wide + i + 1))
                        vec.tensor_copy(out_v[:, 1, columns(s, i)], bank[5][:, :]).then_inc(taken[1], 1)
                    low_wide(s.wide + 1 + i, WP - 1)

                if s.blocks == 1:
                    one(0)
                else:
                    with dve.Fori(0, s.blocks) as i:
                        one(i)

            def residual(s):
                nxt = after(s)

                def add(t, half, i):
                    if t == 0:
                        dve.wait_ge(rows0_done, s.wide + i + 1)
                    else:
                        dve.wait_ge(used_w, WP * (s.wide + i + 1))
                    hs = hv[:, t, half * WIDE:(half + 1) * WIDE]
                    vec.tensor_tensor(hs, hs, bank[4 + t][:, :], ALU.add).then_inc(taken[t], 1)

                for i in range(2 * s.halves - 1):
                    last = i == s.halves - 1
                    if last:
                        add(0, 0, i)
                    for p in range(WP - 1):
                        low_wide(s.wide + 1 + i, p)
                    if last:
                        add(1, 0, i)
                    low_wide(s.wide + 1 + i, WP - 1)
                i = 2 * s.halves - 1
                add(0, 1, i)
                dve.wait_ge(taken[0], s.out + 2)
                signal(h_ready[0], 190)
                mean(nxt, 0)
                low_wide(s.wide + 1 + i, 0)
                scale(nxt, 0)
                for p in range(1, WP - 2):
                    low_wide(s.wide + 1 + i, p)
                keep_early(nxt)
                low_wide(s.wide + 1 + i, WP - 2)
                add(1, 1, i)
                dve.wait_ge(taken[1], s.out + 2)
                signal(h_ready[1], 191)
                low_wide(s.wide + 1 + i, WP - 1)
                mean(nxt, 1)
                scale(nxt, 1)

            def keep_early(s):
                if after(s).early:
                    keep_split(after(s).turn, after(s).chunk, range(2))

            def route(s):
                lg = stat[:, 16:16 + T * ROUTER].rearrange("p (t n) -> p t n", t=T)
                pg = stat[:, 0:8].rearrange("p (t g) -> p t g", t=T)
                dv2 = stat[:, 8:10].rearrange("p (t g) -> p t g", t=T)
                rank = stat[:, 168:176].rearrange("p (t g) -> p t g", t=T)

                def rows(a, g):
                    return tmp[:, a:a + T * g].rearrange("p (t g) -> p t g", t=T)

                m, km, gate, v1, v2, w1, w2 = (rows(2 * i, 1) for i in range(7))
                key, one_g, el, e1, e2, wi, rest = (rows(16 + 8 * i, 4) for i in range(7))
                prod = rows(128, 16)

                def wide(a, g):
                    return a.broadcast_to([P, T, g])

                def best(values, top, one):
                    link(vec.tensor_reduce(top, values, AX.X, ALU.max))
                    link(vec.tensor_tensor(key, values, wide(top, 4), ALU.is_equal))
                    link(vec.tensor_tensor(key, key, rank, ALU.mult))
                    link(vec.tensor_reduce(km, key, AX.X, ALU.max))
                    link(vec.tensor_tensor(one, key, wide(km, 4), ALU.is_equal))

                for t in range(T):
                    for g in range(4):
                        ins = vec.memset(stat[:, 168 + 4 * t + g:169 + 4 * t + g], float(4 - g))
                link(ins)
                dve.wait_ge(late_in, 96)
                dve.wait_ge(used_router, s.moe + 1)
                bias = stat[:, 128 + ROUTER * s.moe:128 + ROUTER * (s.moe + 1)].rearrange("p (t n) -> p t n", t=1)
                link(vec.tensor_tensor(lg, bank[7][:, 0:T * ROUTER].rearrange("p (t n) -> p t n", t=T),
                                       bias.broadcast_to([P, T, ROUTER]), ALU.add))
                best(lg[:, :, 0:4], m, one_g)
                signal(grouped)
                link(vec.tensor_tensor(pg, lg[:, :, 0:4], wide(m, 4), ALU.subtract))
                ev = lg[:, :, 4:ROUTER].rearrange("p t (g e) -> p t e g", g=GROUPS)
                pr = prod.rearrange("p t (e g) -> p t e g", e=EXPERTS)
                for t in range(T):
                    ins = vec.tensor_tensor(pr[:, t], ev[:, t], one_g[:, t:t + 1, :].broadcast_to([P, EXPERTS, GROUPS]),
                                            ALU.mult)
                link(ins)
                link(vec.tensor_reduce(el, pr, AX.X, ALU.add))
                best(el, v1, e1)
                link(vec.tensor_scalar(rest, e1, 3e38, None, ALU.mult))
                link(vec.tensor_tensor(rest, el, rest, ALU.subtract))
                best(rest, v2, e2)
                link(vec.tensor_tensor(dv2, v2, v1, ALU.subtract))
                signal(logits_done)
                dve.wait_ge(logits_done, 2 * s.moe + 2)
                link(vec.tensor_reduce(gate, pg, AX.X, ALU.add))
                link(vec.reciprocal(gate, gate))
                link(vec.tensor_scalar(w1, dv2, 1.0, None, ALU.add))
                link(vec.reciprocal(w1, w1))
                link(vec.tensor_tensor(w1, w1, gate, ALU.mult))
                link(vec.tensor_tensor(w2, w1, dv2, ALU.mult))
                vec.tensor_tensor(e1, e1, wide(w1, 4), ALU.mult)
                link(vec.tensor_tensor(e2, e2, wide(w2, 4), ALU.mult))
                link(vec.tensor_tensor(wi, e1, e2, ALU.add))
                dve.wait_ge(ranked, s.moe + 1)
                link(vec.tensor_scalar(tmp[:, 160:168], bank[7][:, 64:72], -1.0, None, ALU.add))
                link(vec.tensor_reduce(tmp[:, 168:169], bank[7][:, 72:76], AX.X, ALU.max))
                vec.tensor_copy(largest[:, :], tmp[:, 168:169]).then_inc(counted, 1)
                return one_g, wi

            def every_unit(s, one_g, wi):
                way = ways[s.moe]
                cv = comb[:, :].rearrange("p (t g e u) -> p t g e u", t=T, g=GROUPS, e=EXPERTS)
                for t in range(T):
                    for u in range(PER_EXPERT):
                        ins = vec.tensor_tensor(
                            cv[:, t, :, :, u], one_g[:, t, :].rearrange("p (g e) -> p g e", e=1)
                            .broadcast_to([P, GROUPS, EXPERTS]),
                            wi[:, t:t + 1, :].broadcast_to([P, GROUPS, EXPERTS]), ALU.mult)
                ins.then_inc(way.v_step, 1)
                dve.wait_ge(way.v_step, 1)

            def sparse(s):
                way = ways[s.moe]
                for t in range(T):
                    for g in range(GROUPS):
                        ins = vec.tensor_scalar(qk[:, PICK0 + (t * GROUPS + g) * P:][:, 0:P], table[:, IOTA0:IOTA0 + P],
                                                tmp[:, 160 + 4 * t + g:161 + 4 * t + g],
                                                tmp[:, 24 + 4 * t + g:25 + 4 * t + g], ALU.is_equal, ALU.mult)
                ins.then_inc(way.v_step, 1)

                def keep_gathered(g):
                    dve.wait_ge(way.gathered, 3 * g + 2)
                    w = bank[2 * (g % 2)][:, 0:EXPERTS].rearrange("p (e a) -> p e a", a=1)
                    vec.tensor_copy(comb[:, g * GROUP_UNITS:(g + 1) * GROUP_UNITS].rearrange("p (e a) -> p e a", e=EXPERTS),
                                    w.broadcast_to([P, EXPERTS, PER_EXPERT])).then_inc(way.v_step, 1)
                    for i in range(2):
                        dve.wait_ge(way.gathered_h, 2 * g + i + 1)
                        c = KC * (g % 2) + 4 * i
                        vec.tensor_tensor(xlv[:, c:c + 4, 0:P], bank[5 + 2 * i][:, :].rearrange("p (k m) -> p k m", k=4),
                                          xhv[:, c:c + 4, 0:P].bitcast(F32), ALU.subtract).then_inc(way.gathered_l, 1)

                def keep_z(g):
                    dve.wait_ge(used_d, DP * (s.down + GROUP_UNITS * (g + 1)))
                    if g >= 2:
                        dve.wait_ge(way.scattered, 4 * (g - 1))
                    z = Z0 + (g % 2) * D + WIDE
                    vec.tensor_copy(proj[:, z:z + WIDE], bank[2 * (g % 2) + 1][:, :]).then_inc(way.z_right, 1)

                def add(g):
                    for i in range(2 * T):
                        t, half = i // 2, i % 2
                        dve.wait_ge(way.scattered, 4 * g + i + 1)
                        if g:
                            dve.wait_ge(way.added, 4 * (g - 1) + i + 1)
                        hs = hv[:, t, half * WIDE:(half + 1) * WIDE]
                        vec.tensor_tensor(hs, hs, bank[5 + 2 * half][:, :], ALU.add).then_inc(way.added, 1)

                def unit(u):
                    for p in range(WP - 1):
                        low_wide(s.wide + u + 1, p)
                    dve.wait_ge(silu_done, 2 * (s.down + u) + 2)
                    for c in range(2):
                        w = comb[:, u:u + 1] if isinstance(u, int) else comb[:, bass.ds(u, 1)]
                        vec.scalar_tensor_tensor(out=qk[:, GATED0 + FU + c * P:GATED0 + FU + (c + 1) * P],
                                                 in0=qk[:, GATED0 + c * P:GATED0 + (c + 1) * P], scalar=w,
                                                 in1=bank[4][:, FU + c * P:FU + (c + 1) * P], op0=ALU.mult,
                                                 op1=ALU.mult).then_inc(taken[c], 1)
                    low_wide(s.wide + u + 1, WP - 1)

                def hidden(u):
                    dve.wait_ge(hidden_high, s.down + u + 1)
                    vec.tensor_tensor(hidden_l[:, 0:FU], bank[6][:, 0:FU], hidden_h[:, 0:FU].bitcast(F32), ALU.subtract)\
                       .then_inc(hidden_low, 1)
                    for p in range(DP):
                        low_down(s.down + u, p)

                keep_gathered(0)
                dve.wait_ge(way.v_step, 2)
                unit(0)
                for g in range(GROUPS):
                    u0 = g * GROUP_UNITS
                    if g:
                        hidden(u0 - 1)
                        dve.wait_ge(way.v_step, g + 2)
                        unit(u0)
                    hidden(u0)
                    if g:
                        keep_z(g - 1)
                    unit(u0 + 1)
                    if g:
                        add(g - 1)
                    if g + 1 < GROUPS:
                        keep_gathered(g + 1)
                    with dve.Fori(u0 + 2, u0 + GROUP_UNITS) as u:
                        hidden(u - 1)
                        unit(u)
                hidden(MOE_UNITS - 1)
                keep_z(GROUPS - 1)
                add(GROUPS - 1)
                dve.wait_ge(way.added, 4 * GROUPS)

            def gated(s):
                if s.moe is None:
                    dense(s)
                    return
                one_g, wi = route(s)
                dve.wait_ge(counted, s.moe + 1)
                with dve.If(dve.value_load(largest[0:1, 0:1], min_val=0, max_val=S) < P + 1):
                    sparse(s)
                with dve.Else():
                    every_unit(s, one_g, wi)
                    dense(s)
                for t in range(T):
                    signal(h_ready[t], 190 + t)

            def dense(s):
                def gate(u, t):
                    dve.wait_ge(silu_done, 2 * (s.down + u) + t + 1)
                    up, sl = bank[4 + t][:, FU:2 * FU], y[:, t * FU:(t + 1) * FU]
                    o = y[:, 512 + t * FU:512 + (t + 1) * FU]
                    if s.moe is None:
                        ins = vec.tensor_tensor(o, sl, up, ALU.mult)
                    else:
                        w = comb[:, t * MOE_UNITS + u:t * MOE_UNITS + u + 1] if isinstance(u, int) else \
                            comb[:, bass.ds(u + t * MOE_UNITS, 1)]
                        ins = vec.scalar_tensor_tensor(out=o, in0=sl, scalar=w, in1=up, op0=ALU.mult, op1=ALU.mult)
                    ins.then_inc(taken[t], 1)

                def unit(u, prefetch=True):
                    gate(u, 0)
                    if prefetch:
                        for p in range(WP - 1):
                            low_wide(s.wide + u + 1, p)
                    gate(u, 1)
                    if prefetch:
                        low_wide(s.wide + u + 1, WP - 1)

                def hidden(u):
                    dve.wait_ge(hidden_high, s.down + u + 1)
                    hh, hl = hidden_of(s, u)
                    vec.tensor_tensor(hl, bank[6][:, :], hh.bitcast(F32), ALU.subtract).then_inc(hidden_low, 1)
                    for p in range(DP):
                        low_down(s.down + u, p)

                unit(0)
                with dve.Fori(1, s.units - (1 if s.last else 0)) as u:
                    hidden(u - 1)
                    unit(u)
                if s.last:
                    hidden(s.units - 2)
                    unit(s.units - 1, prefetch=False)
                hidden(s.units - 1)
                for t in range(T):
                    if t == 0:
                        dve.wait_ge(down0_done, down0(s))
                    else:
                        dve.wait_ge(used_d, DP * (s.down + s.units))
                    for half in range(2):
                        hs = hv[:, t, half * WIDE:(half + 1) * WIDE]
                        ins = vec.tensor_tensor(hs, hs, bank[2 * t + half][:, :], ALU.add)
                    if s.moe is None:
                        ins.then_inc(h_ready[t], 1)
                        if after(s).kind == "prenorm":
                            if t:
                                keep_early(after(s))
                            mean(after(s), t)
                            scale(after(s), t)

            def lambdas():
                dve.wait_ge(lam_in, 16)
                v = qk[:, 0:512].rearrange("p (l a d) -> p l a d", l=2, a=4)
                for layer in range(2):
                    for c in range(2):
                        ins = vec.tensor_tensor_reduce(qk[:, 512:576], v[:, layer, 2 * c, :], v[:, layer, 2 * c + 1, :],
                                                       1.0, 0.0, ALU.mult, ALU.add,
                                                       lam[:, 2 * layer + c:2 * layer + c + 1])
                        link(ins)
                signal(lam_exp)
                dve.wait_ge(lam_exp, 2)
                for layer in range(2):
                    link(vec.tensor_tensor(lam[:, 2 * layer:2 * layer + 1], lam[:, 2 * layer + 1:2 * layer + 2],
                                           lam[:, 2 * layer:2 * layer + 1], ALU.subtract))
                    link(vec.tensor_scalar(lam[:, 2 * layer:2 * layer + 1], lam[:, 2 * layer:2 * layer + 1],
                                           -lam_init(layer), None, ALU.add))

            def retention(s):
                dve.wait_ge(table_in, 16)
                decay = table[:, 0:1024].rearrange("p (j c) -> p j c", j=RET_HEADS)
                for j in range(RET_HEADS):
                    dve.wait_ge(ret_scored, j + 1)
                    if j >= 2:
                        dve.wait_ge(ret_done, 2 * (j - 1))
                    st, b = tmp[:, (j % 2) * 512:], bank[4 + j % 2]
                    vec.tensor_tensor(st[:, 0:256], b[:, 0:256], decay[:, j, :], ALU.mult)
                    vec.tensor_tensor(st[:, 256:384], b[:, 256:384], decay[:, j, 0:128], ALU.mult).then_inc(ret_masked, 1)
                dve.wait_ge(ret_taken, 2 * RET_HEADS)
                signal(table_free)
                rstd(16, 8, RET_V)
                o = pv(6144)
                for j in range(RET_HEADS):
                    for t in range(T):
                        oj = o[:, t, j * RET_V:(j + 1) * RET_V]
                        ins = vec.scalar_tensor_tensor(
                            out=oj, in0=oj, scalar=stat[:, 16 + 2 * j + t:17 + 2 * j + t],
                            in1=o[:, t, 4096 + j * RET_V:4096 + (j + 1) * RET_V], op0=ALU.mult, op1=ALU.mult)
                    if j % 2:
                        ins.then_inc(mixed, 1)
                keep_split(s.turn, 0)
                keep_split(s.turn + 1, 8)

            def rope(s, col, scratch):
                dve.wait_ge(late_in, 96)
                for t in range(T):
                    dve.wait_ge(taken[t], s.out)
                x = pv(3072)[:, :, col:col + 1024].rearrange("p t (h d) -> p t h d", h=8)
                x1, x2 = x[:, :, :, 0:16], x[:, :, :, 16:32]
                cos, sin = (table[:, o:o + 32].rearrange("p (t h c) -> p t h c", t=T, h=1)
                            .broadcast_to([P, T, 8, 16]) for o in (ROPE0, ROPE0 + 32))
                a, b = (scratch[:, o:o + 256].rearrange("p (t h c) -> p t h c", t=T, h=8) for o in (0, 256))
                vec.tensor_tensor(a, x1, sin, ALU.mult)
                link(vec.tensor_tensor(b, x2, sin, ALU.mult))
                vec.tensor_tensor(x1, x1, cos, ALU.mult)
                link(vec.tensor_tensor(x2, x2, cos, ALU.mult))
                vec.tensor_tensor(x1, x1, b, ALU.subtract)
                link(vec.tensor_tensor(x2, x2, a, ALU.add))

            def attention(s):
                if s.which == "diff":
                    dve.wait_ge(unskewed, 16)
                    g = table[:, 1024 + s.layer * P:1024 + (s.layer + 1) * P]
                    vec.tensor_scalar(g, g, 1.0 - lam_init(s.layer), None, ALU.mult)
                H, C = s.n_heads, s.comps

                def masked(i):
                    j = i // C
                    dve.wait_ge(scored, s.soft + i + 1)
                    if i >= 2:
                        dve.wait_ge(exped, s.soft + i - 1)
                    lg, b = proj[:, SOFT0 + (i % 2) * 512:], bank[4 + i % 2]
                    if not s.causal:
                        link(vec.tensor_scalar(lg[:, 0:512], b[:, :], s.scale, None, ALU.mult))
                    else:
                        m = proj[:, BIAS0 + j * S:BIAS0 + (j + 1) * S] if s.which == "diff" else \
                            table[:, CAUSAL0:CAUSAL0 + S]
                        vec.scalar_tensor_tensor(out=lg[:, 0:P], in0=b[:, 0:P], scalar=s.scale, in1=m[:, P:S],
                                                 op0=ALU.mult, op1=ALU.add)
                        link(vec.scalar_tensor_tensor(out=lg[:, S:2 * S], in0=b[:, S:2 * S], scalar=s.scale,
                                                      in1=m[:, :], op0=ALU.mult, op1=ALU.add))
                    for t in range(T):
                        n = P * (t + 1) if s.causal else S
                        ins = vec.tensor_reduce(stat[:, 16 + 2 * i + t:17 + 2 * i + t], lg[:, t * S:t * S + n], AX.X,
                                                ALU.max, negate=True)
                    ins.then_inc(maxed, 1)

                def combine(j):
                    dve.wait_ge(exped, s.soft + 2 * j + 2)
                    link(vec.reciprocal(stat[:, 80 + 4 * j:84 + 4 * j], stat[:, 48 + 4 * j:52 + 4 * j]))
                    link(vec.tensor_scalar(stat[:, 82 + 4 * j:84 + 4 * j], stat[:, 82 + 4 * j:84 + 4 * j],
                                           lam[:, 2 * s.layer:2 * s.layer + 1], None, ALU.mult))
                    for t in range(T):
                        n = P * (t + 1)
                        e0, e1 = (tmp[:, ((j % 2) * 2 + c) * 512 + t * S:][:, 0:n] for c in range(2))
                        link(vec.tensor_scalar(e0, e0, stat[:, 80 + 4 * j + t:81 + 4 * j + t], None, ALU.mult))
                        ins = vec.scalar_tensor_tensor(out=e0, in0=e1, scalar=stat[:, 82 + 4 * j + t:83 + 4 * j + t],
                                                       in1=e0, op0=ALU.mult, op1=ALU.add)
                    ins.then_inc(combined, 1)

                def take(j):
                    dve.wait_ge(head_done, s.heads + j + 1)
                    o = bank[2 + j % 2]
                    link(vec.reciprocal(stat[:, 80 + 2 * j:82 + 2 * j], stat[:, 48 + 2 * j:50 + 2 * j]))
                    for t in range(T):
                        ins = vec.tensor_scalar(yv[:, t, j * s.dv:(j + 1) * s.dv], o[:, t * s.dv:(t + 1) * s.dv],
                                                stat[:, 80 + 2 * j + t:81 + 2 * j + t], None, ALU.mult)
                    ins.then_inc(head_taken, 1)

                for j in range(H):
                    for c in range(C):
                        masked(C * j + c)
                    if C == 2:
                        combine(j)
                    elif j >= 2:
                        take(j - 2)
                if C == 1:
                    take(H - 2)
                    take(H - 1)
                dve.wait_ge(head_taken, s.heads + H)
                if s.which == "diff":
                    norm_heads(lambda t, j: g)
                else:
                    for t in range(T):
                        signal(mixed, 188 + t)

            def norm_heads(factor):
                rstd(HEADS0, 16, P)
                for t in range(T):
                    for j in range(8):
                        o, n = yv[:, t, j * P:(j + 1) * P], HEADS0 + 8 * t + j
                        ins = vec.scalar_tensor_tensor(out=o, in0=o, scalar=stat[:, n:n + 1], in1=factor(t, j),
                                                       op0=ALU.mult, op1=ALU.mult)
                    ins.then_inc(mixed, 1)

            def lower_bound():
                lb = stat[:, 128:160].rearrange("p (k l) -> p k l", l=4)
                dve.wait_ge(lb_in, 16)
                link(vec.tensor_reduce(stat[:, 176:184], lb, AX.X, ALU.max))
                vec.tensor_tensor(lb, lb, stat[:, 176:184].rearrange("p (k l) -> p k l", l=1)
                                  .broadcast_to([P, 8, 4]), ALU.subtract).then_inc(lb_exp, 1)
                dve.wait_ge(lb_exp, 2)
                link(vec.tensor_reduce(stat[:, 176:184], lb, AX.X, ALU.add))
                link(vec.reciprocal(stat[:, 176:184], stat[:, 176:184]))
                link(vec.tensor_tensor(lb, lb, stat[:, 176:184].rearrange("p (k l) -> p k l", l=1)
                                       .broadcast_to([P, 8, 4]), ALU.mult))
                link(vec.tensor_tensor(stat[:, 176:184], lb[:, :, 0], lb[:, :, 1], ALU.add))
                link(vec.tensor_tensor(stat[:, 176:184], stat[:, 176:184], lb[:, :, 0], ALU.subtract))
                signal(lb_ready)

            def keep_bound():
                for b in range(2):
                    dve.wait_ge(lb_spread, b + 1)
                    ins = vec.tensor_copy(table[:, b * 512:(b + 1) * 512], bank[6 + b][:, :])
                link(ins)

            def gates(s):
                f = pv(4096)[:, :, 1024:2048]
                lb = table[:, 0:1024].rearrange("p (t n) -> p t n", t=1).broadcast_to([P, T, D])
                keep_bound()
                for t in range(T):
                    dve.wait_ge(taken[t], s.out)
                link(vec.tensor_tensor(tv, f, lb, ALU.mult))
                link(vec.tensor_tensor(f, f, tv, ALU.subtract))
                link(vec.tensor_tensor(f, f, lb, ALU.add))
                link(vec.tensor_scalar(yv, f, -1.0, 1.0, ALU.mult, ALU.add))
                vec.tensor_scalar(f, f, 1e-19, None, ALU.max).then_inc(hg_f, 1)
                signal(mixed, 189)

            def hgrn(s):
                v = pv(4096)
                at_b = [at_of(b) for b in range(4)]
                for b in range(4):
                    dve.wait_ge(hg_prod, b + 1)
                    vec.tensor_tensor(at_b[b], bank[4 + b][:, :].rearrange("p (n m) -> p n m", n=4),
                                      ident[:, :].rearrange("p (n m) -> p n m", n=1).broadcast_to([P, 4, P]),
                                      ALU.mult).then_inc(hg_kept, 1)
                qf, kf = qk[:, 0:2048], qk[:, 2048:4096]
                for lv in range(HG_LEVELS):
                    L = 1 << lv
                    dve.wait_ge(hg_decay, 4 * (lv + 1))
                    dve.wait_ge(hg_prod, 4 * (lv + 1))
                    e, x, q_, k_ = (a.rearrange("p (n b l) -> p n b l", b=2, l=L)
                                    for a in (y[:, :], tmp[:, :], qf, kf))
                    vec.tensor_tensor(x[:, :, 1], e[:, :, 1], q_[:, :, 1], ALU.mult)
                    vec.tensor_tensor(x[:, :, 0], e[:, :, 0], k_[:, :, 0], ALU.mult).then_inc(hg_x, 1)
                    mask = proj[:, MASK0 + lv * P:MASK0 + (lv + 1) * P].bitcast(U32)\
                        .rearrange("p (n m) -> p n m", n=1).broadcast_to([P, 4, P])
                    for b in range(4):
                        dve.wait_ge(hg_prod, 4 * (lv + 1) + b + 1)
                        dve.wait_ge(hg_kept, 4 * (lv + 1) - 3 + b)
                        vec.copy_predicated(at_b[b], mask,
                                            bank[4 + b][:, :].rearrange("p (n m) -> p n m", n=4)).then_inc(hg_kept, 1)
                dve.wait_ge(hg_decay, 4 * (HG_LEVELS + 1))
                dve.wait_ge(hg_prod, 4 * (HG_LEVELS + 1))
                e, x, q_, k_ = (a.rearrange("p (n t l) -> p n t l", t=T, l=P) for a in (y[:, :], tmp[:, :], qf, kf))
                vec.tensor_tensor(x[:, :, 1], e[:, :, 1], q_[:, :, 1], ALU.mult)
                vec.tensor_tensor(x[:, :, 0], e[:, :, 0], k_[:, :, 0], ALU.mult).then_inc(hg_x, 1)
                for b in range(2):
                    dve.wait_ge(hg_prod, 4 * (HG_LEVELS + 1) + b + 1)
                    ins = vec.tensor_copy(table[:, b * 512:(b + 1) * 512], bank[4 + b][:, :])
                ins.then_inc(hg_kept, 1)
                for t in range(T):
                    dve.wait_ge(taken[t], s.out)
                gates = v[:, :, 3072:4096].rearrange("p t (j d) -> p t j d", j=8)
                for t in range(T):
                    ins = vec.tensor_tensor(gates[:, t], gates[:, t], table[:, 1280:1408]
                                            .rearrange("p (j d) -> p j d", j=1).broadcast_to([P, 8, P]), ALU.mult)
                link(ins)
                dve.wait_ge(hg_taken, 4)
                norm_heads(lambda t, j: gates[:, t, j, :])

            def values(s):
                g = pv(2048)[:, :, 1024:2048]
                dve.wait_ge(sg_w_in, 48)
                w = proj[:, 4096:5120].rearrange("p (g t) -> p g t", g=8)
                link(vec.tensor_tensor(w, w, tril_mask(), ALU.mult))
                for t in range(T):
                    dve.wait_ge(taken[t], s.out)
                link(vec.tensor_tensor(tv, g, g, ALU.mult))
                link(vec.tensor_reduce(stat[:, 0:2], tv, AX.X, ALU.add))
                rstd(0, 2, D)
                for t in range(T):
                    ins = vec.scalar_tensor_tensor(out=g[:, t, :], in0=g[:, t, :], scalar=stat[:, t:t + 1],
                                                   in1=proj[:, 5120:6144], op0=ALU.mult, op1=ALU.mult)
                ins.then_inc(sg_w_ready, 1)

            def sgu(s):
                u = pv(2048)[:, :, 0:1024]
                for t in range(T):
                    dve.wait_ge(taken[t], s.out)
                for t in range(T):
                    for grp in range(8):
                        dve.wait_ge(sg_mixed, grp // 2 + 1)
                        c = slice(grp * P, (grp + 1) * P)
                        b = bank[4 + grp // 2][:, (grp % 2) * S + t * P:][:, 0:P]
                        ins = vec.scalar_tensor_tensor(out=yv[:, t, c], in0=b, scalar=stat[:, 128 + grp:129 + grp],
                                                       in1=u[:, t, c], op0=ALU.add, op1=ALU.mult)
                    ins.then_inc(mixed, 1)

            def tril_mask():
                m = proj[:, CUM0 + (HG_LEVELS + 1) * P:CUM0 + (HG_LEVELS + 2) * P]
                return m.rearrange("p (a t) -> p a t", a=1).broadcast_to([P, 8, P])

            for p in range(WP):
                low_wide(0, p)
            for s in PLAN:
                if s.kind == "prenorm":
                    if not s.fused:
                        norm(s)
                    if s.src == "mem":
                        lower_bound()
                elif s.kind == "turn":
                    if TURNS[s.turn] == "s":
                        keep_split(s.turn, s.chunk, range(2 if s.early else 0, 4))
                    else:
                        keep_plain(s.turn, s.chunk)
                    if s.turn == 0:
                        lambdas()
                elif s.kind == "rope":
                    rope(s, s.col, tmp)
                    signal(mixed, 189)
                elif s.kind == "gates":
                    gates(s)
                elif s.kind == "values":
                    values(s)
                elif s.kind == "between":
                    for t in range(T):
                        mean(s, t)
                    for t in range(T):
                        scale(s, t)
                        dve.wait_ge(normed, 2 * s.norm + t + 1)
                        signal(h_ready[t], 190 + t)
                elif s.kind == "finish":
                    norm(s)
                    dve.wait_ge(normed, 2 * (s.norm + 1))
                    signal(stored)
                elif s.kind == "linear":
                    linear(s)
                elif s.kind == "residual":
                    residual(s)
                elif s.kind == "gated":
                    gated(s)
                elif s.kind == "retention":
                    retention(s)
                elif s.kind == "attention":
                    attention(s)
                elif s.kind == "hgrn":
                    hgrn(s)
                elif s.kind == "sgu":
                    sgu(s)

        @block.tensor
        def _(pe):
            def three(o, hi, lo, wh, wl, start, stop):
                pe.matmul(o, hi, wh, start=start, stop=False)
                pe.matmul(o, hi, wl, start=False, stop=False)
                return pe.matmul(o, lo, wh, start=False, stop=stop)

            def wide_block(n, q, chunk, start=True, stop=True):
                for t in range(T):
                    if start and not (isinstance(q, int) and q == 0):
                        pe.wait_ge(taken[t], q)
                    for p in range(WP):
                        if (t, p) in pending:
                            pending.pop((t, p))()
                        if t == 0:
                            pe.wait_ge(split_lw, WP * n + p + 1)
                        for k in range(KP):
                            c = KP * p + k
                            w = slice(c * WIDE, (c + 1) * WIDE)
                            x = slice(t * P, (t + 1) * P)
                            mm = three(bank[4 + t][:, :], xhv[:, chunk + c, x], xlv[:, chunk + c, x],
                                       high_w[:, w], low_w[:, w], start and c == 0, stop and c == KC - 1)
                        if t == T - 1:
                            mm.then_inc(used_w, 1)
                        elif p == WP - 1:
                            mm.then_inc(rows0_done, 1)

            pending = {}

            def turn(m, src, t, ready=None):
                if ready is not None:
                    pe.wait_ge(*ready)
                if m:
                    pe.wait_ge(kept_h, kept(m))
                    pe.wait_ge(kept_l, kept(m))
                for i in range(2):
                    for k in range(4):
                        mm = pe.transpose(bank[2 * t + i][:, k * P:(k + 1) * P],
                                          src[:, t, (4 * i + k) * P:(4 * i + k + 1) * P], ident[:, :])
                    mm.then_inc(turned, 1)

            def outs_of(s, col):
                p = [p for p in PLAN[:PLAN.index(s)] if p.kind == "linear" and p.col <= col < p.col + p.blocks * WIDE][-1]
                return p.out + (col + D - p.col) // WIDE

            def turn_stage(s):
                ready = {"norm": lambda t: (normed, 2 * s.norm - 1 + t), "q rotated": lambda t: (rotated, 1),
                         "k rotated": lambda t: (rotated, 2), "k roped": lambda t: (mixed, s.mixed),
                         "q roped": lambda t: (mixed, s.mixed), "gates": lambda t: (mixed, s.mixed),
                         "y": lambda t: (mixed, s.mixed - 1 + t), "q": lambda t: (taken[t], outs_of(s, 0)),
                         "k": lambda t: (taken[t], outs_of(s, D))}[s.src]
                width = ([p.width for p in PLAN[:PLAN.index(s)] if p.kind == "linear"] or [D])[-1]
                src = pv(width)[:, :, 0:1024] if s.src[0] == "q" else \
                    pv(width)[:, :, 1024:2048] if s.src[0] == "k" else yv
                if not s.early:
                    turn(s.turn, src, 0, ready(0))
                if s.hook:
                    def keep(b):
                        pe.wait_ge(kept_h, kept(s.turn) + b + 1)
                        pe.wait_ge(kept_l, kept(s.turn) + b + 1)

                    pending[0, 0] = lambda: keep(0)
                    pending[0, WP // 2] = lambda: keep(1)
                    pending[0, WP - 1] = lambda: turn(s.turn, src, 1, ready(1))
                    pending[1, 0] = lambda: keep(2)
                    pending[1, WP // 2] = lambda: keep(3)
                else:
                    turn(s.turn, src, 1, ready(1))

            def turn_early(s):
                if after(s).kind == "turn" and after(s).early:
                    turn(after(s).turn, yv, 0, (normed, 2 * s.norm + 1))

            def wait_kept(m):
                pe.wait_ge(kept_h, kept(m + 1))
                pe.wait_ge(kept_l, kept(m + 1))

            def linear(s):
                if not pending:
                    wait_kept([p.turn for p in PLAN[:PLAN.index(s)]
                               if p.kind == "turn" and TURNS[p.turn] == "s" and p.chunk == s.chunk][-1])
                first = 0
                if pending or s.blocks == 1:
                    wide_block(s.wide, s.out, s.chunk)
                    first = 1
                if s.blocks > 1:
                    with pe.Fori(first, s.blocks) as i:
                        wide_block(s.wide + i, s.out + i, s.chunk)

            def residual(s):
                for half in range(2):
                    for k in range(s.halves):
                        if half and k == s.halves - 1:
                            pending[1, WP - 1] = lambda: turn_early(after(s))
                        wide_block(s.wide + half * s.halves + k, s.out + half, KC * k, k == 0, k == s.halves - 1)

            def router(s):
                for t in range(T):
                    for i, part in enumerate((xhv, xlv)):
                        for k in range(KC):
                            w = table[:, ROUTER0 + (s.moe * KC + k) * ROUTER:][:, 0:ROUTER]
                            mm = pe.matmul(bank[7][:, t * ROUTER:(t + 1) * ROUTER],
                                           part[:, k, t * P:(t + 1) * P].bitcast(F32), w,
                                           start=i == 0 and k == 0, stop=i == 1 and k == KC - 1)
                mm.then_inc(used_router, 1)
                pe.wait_ge(grouped, s.moe + 1)
                upto = proj[:, CUM0 + (HG_LEVELS + 1) * P:CUM0 + (HG_LEVELS + 2) * P]
                ones = table[:, ONE0:ONE0 + 1].broadcast_to([P, P])
                one_g = [tmp[:, 24 + 4 * t:28 + 4 * t] for t in range(T)]
                pe.matmul(bank[7][:, 64:68], upto, one_g[0], start=True, stop=True)
                pe.matmul(bank[7][:, 68:72], upto, one_g[1], start=True, stop=False)
                pe.matmul(bank[7][:, 68:72], ones, one_g[0], start=False, stop=True)
                pe.matmul(bank[7][:, 72:76], ones, one_g[0], start=True, stop=False)
                pe.matmul(bank[7][:, 72:76], ones, one_g[1], start=False, stop=True).then_inc(ranked, 1)

            def sparse(s):
                way = ways[s.moe]

                def gather(g):
                    pick = [qk[:, PICK0 + (t * GROUPS + g) * P:][:, 0:P] for t in range(T)]
                    for t in range(T):
                        mm = pe.transpose(bank[6][:, S + t * P:S + (t + 1) * P], pick[t], ident[:, :])
                    mm.then_inc(way.gathered, 1)
                    if g >= 2:
                        pe.wait_ge(way.added, 4 * (g - 1))
                    for t in range(T):
                        pe.matmul(bank[2 * (g % 2)][:, 0:EXPERTS], pick[t], tmp[:, WI0 + 4 * t:WI0 + 4 * t + 4],
                                  start=t == 0, stop=t == T - 1)
                    for k in range(KC):
                        for t in range(T):
                            mm = pe.matmul(bank[5 + 2 * (k // 4)][:, (k % 4) * P:(k % 4 + 1) * P],
                                           yv[:, t, k * P:(k + 1) * P], pick[t], start=t == 0, stop=t == T - 1)
                        if k % 4 == 3:
                            mm.then_inc(way.gathered, 1)

                def scatter(g):
                    pe.wait_ge(way.z_left, g + 1)
                    pe.wait_ge(way.z_right, g + 1)
                    for i in range(2 * T):
                        t, half = i // 2, i % 2
                        if i >= 2:
                            pe.wait_ge(way.added, 4 * g + i - 1)
                        z = Z0 + (g % 2) * D + half * WIDE
                        pe.matmul(bank[5 + 2 * half][:, :], qk[:, SLOT0 + g * S + t * P:][:, 0:P], proj[:, z:z + WIDE],
                                  start=True, stop=True).then_inc(way.scattered, 1)

                def unit(u, g):
                    n = s.wide + u
                    for t in range(T):
                        pe.wait_ge(taken[t], s.out + u)
                    for p in range(WP):
                        pe.wait_ge(split_lw, WP * n + p + 1)
                        for k in range(KP):
                            c = KP * p + k
                            w, x = slice(c * WIDE, (c + 1) * WIDE), KC * (g % 2) + c
                            mm = three(bank[4][:, :], xhv[:, x, 0:P], xlv[:, x, 0:P], high_w[:, w], low_w[:, w],
                                       c == 0, c == KC - 1)
                            if c == KC - 2:
                                mm.then_inc(rows0_done, 1)
                        mm.then_inc(used_w, 1)

                def turn_hidden(u):
                    for t in range(T):
                        pe.wait_ge(taken[t], s.out + u + 1)
                    for c in range(DP):
                        o = GATED0 + FU + c * P
                        mm = pe.transpose(bank[6][:, c * P:(c + 1) * P], qk[:, o:o + P], ident[:, :])
                    mm.then_inc(hidden_turned, 1)

                def down(u, g, first=False, last=False):
                    pe.wait_ge(hidden_low, s.down + u + 1)
                    for p in range(DP):
                        pe.wait_ge(split_ld, DP * (s.down + u) + p + 1)
                        for half in range(2):
                            x = slice(p * P, (p + 1) * P)
                            w = slice(p * PIECE + half * WIDE, p * PIECE + (half + 1) * WIDE)
                            mm = three(bank[2 * (g % 2) + half][:, :], hidden_h[:, x], hidden_l[:, x],
                                       high_d[:, w], low_d[:, w], first and p == 0, last and p == DP - 1)
                        mm.then_inc(used_d, 1)

                pe.wait_ge(way.v_step, 1)
                gather(0)
                pe.wait_ge(way.gathered_l, 2)
                unit(0, 0)
                turn_hidden(0)
                for g in range(GROUPS):
                    u0 = g * GROUP_UNITS
                    if g:
                        pe.wait_ge(way.gathered_l, 2 * (g + 1))
                        unit(u0, g)
                        down(u0 - 1, g - 1, last=True)
                        turn_hidden(u0)
                    unit(u0 + 1, g)
                    down(u0, g, first=True)
                    turn_hidden(u0 + 1)
                    if g:
                        scatter(g - 1)
                    if g + 1 < GROUPS:
                        if g == 0:
                            pe.wait_ge(way.gathered_l, 2)
                        gather(g + 1)
                    with pe.Fori(u0 + 2, u0 + GROUP_UNITS) as u:
                        unit(u, g)
                        down(u - 1, g)
                        turn_hidden(u)
                down(MOE_UNITS - 1, GROUPS - 1, last=True)
                scatter(GROUPS - 1)

            def gated(s):
                if s.moe is None:
                    dense(s)
                    return
                wait_kept(s.turn - 1)
                pe.wait_ge(late_in, 96)
                router(s)
                pe.wait_ge(counted, s.moe + 1)
                with pe.If(pe.value_load(largest[0:1, 0:1], min_val=0, max_val=S) < P + 1):
                    sparse(s)
                with pe.Else():
                    dense(s)

            def dense(s):
                def turn_hidden(u):
                    for t in range(T):
                        pe.wait_ge(taken[t], s.out + u + 1)
                    for c in range(DP):
                        for t in range(T):
                            mm = pe.transpose(bank[6][:, c * S + t * P:c * S + (t + 1) * P],
                                              y[:, 512 + t * FU + c * P:512 + t * FU + (c + 1) * P], ident[:, :])
                    mm.then_inc(hidden_turned, 1)

                def down(u, first=False, last=False, pieces=range(DP)):
                    pe.wait_ge(hidden_low, s.down + u + 1)
                    for p in pieces:
                        pe.wait_ge(split_ld, DP * (s.down + u) + p + 1)
                        for t in range(T):
                            for half in range(2):
                                x = slice(p * S + t * P, p * S + (t + 1) * P)
                                w = slice(p * PIECE + half * WIDE, p * PIECE + (half + 1) * WIDE)
                                mm = three(bank[2 * t + half][:, :], hidden_h[:, x], hidden_l[:, x],
                                           high_d[:, w], low_d[:, w], first and p == 0, last and p == DP - 1)
                        mm.then_inc(used_d, 1)

                wide_block(s.wide, s.out, 0)
                turn_hidden(0)
                wide_block(s.wide + 1, s.out + 1, 0)
                down(0, first=True)
                turn_hidden(1)
                u = s.units - 1
                with pe.Fori(2, u) as i:
                    wide_block(s.wide + i, s.out + i, 0)
                    down(i - 1)
                    turn_hidden(i)
                wide_block(s.wide + u, s.out + u, 0)
                down(u - 1, pieces=range(1))
                turn_hidden(u)
                down(u - 1, pieces=range(1, DP))
                hh, hl = hidden_of(s, u)
                pe.wait_ge(hidden_low, s.down + u + 1)
                for t in range(T):
                    for p in range(DP):
                        pe.wait_ge(split_ld, DP * (s.down + u) + p + 1)
                        for half in range(2):
                            x = slice(p * S + t * P, p * S + (t + 1) * P)
                            w = slice(p * PIECE + half * WIDE, p * PIECE + (half + 1) * WIDE)
                            mm = three(bank[2 * t + half][:, :], hh[:, x], hl[:, x], high_d[:, w], low_d[:, w],
                                       False, p == DP - 1)
                        if t:
                            mm.then_inc(used_d, 1)
                        elif p == DP - 1:
                            mm.then_inc(down0_done, 1)
                if s.moe is None and after(s).kind == "prenorm":
                    turn_early(after(s))

            def retention(s):
                v = pv(6144)
                for t in range(T):
                    pe.wait_ge(taken[t], s.out)
                wait_kept(s.turn - 1)

                def scores(j):
                    if j >= 2:
                        pe.wait_ge(ret_masked, j - 1)
                    b = bank[4 + j % 2]
                    for mt in range(T):
                        for c in range(2):
                            mm = pe.matmul(b[:, mt * S:mt * S + S - mt * P],
                                           qkv[:, 8 + 2 * j + c, mt * P:(mt + 1) * P],
                                           qkv[:, 2 * j + c, mt * P:S], start=c == 0, stop=c == 1)
                    mm.then_inc(ret_scored, 1)

                def heads(j):
                    pe.wait_ge(ret_masked, j + 1)
                    st = tmp[:, (j % 2) * 512:]
                    vj = [v[:, t, 2048 + j * RET_V:2048 + (j + 1) * RET_V] for t in range(T)]
                    if j:
                        pe.wait_ge(ret_taken, 2 * j - 1)
                    pe.matmul(bank[6][:, :], st[:, 0:P], vj[0], start=True, stop=True).then_inc(ret_done, 1)
                    if j:
                        pe.wait_ge(ret_taken, 2 * j)
                    pe.matmul(bank[7][:, :], st[:, P:S], vj[0], start=True, stop=False)
                    pe.matmul(bank[7][:, :], st[:, S:S + P], vj[1], start=False, stop=True).then_inc(ret_done, 1)

                scores(0)
                for j in range(RET_HEADS):
                    if j + 1 < RET_HEADS:
                        scores(j + 1)
                    heads(j)
                for m in range(2):
                    for t in range(T):
                        turn(s.turn + m, v[:, :, m * D:(m + 1) * D], t, (mixed, m + 1))

            def bias_table():
                pe.wait_ge(late_in, 96)
                pe.wait_ge(ret_taken, 2 * RET_HEADS)
                for j in range(8):
                    if j >= 2:
                        pe.wait_ge(bias_copied, j - 1)
                    pe.matmul(bank[6 + j % 2][:, 0:384], proj[0:33, 384 + j:385 + j].broadcast_to([33, P]),
                              proj[0:33, 0:384], start=True, stop=True).then_inc(bias_rows, 1)

            def attention(s):
                v = pv(s.width)
                for t in range(T):
                    pe.wait_ge(taken[t], s.out)
                wait_kept(s.turn - 1)
                H, C, dv = s.n_heads, s.comps, s.dv

                def scores(i):
                    j, c = i // C, i % C
                    if i >= 2:
                        pe.wait_ge(maxed, s.soft + i - 1)
                    r = slice(c * 64, (c + 1) * 64) if C == 2 else slice(0, P)
                    for t in range(T):
                        n = P * (t + 1) if s.causal else S
                        for k in range(s.chunks):
                            mm = pe.matmul(bank[4 + i % 2][:, t * S:t * S + n],
                                           qkv[r, s.chunks * j + k, t * P:(t + 1) * P],
                                           qkv[r, 8 + s.chunks * j + k, 0:n], start=k == 0, stop=k == s.chunks - 1)
                    mm.then_inc(scored, 1)

                def turn_probs(j):
                    if C == 2:
                        pe.wait_ge(combined, 8 * s.layer + j + 1)
                    else:
                        pe.wait_ge(exped, s.soft + j + 1)
                    if j >= 2:
                        pe.wait_ge(probs_kept, s.heads + j - 1)
                    for kt in range(T):
                        for t in range(T):
                            if s.causal and kt > t:
                                continue
                            e = tmp[:, (j % 2) * 1024 + t * S + kt * P:][:, 0:P]
                            mm = pe.transpose(bank[6 + j % 2][:, kt * S + t * P:kt * S + (t + 1) * P], e, ident[:, :])
                    mm.then_inc(probs_turned, 1)

                def head(j):
                    pe.wait_ge(probs_kept, s.heads + j + 1)
                    if j >= 2:
                        pe.wait_ge(head_taken, s.heads + j - 1)
                    slot = proj[:, SOFT0 + 1024 + (j % 2) * 512:]
                    for t in range(T):
                        kts = range(t + 1) if s.causal else range(T)
                        for kt in kts:
                            mm = pe.matmul(bank[2 + j % 2][:, t * dv:(t + 1) * dv],
                                           slot[:, kt * S + t * P:kt * S + (t + 1) * P],
                                           v[:, kt, 2048 + j * dv:2048 + (j + 1) * dv],
                                           start=kt == 0, stop=kt == kts[-1])
                    mm.then_inc(head_done, 1)

                for j in range(H):
                    for c in range(C):
                        scores(C * j + c)
                    if j:
                        turn_probs(j - 1)
                    if j >= 2:
                        head(j - 2)
                turn_probs(H - 1)
                head(H - 2)
                head(H - 1)

            def spread_bound():
                pe.wait_ge(lb_ready, 1)
                for j in range(8):
                    mm = pe.matmul(bank[6 + j // 4][:, (j % 4) * P:(j % 4 + 1) * P],
                                   stat[:, 176 + j:177 + j].broadcast_to([P, P]), ident[:, :], start=True, stop=True)
                    if j % 4 == 3:
                        mm.then_inc(lb_spread, 1)

            def hgrn(s):
                v = pv(4096)
                for t in range(T):
                    pe.wait_ge(taken[t], s.out)
                wait_kept(s.turn - 1)
                pe.wait_ge(hg_log, 1)

                def sums(lv):
                    for j in range(8):
                        if lv and j % 2 == 0:
                            pe.wait_ge(hg_decay, 4 * (lv - 1) + j // 2 + 1)
                        for t in range(T):
                            m = lv if lv < HG_LEVELS else HG_LEVELS + t
                            mm = pe.matmul(bank[j // 2][:, (j % 2) * S + t * P:(j % 2) * S + (t + 1) * P],
                                           v[:, t, 1024 + j * P:1024 + (j + 1) * P],
                                           proj[:, CUM0 + m * P:CUM0 + (m + 1) * P], start=True, stop=True)
                        if j % 2:
                            mm.then_inc(hg_sums, 1)

                def products(lv):
                    if lv:
                        pe.wait_ge(hg_x, lv)
                    for n in range(16):
                        if n % 4 == 0 and lv:
                            pe.wait_ge(hg_kept, 4 * (lv - 1) + n // 4 + 1)
                        j, t = n // 2, n % 2
                        c = slice(j * S + t * P, j * S + (t + 1) * P)
                        a, b = (tmp[:, c], tmp[:, c]) if lv else (qk[:, 2048 + j * S + t * P:][:, 0:P], qk[:, c])
                        mm = pe.matmul(bank[4 + n // 4][:, (n % 4) * P:(n % 4 + 1) * P], a, b, start=True, stop=True)
                        if n % 4 == 3:
                            mm.then_inc(hg_prod, 1)

                sums(0)
                products(0)
                for lv in range(HG_LEVELS):
                    sums(lv + 1)
                    products(lv + 1)
                pe.wait_ge(hg_x, HG_LEVELS + 1)
                for j in range(8):
                    if j % 4 == 0:
                        pe.wait_ge(hg_kept, 4 * HG_LEVELS + j // 4 + 1)
                    mm = pe.matmul(bank[4 + j // 4][:, (j % 4) * P:(j % 4 + 1) * P], tmp[:, j * S:j * S + P],
                                   tmp[:, j * S + P:(j + 1) * S], start=True, stop=True)
                    if j % 4 == 3:
                        mm.then_inc(hg_prod, 1)
                pe.wait_ge(hg_kept, 4 * (HG_LEVELS + 1) + 1)
                for t in range(T):
                    for j in range(8):
                        o = bank[2 * t + j // 4][:, (j % 4) * P:(j % 4 + 1) * P]
                        at = at_of(j // 2)[:, (j % 2) * 2 + t, :]
                        mm = pe.matmul(o, at, v[:, t, 2048 + j * P:2048 + (j + 1) * P], start=True, stop=t == 0)
                        if t:
                            mm = pe.matmul(o, table[:, j * P:(j + 1) * P], v[:, 0, 2048 + j * P:2048 + (j + 1) * P],
                                           start=False, stop=True)
                        if j % 4 == 3:
                            mm.then_inc(hg_out, 1)

            def sgu(s):
                pe.wait_ge(sg_w_ready, 1)
                pe.wait_ge(taken[0], s.out)
                pe.wait_ge(taken[1], s.out)
                for grp in range(8):
                    for t in range(T):
                        mm = pe.matmul(bank[4 + grp // 2][:, (grp % 2) * S + t * P:(grp % 2) * S + (t + 1) * P],
                                       proj[:, 4096 + grp * P:4096 + (grp + 1) * P],
                                       pv(2048)[:, t, 1024 + grp * P:1024 + (grp + 1) * P], start=True, stop=True)
                    if grp % 2:
                        mm.then_inc(sg_mixed, 1)

            pe.wait_ge(ident_in, 16)
            for s in PLAN:
                if s.kind == "turn":
                    turn_stage(s)
                elif s.kind == "bias":
                    bias_table()
                elif s.kind == "gates":
                    spread_bound()
                elif s.kind == "linear":
                    linear(s)
                elif s.kind == "residual":
                    residual(s)
                elif s.kind == "gated":
                    gated(s)
                elif s.kind == "retention":
                    retention(s)
                elif s.kind == "attention":
                    attention(s)
                elif s.kind == "hgrn":
                    hgrn(s)
                elif s.kind == "sgu":
                    sgu(s)


def _wide(w):
    n = w.shape[1] // WIDE
    return w.reshape(WP, KP, P, n, WIDE).transpose(3, 0, 2, 1, 4).reshape(n, WP, P, PIECE)


def _gated(gate, up):
    n = gate.shape[1] // FU
    both = np.concatenate([gate.reshape(D, n, FU), up.reshape(D, n, FU)], axis=2)
    return _wide(both.reshape(D, n * WIDE))


def _out(w):
    m = w.shape[0] // D
    return np.concatenate([_wide(w[k * D:(k + 1) * D, c * WIDE:(c + 1) * WIDE]) for c in range(2) for k in range(m)])


def _streams(a):
    wide, down = [], []

    def moe(layer):
        for g in range(GROUPS):
            for e in range(EXPERTS):
                wide.append(_gated(a["expert_w_gate"][layer, g, e], a["expert_w_up"][layer, g, e]))
                down.append(a["expert_w_down"][layer, g, e].reshape(-1, DP, P, PIECE))

    wide += [_wide(a["ret_w_in"][0]), _out(a["ret_w_out"][0])]
    moe(0)
    wide += [_wide(a["w_kv"][:, :D]), _wide(a["w_q"][0]), _wide(a["w_kv"][:, D:]), _out(a["w_o"][0])]
    moe(1)
    for i in range(4):
        mix = ("da", "hg", "sg")[i % 3]
        w_in = a[mix + "_w_in_2"][i // 3]
        if mix == "sg":
            w_in = np.concatenate([w_in[:, D:], w_in[:, :D]], axis=1)
        wide += [_wide(w_in), _out(a[mix + "_w_out_2"][i // 3])]
        kv = a["ca_w_kv_2"][i]
        wide += [_wide(kv[:, :D]), _wide(a["ca_w_q_2"][i]), _wide(kv[:, D:]), _out(a["ca_w_o_2"][i])]
        gu = a["ffn_w_gu_2"][i]
        wide.append(_gated(gu[:, :D_FF], gu[:, D_FF:]))
        down.append(a["ffn_w_down_2"][i].reshape(-1, DP, P, PIECE))
    return np.concatenate(wide), np.concatenate(down)


def _rope_table(dim, theta):
    half = dim // 2
    inv = (1.0 / (np.float32(theta) ** (np.arange(half, dtype=np.float32) / np.float32(half)))).astype(np.float32)
    ang = np.arange(S, dtype=np.float32)[:, None] * inv[None, :]

    def lay(x):
        return x.astype(np.float32).reshape(T, P, half).transpose(1, 0, 2).reshape(P, T * half)
    return lay(np.cos(ang)), lay(np.sin(ang))


def _constants():
    f = np.float32
    p = np.arange(P)[:, None]
    c = np.arange(S)[None, :]
    gamma = np.log1p(-np.power(2.0, -5.0 - np.arange(RET_HEADS)))
    decay = [np.where(c >= p, np.exp(g * np.maximum(c - p, 0)), 0.0) * RET_QK ** -0.5 for g in gamma]
    ret = np.concatenate([*decay, *_rope_table(RET_QK, 10000.0)], axis=1).astype(f)
    causal = np.where(c <= p + P, 0.0, NEG)
    iota_one = np.concatenate([np.tile(np.arange(P), (P, 1)), np.ones((P, 1))], axis=1)
    small = np.concatenate([np.zeros((P, CAUSAL0)), causal, *_rope_table(32, 500000.0), iota_one], axis=1).astype(f)
    s, t = np.arange(P)[:, None], np.arange(P)[None, :]
    sums, masks = [], []
    for lv in range(HG_LEVELS):
        L = 1 << lv
        mid = (t // (2 * L)) * 2 * L + L - 1
        second = t > mid
        sums.append(np.where(second, (s > mid) & (s <= t), (s > t) & (s <= mid)))
        masks.append((s // (2 * L) == t // (2 * L)) & (s <= mid) & second)
    sums += [s > t, s <= t]
    hg = np.concatenate(sums + masks, axis=1).astype(f)
    dist = 255 - np.arange(384)
    n = np.maximum(dist, 0)
    nf = np.maximum(n, 16).astype(f)
    large = np.minimum(16 + (np.log(nf / f(16)) / f(math.log(8.0)) * f(16)).astype(np.int32), 31)
    bucket = np.where(n < 16, n, large)
    buckets = np.zeros((33, 384), f)
    buckets[bucket, np.arange(384)] = dist >= 0
    buckets[32] = np.where(dist < 0, NEG, 0.0)
    return ret, small, hg, buckets


def kernel(**inputs):
    import concourse.bacc as bacc
    from concourse.bass_utils import run_bass_kernel_spmd

    a = {k: np.asarray(v) for k, v in inputs.items()}
    f = np.float32
    ret, small, hg, buckets = _constants()
    router = np.concatenate([a["router_group_w"], a["router_expert_w"].transpose(0, 2, 1, 3).reshape(2, D, -1)], axis=2)
    small[:, ROUTER0:CAUSAL0] = router.reshape(2, KC, P, ROUTER).transpose(2, 0, 1, 3).reshape(P, -1)
    gains = [a["ret_norm"][0], a["ffn_norm"][0], a["kv_norm"], a["attn_norm"][0], a["ffn_norm"][1], a["final_norm"]]
    for i in range(4):
        gains += [a["norm_mix_2"][i]] + ([a["norm_mem_2"]] if i == 0 else [])
        gains += [a["norm_cross_2"][i], a["norm_ffn_2"][i]]
    gains.append(a["norm_final_2"])
    wide, down = _streams(a)
    rel = np.ones((33, 8), f)
    rel[:32] = a["rel_bias_2"].T
    arrays = {
        "x": a["x"][0], "mem": a["mem_2"][0], "wide": wide, "down": down, "gains": np.stack(gains),
        "ident": np.eye(P, dtype=f), "ret_table": ret, "small_table": small, "hg_consts": hg, "buckets": buckets,
        "rel_bias": rel,
        "head_gains": np.concatenate([a["da_subln_2"].reshape(-1), a["hg_onorm_2"].reshape(-1)])[None],
        "router_bias": np.concatenate([np.concatenate([a["router_group_b"][i], a["router_expert_b"][i].reshape(-1)])
                                       for i in range(2)])[None],
        "lambdas": np.stack([a["da_" + n + "_2"] for n in ("lq1", "lk1", "lq2", "lk2")], axis=1).reshape(1, -1),
        "lower_bounds": a["hg_lower_bounds_2"].reshape(4, 8, P).transpose(2, 1, 0).reshape(P, 32),
        "sg_w": a["sg_w_s_2"][0].transpose(2, 0, 1).reshape(P, -1), "sg_gain": a["sg_vnorm_2"],
        "sg_bias": a["sg_b_s_2"][0].T,
    }
    nc = bacc.Bacc("TRN2", target_bir_lowering=False, num_devices=1)
    dram = {}
    for name, v in arrays.items():
        arrays[name] = np.ascontiguousarray(v)
        dram[name] = nc.dram_tensor("in_" + name, v.shape, F32, kind="ExternalInput").ap()
    out = nc.dram_tensor("out_h", (S, D), F32, kind="ExternalOutput").ap()
    build(nc, dram, out)
    r = run_bass_kernel_spmd(nc, [{"in_" + k: v for k, v in arrays.items()}], core_ids=[0])
    return r.results[0]["out_h"].reshape(1, S, D)
```
